# Optimizing a Trainium2 kernel written in Bass

```python
import math
import jax, jax.numpy as jnp
from jax import lax
import numpy as np

D_MODEL = 2048
BATCH = 1
SEQ = 256
DEPTH = 1

CHUNK = 64
Q_BLOCK = 128
ROPE_THETA = 10000.0
EPS = 1e-6

DA_HEADS = 8
DA_HEAD_DIM = 128
DA_V_DIM = 2 * DA_HEAD_DIM
DA_QK_WIDTH = DA_HEADS * 2 * DA_HEAD_DIM
DA_WIDTH = DA_HEADS * DA_V_DIM

RW_HEAD_DIM = 64
RW_HEADS = D_MODEL // RW_HEAD_DIM
RW_WIDTH = RW_HEADS * RW_HEAD_DIM
RW_DECAY_RANK = max(32, int(round(math.sqrt(D_MODEL) * 1.8 / 32)) * 32)
RW_AAA_RANK = max(32, int(round(math.sqrt(D_MODEL) * 1.8 / 32)) * 32)
RW_GATE_RANK = max(32, int(round(0.6 * D_MODEL ** 0.8 / 32)) * 32)
RW_GN_EPS = 1e-5 * RW_HEAD_DIM
RW_TOTAL = 3 * RW_WIDTH + RW_DECAY_RANK + RW_AAA_RANK + RW_GATE_RANK

D_FF = -(-8 * D_MODEL // (3 * 256)) * 256

OFF_DA_Q = 0
OFF_DA_K = OFF_DA_Q + DA_QK_WIDTH
OFF_DA_V = OFF_DA_K + DA_QK_WIDTH
OFF_RW = OFF_DA_V + DA_WIDTH
OFF_GATE = OFF_RW + RW_TOTAL
N_IN = OFF_GATE + 2 * D_MODEL


def _rmsnorm(x, g, eps=EPS):
    xf = x.astype(jnp.float32)
    y = xf * lax.rsqrt(jnp.mean(xf * xf, axis=-1, keepdims=True) + eps)
    return (y * g.astype(jnp.float32)).astype(x.dtype)

def _rope(t, pos):
    half = t.shape[-1] // 2
    inv = ROPE_THETA ** (-jnp.arange(half, dtype=jnp.float32) / half)
    ang = pos.astype(jnp.float32)[:, None] * inv[None, :]
    cos = jnp.cos(ang)[:, None, None, :]
    sin = jnp.sin(ang)[:, None, None, :]
    tf = t.astype(jnp.float32)
    t1, t2 = tf[..., :half], tf[..., half:]
    out = jnp.concatenate([t1 * cos - t2 * sin, t2 * cos + t1 * sin], axis=-1)
    return out.astype(t.dtype)

def _diff_attention(q, k, v, lam, subln_g, lambda_init):
    B, S = q.shape[0], q.shape[1]
    n_blocks = S // Q_BLOCK
    scale = DA_HEAD_DIM ** -0.5
    key_chunk = jnp.arange(S) // CHUNK
    qb = jnp.moveaxis(q.reshape(B, n_blocks, Q_BLOCK, DA_HEADS, 2, DA_HEAD_DIM), 1, 0)
    neg = jnp.finfo(jnp.float32).min

    def one_block(args):
        q_blk, i = args
        q_chunk = (i * Q_BLOCK + jnp.arange(Q_BLOCK)) // CHUNK
        mask = key_chunk[None, :] <= q_chunk[:, None]
        s = jnp.einsum('bqhcd,bkhcd->bhcqk', q_blk, k).astype(jnp.float32) * scale
        s = jnp.where(mask, s, neg)
        p = jax.nn.softmax(s, axis=-1)
        p = p[:, :, 0] - lam * p[:, :, 1]
        return jnp.einsum('bhqk,bkhe->bqhe', p.astype(v.dtype), v)

    o = lax.map(one_block, (qb, jnp.arange(n_blocks)))
    o = jnp.moveaxis(o, 0, 1).reshape(B, S, DA_HEADS, DA_V_DIM)
    o = _rmsnorm(o, subln_g, eps=1e-5) * (1.0 - lambda_init)
    return o.reshape(B, S, DA_WIDTH)

def _rwkv7_step(state, inp):
    r_t, w_t, k_t, v_t, a_t, b_t = inp
    sa = jnp.einsum('bhij,bhj->bhi', state, a_t)
    state = (state * w_t[:, :, None, :] + sa[..., None] * b_t[:, :, None, :]
             + v_t[..., None] * k_t[:, :, None, :])
    y = jnp.einsum('bhij,bhj->bhi', state, r_t)
    return state, y

def _rwkv7(p, mu, w0, w_up, a0, a_up, g_up, k_k, k_a, r_k, ln_w, ln_b):
    B, S, _ = p.shape
    prev = jnp.pad(p, ((0, 0), (1, 0), (0, 0)))[:, :S]
    xs = p + mu * (prev - p)
    o0, o1, o2, o3 = RW_WIDTH, 2 * RW_WIDTH, 3 * RW_WIDTH, 3 * RW_WIDTH + RW_DECAY_RANK
    o4 = o3 + RW_AAA_RANK
    r, k, v = xs[..., :o0], xs[..., o0:o1], xs[..., o1:o2]
    wl, al, gl = xs[..., o2:o3], xs[..., o3:o4], xs[..., o4:]
    w = -jax.nn.softplus(-(w0 + jnp.tanh(wl) @ w_up)) - 0.5
    decay = jnp.exp(-jnp.exp(w.astype(jnp.float32)))
    a = jax.nn.sigmoid(a0 + al @ a_up)
    g = jax.nn.sigmoid(gl) @ g_up

    def heads(t):
        return t.reshape(B, S, RW_HEADS, RW_HEAD_DIM).astype(jnp.float32)

    kk = heads(k * k_k)
    kk = kk / jnp.maximum(jnp.linalg.norm(kk, axis=-1, keepdims=True), 1e-12)
    k = k * (1.0 + (a - 1.0) * k_a)
    rh, kh, vh, ah, wh = heads(r), heads(k), heads(v), heads(a), heads(decay)

    def tm(t):
        return jnp.swapaxes(t, 0, 1)

    state0 = jnp.zeros((B, RW_HEADS, RW_HEAD_DIM, RW_HEAD_DIM), jnp.float32)
    _, y = lax.scan(_rwkv7_step, state0,
                    (tm(rh), tm(wh), tm(kh), tm(vh), tm(-kk), tm(kk * ah)))
    y = tm(y)
    mean = jnp.mean(y, axis=-1, keepdims=True)
    var = jnp.mean(jnp.square(y - mean), axis=-1, keepdims=True)
    y = ((y - mean) * lax.rsqrt(var + RW_GN_EPS)).reshape(B, S, RW_WIDTH)
    y = y * ln_w.astype(jnp.float32) + ln_b.astype(jnp.float32)
    bonus = jnp.sum(rh * kh * r_k.astype(jnp.float32), axis=-1, keepdims=True) * vh
    y = y + bonus.reshape(B, S, RW_WIDTH)
    return (y * g.astype(jnp.float32)).astype(p.dtype)

def first_inputs(seed: int = 0) -> dict:
    key = jax.random.key(seed)
    ks = jax.random.split(key, 28)
    L = DEPTH

    def nrm(k, shape, scale):
        return jax.random.normal(k, shape, jnp.float32) * scale

    return {
        "x": nrm(ks[0], (BATCH, SEQ, D_MODEL), 1.0),
        "w_in": nrm(ks[1], (L, D_MODEL, N_IN), D_MODEL ** -0.5),
        "b_gate": nrm(ks[2], (L, 2 * D_MODEL), 0.01),
        "g_mix_pre": 1.0 + nrm(ks[3], (L, D_MODEL), 0.05),
        "g_mix_post": 1.0 + nrm(ks[4], (L, D_MODEL), 0.05),
        "g_ffn_pre": 1.0 + nrm(ks[5], (L, D_MODEL), 0.05),
        "g_ffn_post": 1.0 + nrm(ks[6], (L, D_MODEL), 0.05),
        "da_lambda_q": nrm(ks[7], (L, 2, DA_HEAD_DIM), 0.1),
        "da_lambda_k": nrm(ks[8], (L, 2, DA_HEAD_DIM), 0.1),
        "da_subln_g": 1.0 + nrm(ks[9], (L, DA_V_DIM), 0.05),
        "rw_mu": jax.random.uniform(ks[10], (L, RW_TOTAL), jnp.float32),
        "rw_w0": jax.random.uniform(ks[11], (L, RW_WIDTH), jnp.float32, minval=-6.0, maxval=0.0),
        "rw_w_up": nrm(ks[12], (L, RW_DECAY_RANK, RW_WIDTH), 0.5 * RW_DECAY_RANK ** -0.5),
        "rw_a0": nrm(ks[13], (L, RW_WIDTH), 0.1),
        "rw_a_up": nrm(ks[14], (L, RW_AAA_RANK, RW_WIDTH), 0.5 * RW_AAA_RANK ** -0.5),
        "rw_g_up": nrm(ks[15], (L, RW_GATE_RANK, RW_WIDTH), RW_GATE_RANK ** -0.5),
        "rw_k_k": 0.85 + nrm(ks[16], (L, RW_WIDTH), 0.05),
        "rw_k_a": 1.0 + nrm(ks[17], (L, RW_WIDTH), 0.05),
        "rw_r_k": nrm(ks[18], (L, RW_HEADS, RW_HEAD_DIM), 0.1),
        "rw_ln_w": 1.0 + nrm(ks[19], (L, RW_WIDTH), 0.05),
        "rw_ln_b": nrm(ks[20], (L, RW_WIDTH), 0.01),
        "w_branch_a": nrm(ks[21], (L, DA_WIDTH, D_MODEL), DA_WIDTH ** -0.5),
        "w_branch_b": nrm(ks[22], (L, RW_WIDTH, D_MODEL), RW_WIDTH ** -0.5),
        "w_out": nrm(ks[23], (L, D_MODEL, D_MODEL), D_MODEL ** -0.5),
        "w_ffn_in": nrm(ks[24], (L, D_MODEL, 2 * D_FF), D_MODEL ** -0.5),
        "w_ffn_out": nrm(ks[25], (L, D_FF, D_MODEL), D_FF ** -0.5),
    }

def first_block(x, w_in, b_gate, g_mix_pre, g_mix_post, g_ffn_pre, g_ffn_post,
              da_lambda_q, da_lambda_k, da_subln_g,
              rw_mu, rw_w0, rw_w_up, rw_a0, rw_a_up, rw_g_up, rw_k_k, rw_k_a, rw_r_k,
              rw_ln_w, rw_ln_b, w_branch_a, w_branch_b, w_out, w_ffn_in, w_ffn_out):
    B, S, _ = x.shape
    pos = jnp.arange(S, dtype=jnp.int32)
    for l in range(DEPTH):
        lambda_init = 0.8 - 0.6 * math.exp(-0.3 * l)
        h = _rmsnorm(x, g_mix_pre[l])
        proj = h @ w_in[l]
        q = _rope(proj[..., OFF_DA_Q:OFF_DA_K].reshape(B, S, DA_HEADS, 2, DA_HEAD_DIM), pos)
        k = _rope(proj[..., OFF_DA_K:OFF_DA_V].reshape(B, S, DA_HEADS, 2, DA_HEAD_DIM), pos)
        v = proj[..., OFF_DA_V:OFF_RW].reshape(B, S, DA_HEADS, DA_V_DIM)
        lq = da_lambda_q[l].astype(jnp.float32)
        lk = da_lambda_k[l].astype(jnp.float32)
        lam = jnp.exp(jnp.sum(lq[0] * lk[0])) - jnp.exp(jnp.sum(lq[1] * lk[1])) + lambda_init
        o_a = _diff_attention(q, k, v, lam, da_subln_g[l], lambda_init)
        o_b = _rwkv7(proj[..., OFF_RW:OFF_GATE], rw_mu[l], rw_w0[l], rw_w_up[l], rw_a0[l],
                     rw_a_up[l], rw_g_up[l], rw_k_k[l], rw_k_a[l], rw_r_k[l],
                     rw_ln_w[l], rw_ln_b[l])
        gates = jax.nn.sigmoid(proj[..., OFF_GATE:] + b_gate[l])
        mix = (gates[..., :D_MODEL] * (o_a @ w_branch_a[l])
               + gates[..., D_MODEL:] * (o_b @ w_branch_b[l])) @ w_out[l]
        x = x + _rmsnorm(mix, g_mix_post[l])
        h = _rmsnorm(x, g_ffn_pre[l])
        gu = h @ w_ffn_in[l]
        f = jax.nn.silu(gu[..., :D_FF]) * gu[..., D_FF:]
        x = x + _rmsnorm(f @ w_ffn_out[l], g_ffn_post[l])
    return x


HEAD_DIM = 64
S5_CH = D_MODEL // 4
S5_GROUP = 16
S5_NG = S5_CH // S5_GROUP
S5_P = 64
SB_HEADS = D_MODEL // 4 // HEAD_DIM
SB_W = SB_HEADS * HEAD_DIM
NSA_HEADS = D_MODEL // 2 // HEAD_DIM
NSA_KV = 4
NSA_REP = NSA_HEADS // NSA_KV
NSA_W = NSA_HEADS * HEAD_DIM
NSA_KV_W = NSA_KV * HEAD_DIM
CMP_LEN = 32
CMP_STRIDE = 16
CMP_HID = 128
SEL_BLOCK = 64
SEL_TOPN = 16
WINDOW = 512
FORCE_SCORE = 1e4
N_BUCKETS = 32
MAX_DIST = 1024
N_MEM = 256
XA_HEADS = 4
XA_HEAD_DIM = 128
XA_W = XA_HEADS * XA_HEAD_DIM
D_FF_2 = 256 * ((8 * D_MODEL // 3 + 255) // 256)
CONV_W = 3
ALPHA = (2.0 * DEPTH) ** 0.25
BETA = (8.0 * DEPTH) ** -0.25
LN_EPS = 1e-5
IN_SIZES = (S5_CH, SB_W, SB_W, SB_W, NSA_W,
            NSA_KV_W, NSA_KV_W, NSA_KV_W, NSA_KV_W, NSA_KV_W, NSA_KV_W, 3 * NSA_HEADS)
N_IN_2 = sum(IN_SIZES)
D_MIX = S5_CH + SB_W + NSA_W


def layer_norm(x, g, b):
    xf = x.astype(jnp.float32)
    mu = jnp.mean(xf, axis=-1, keepdims=True)
    var = jnp.mean(jnp.square(xf - mu), axis=-1, keepdims=True)
    return ((xf - mu) * lax.rsqrt(var + LN_EPS) * g + b).astype(x.dtype)

def masked_softmax(logits, mask):
    l = jnp.where(mask, logits.astype(jnp.float32), -1e30)
    m = jnp.max(l, axis=-1, keepdims=True)
    e = jnp.where(mask, jnp.exp(l - m), 0.0)
    return e / jnp.maximum(jnp.sum(e, axis=-1, keepdims=True), 1e-30)

def t5_bucket(dist):
    n = jnp.maximum(dist, 0)
    max_exact = N_BUCKETS // 2
    nf = jnp.maximum(n, 1).astype(jnp.float32)
    large = max_exact + (jnp.log(nf / max_exact) / math.log(MAX_DIST / max_exact)
                         * (N_BUCKETS - max_exact)).astype(jnp.int32)
    large = jnp.minimum(large, N_BUCKETS - 1)
    return jnp.where(n < max_exact, n, large)

def _complex_affine(e1, e2):
    a1r, a1i, b1r, b1i = e1
    a2r, a2i, b2r, b2i = e2
    return (a2r * a1r - a2i * a1i,
            a2r * a1i + a2i * a1r,
            a2r * b1r - a2i * b1i + b2r,
            a2r * b1i + a2i * b1r + b2i)

def s5_mixer(u, lam_re, lam_im, log_dt, b_re, b_im, c_re, c_im, d, w_glu, b_glu):
    bsz, t_len, _ = u.shape
    uf = u.astype(jnp.float32)
    ug = uf.reshape(bsz, t_len, S5_NG, S5_GROUP)
    lr = lam_re.astype(jnp.float32)
    li = lam_im.astype(jnp.float32)
    delta = jnp.exp(log_dt.astype(jnp.float32))[:, None]
    mag = jnp.exp(lr * delta)
    ar = mag * jnp.cos(li * delta)
    ai = mag * jnp.sin(li * delta)
    den = lr * lr + li * li
    cr = ((ar - 1.0) * lr + ai * li) / den
    ci = (ai * lr - (ar - 1.0) * li) / den
    br = cr[..., None] * b_re - ci[..., None] * b_im
    bi = cr[..., None] * b_im + ci[..., None] * b_re
    xr_in = jnp.einsum('btgc,gpc->btgp', ug, br)
    xi_in = jnp.einsum('btgc,gpc->btgp', ug, bi)
    a_r = jnp.broadcast_to(ar, xr_in.shape)
    a_i = jnp.broadcast_to(ai, xr_in.shape)
    _, _, sr, si = lax.associative_scan(_complex_affine, (a_r, a_i, xr_in, xi_in), axis=1)
    y = jnp.einsum('btgp,gcp->btgc', sr, c_re) - jnp.einsum('btgp,gcp->btgc', si, c_im)
    y = y.reshape(bsz, t_len, S5_CH) + d * uf
    z = jax.nn.gelu(y)
    out = z * jax.nn.sigmoid(z @ w_glu + b_glu)
    return out.astype(u.dtype)

def stick_breaking(q, k, v):
    bsz, t_len, n_h, hd = q.shape
    scale = hd ** -0.5
    kpos = jnp.arange(t_len)

    def block(q0):
        qb = lax.dynamic_slice_in_dim(q, q0, Q_BLOCK, axis=1)
        z = jnp.einsum('bqhd,bkhd->bhqk', qb, k).astype(jnp.float32) * scale
        t = q0 + jnp.arange(Q_BLOCK)
        mask = kpos[None, :] < t[:, None]
        log1m = jnp.where(mask, jax.nn.log_sigmoid(-z), 0.0)
        later = lax.cumsum(log1m, axis=3, reverse=True) - log1m
        w = jnp.where(mask, jnp.exp(jax.nn.log_sigmoid(z) + later), 0.0)
        o = jnp.einsum('bhqk,bkhd->bqhd', w.astype(v.dtype), v)
        return o.reshape(bsz, Q_BLOCK, n_h * hd)

    starts = jnp.arange(t_len // Q_BLOCK) * Q_BLOCK
    o = lax.map(block, starts)
    return o.transpose(1, 0, 2, 3).reshape(bsz, t_len, n_h * hd)

def nsa_mixer(q, k_cmp, v_cmp, k_slc, v_slc, k_swa, v_swa, gates,
              cmp_pos, cmp_w1, cmp_w2, rel_bias):
    bsz, t_len, n_h, hd = q.shape
    n_g, n_r = NSA_KV, NSA_REP
    scale = hd ** -0.5
    n_cmp = (t_len - CMP_LEN) // CMP_STRIDE + 1
    n_sel = t_len // SEL_BLOCK
    top_n = min(SEL_TOPN, n_sel)

    cmp_start = jnp.arange(n_cmp) * CMP_STRIDE
    idx = cmp_start[:, None] + jnp.arange(CMP_LEN)[None, :]

    def compress(kv, j):
        blk = kv[:, idx] + cmp_pos[j][None, None, :, None, :]
        blk = blk.transpose(0, 1, 3, 2, 4).reshape(bsz, n_cmp, n_g, CMP_LEN * hd)
        return jax.nn.gelu(blk @ cmp_w1[j]) @ cmp_w2[j]

    kc = compress(k_cmp, 0)
    vc = compress(v_cmp, 1)
    cmp_end = cmp_start + CMP_LEN - 1
    sel_ids = jnp.arange(n_sel)
    overlap = ((cmp_start[:, None] < (sel_ids[None, :] + 1) * SEL_BLOCK)
               & (cmp_end[:, None] >= sel_ids[None, :] * SEL_BLOCK)).astype(jnp.float32)

    kb = k_slc.reshape(bsz, n_sel, SEL_BLOCK, n_g, hd).transpose(0, 3, 1, 2, 4)
    vb = v_slc.reshape(bsz, n_sel, SEL_BLOCK, n_g, hd).transpose(0, 3, 1, 2, 4)
    pad = ((0, 0), (WINDOW, 0), (0, 0), (0, 0))
    kw = jnp.pad(k_swa, pad)
    vw = jnp.pad(v_swa, pad)

    tab = rel_bias.astype(jnp.float32)
    tab_g = tab.reshape(N_BUCKETS, n_g, n_r).transpose(1, 0, 2)
    b_idx = jnp.arange(bsz)[:, None, None, None]
    g_idx = jnp.arange(n_g)[None, :, None, None]

    def head_bias(dist):
        return tab[t5_bucket(dist)].reshape(*dist.shape, n_g, n_r).transpose(2, 3, 0, 1)

    def block(q0):
        t = q0 + jnp.arange(Q_BLOCK)
        qb = lax.dynamic_slice_in_dim(q, q0, Q_BLOCK, axis=1).reshape(bsz, Q_BLOCK, n_g, n_r, hd)
        dist_c = t[:, None] - cmp_end[None, :]
        s_c = jnp.einsum('bqgrd,bngd->bgrqn', qb, kc).astype(jnp.float32) * scale + head_bias(dist_c)
        p_c = masked_softmax(s_c, dist_c >= 0)
        o_c = jnp.einsum('bgrqn,bngd->bqgrd', p_c.astype(vc.dtype), vc)
        imp = jnp.einsum('bgrqn,nj->bgqj', p_c, overlap)
        cur = t // SEL_BLOCK
        forced = ((sel_ids[None, :] == 0) | (sel_ids[None, :] == cur[:, None])
                  | (sel_ids[None, :] == cur[:, None] - 1))
        valid = sel_ids[None, :] <= cur[:, None]
        score = jnp.where(valid, jnp.where(forced, FORCE_SCORE, imp), -1.0)
        _, sel = lax.top_k(score, top_n)
        ks = kb[b_idx, g_idx, sel].reshape(bsz, n_g, Q_BLOCK, top_n * SEL_BLOCK, hd)
        vs = vb[b_idx, g_idx, sel].reshape(bsz, n_g, Q_BLOCK, top_n * SEL_BLOCK, hd)
        pos_s = sel[..., None] * SEL_BLOCK + jnp.arange(SEL_BLOCK)
        dist_s = (t[:, None, None] - pos_s).reshape(bsz, n_g, Q_BLOCK, top_n * SEL_BLOCK)
        bias_s = tab_g[g_idx, t5_bucket(dist_s)].transpose(0, 1, 4, 2, 3)
        s_s = jnp.einsum('bqgrd,bgqmd->bgrqm', qb, ks).astype(jnp.float32) * scale + bias_s
        p_s = masked_softmax(s_s, (dist_s >= 0)[:, :, None])
        o_s = jnp.einsum('bgrqm,bgqmd->bqgrd', p_s.astype(vs.dtype), vs)
        kwb = lax.dynamic_slice_in_dim(kw, q0, WINDOW + Q_BLOCK, axis=1)
        vwb = lax.dynamic_slice_in_dim(vw, q0, WINDOW + Q_BLOCK, axis=1)
        pos_w = q0 - WINDOW + jnp.arange(WINDOW + Q_BLOCK)
        dist_w = t[:, None] - pos_w[None, :]
        mask_w = (dist_w >= 0) & (dist_w < WINDOW) & (pos_w[None, :] >= 0)
        s_w = jnp.einsum('bqgrd,bkgd->bgrqk', qb, kwb).astype(jnp.float32) * scale + head_bias(dist_w)
        p_w = masked_softmax(s_w, mask_w)
        o_w = jnp.einsum('bgrqk,bkgd->bqgrd', p_w.astype(vwb.dtype), vwb)
        gb = lax.dynamic_slice_in_dim(gates, q0, Q_BLOCK, axis=1).reshape(bsz, Q_BLOCK, n_g, n_r, 3)
        o = gb[..., 0:1] * o_c + gb[..., 1:2] * o_s + gb[..., 2:3] * o_w
        return o.reshape(bsz, Q_BLOCK, n_h * hd)

    starts = jnp.arange(t_len // Q_BLOCK) * Q_BLOCK
    o = lax.map(block, starts)
    return o.transpose(1, 0, 2, 3).reshape(bsz, t_len, n_h * hd)

def hybrid_mixer(h, w_in, w_out, lam_re, lam_im, log_dt, b_re, b_im, c_re, c_im, d,
                 w_glu, b_glu, cmp_pos, cmp_w1, cmp_w2, rel_bias):
    bsz, t_len, _ = h.shape
    proj = h @ w_in
    offsets = tuple(int(o) for o in np.cumsum(IN_SIZES)[:-1])
    (u5, sq, sk, sv, nq, kc, vc, ksl, vsl, ksw, vsw, g) = jnp.split(proj, offsets, axis=-1)

    def heads(a, n):
        return a.reshape(bsz, t_len, n, HEAD_DIM)

    y_s5 = s5_mixer(u5, lam_re, lam_im, log_dt, b_re, b_im, c_re, c_im, d, w_glu, b_glu)
    y_sb = stick_breaking(heads(sq, SB_HEADS), heads(sk, SB_HEADS), heads(sv, SB_HEADS))
    gates = jax.nn.sigmoid(g.reshape(bsz, t_len, NSA_HEADS, 3))
    y_nsa = nsa_mixer(heads(nq, NSA_HEADS), heads(kc, NSA_KV), heads(vc, NSA_KV),
                      heads(ksl, NSA_KV), heads(vsl, NSA_KV), heads(ksw, NSA_KV), heads(vsw, NSA_KV),
                      gates, cmp_pos, cmp_w1, cmp_w2, rel_bias)
    return jnp.concatenate([y_s5, y_sb, y_nsa], axis=-1) @ w_out

def memory_cross_attention(h, mem, wq, wkv, wo):
    bsz, t_len, _ = h.shape
    n_mem = mem.shape[1]
    q = (h @ wq).reshape(bsz, t_len, XA_HEADS, XA_HEAD_DIM)
    k, v = jnp.split(mem @ wkv, 2, axis=-1)
    k = k.reshape(bsz, n_mem, XA_HEADS, XA_HEAD_DIM)
    v = v.reshape(bsz, n_mem, XA_HEADS, XA_HEAD_DIM)
    s = jnp.einsum('bqhd,bmhd->bhqm', q, k).astype(jnp.float32) * (XA_HEAD_DIM ** -0.5)
    p = jax.nn.softmax(s, axis=-1)
    o = jnp.einsum('bhqm,bmhd->bqhd', p.astype(v.dtype), v).reshape(bsz, t_len, XA_W)
    return o @ wo

def conv_ffn(h, w_up, conv_w, conv_b, w_down):
    u = h @ w_up
    ch = u.shape[-1]
    u = lax.conv_general_dilated(u, conv_w[:, None, :], window_strides=(1,),
                                 padding=((CONV_W - 1, 0),),
                                 dimension_numbers=('NWC', 'WIO', 'NWC'),
                                 feature_group_count=ch) + conv_b
    a, g = jnp.split(u, 2, axis=-1)
    return (a * jax.nn.gelu(g)) @ w_down

def second_inputs(seed: int = 0) -> dict:
    key = jax.random.key(seed)
    ks = iter(jax.random.split(key, 32))
    f32 = jnp.float32
    L = DEPTH

    def nrm(shape, scale):
        return scale * jax.random.normal(next(ks), shape, f32)

    lam_im0 = math.pi * jnp.arange(S5_P, dtype=f32)
    return {
        "x": nrm((BATCH, SEQ, D_MODEL), 1.0),
        "mem": nrm((BATCH, N_MEM, D_MODEL), 1.0),
        "w_in": nrm((L, D_MODEL, N_IN_2), D_MODEL ** -0.5),
        "w_out": nrm((L, D_MIX, D_MODEL), BETA * D_MIX ** -0.5),
        "s5_lambda_re": -0.5 + nrm((L, S5_NG, S5_P), 0.01),
        "s5_lambda_im": lam_im0 + nrm((L, S5_NG, S5_P), 0.01),
        "s5_log_dt": jax.random.uniform(next(ks), (L, S5_NG), f32, math.log(0.001), math.log(0.1)),
        "s5_b_re": nrm((L, S5_NG, S5_P, S5_GROUP), (2 * S5_GROUP) ** -0.5),
        "s5_b_im": nrm((L, S5_NG, S5_P, S5_GROUP), (2 * S5_GROUP) ** -0.5),
        "s5_c_re": nrm((L, S5_NG, S5_GROUP, S5_P), (2 * S5_P) ** -0.5),
        "s5_c_im": nrm((L, S5_NG, S5_GROUP, S5_P), (2 * S5_P) ** -0.5),
        "s5_d": nrm((L, S5_CH), 1.0),
        "s5_w_glu": nrm((L, S5_CH, S5_CH), S5_CH ** -0.5),
        "s5_b_glu": nrm((L, S5_CH), 0.01),
        "nsa_cmp_pos": nrm((L, 2, CMP_LEN, HEAD_DIM), 0.02),
        "nsa_cmp_w1": nrm((L, 2, CMP_LEN * HEAD_DIM, CMP_HID), (CMP_LEN * HEAD_DIM) ** -0.5),
        "nsa_cmp_w2": nrm((L, 2, CMP_HID, HEAD_DIM), CMP_HID ** -0.5),
        "rel_bias": nrm((N_BUCKETS, NSA_HEADS), 0.1),
        "xa_wq": nrm((L, D_MODEL, XA_W), D_MODEL ** -0.5),
        "xa_wkv": nrm((L, D_MODEL, 2 * XA_W), D_MODEL ** -0.5),
        "xa_wo": nrm((L, XA_W, D_MODEL), BETA * XA_W ** -0.5),
        "ffn_w_up": nrm((L, D_MODEL, 2 * D_FF_2), D_MODEL ** -0.5),
        "ffn_conv_w": nrm((L, CONV_W, 2 * D_FF_2), CONV_W ** -0.5),
        "ffn_conv_b": nrm((L, 2 * D_FF_2), 0.01),
        "ffn_w_down": nrm((L, D_FF_2, D_MODEL), BETA * D_FF_2 ** -0.5),
        "ln_g": 1.0 + nrm((L, 3, D_MODEL), 0.01),
        "ln_b": nrm((L, 3, D_MODEL), 0.01),
    }

def second_block(x, mem, w_in, w_out, s5_lambda_re, s5_lambda_im, s5_log_dt, s5_b_re, s5_b_im,
              s5_c_re, s5_c_im, s5_d, s5_w_glu, s5_b_glu, nsa_cmp_pos, nsa_cmp_w1, nsa_cmp_w2,
              rel_bias, xa_wq, xa_wkv, xa_wo, ffn_w_up, ffn_conv_w, ffn_conv_b, ffn_w_down,
              ln_g, ln_b):
    h = x
    for l in range(DEPTH):
        mix = hybrid_mixer(h, w_in[l], w_out[l], s5_lambda_re[l], s5_lambda_im[l], s5_log_dt[l],
                           s5_b_re[l], s5_b_im[l], s5_c_re[l], s5_c_im[l], s5_d[l],
                           s5_w_glu[l], s5_b_glu[l], nsa_cmp_pos[l], nsa_cmp_w1[l], nsa_cmp_w2[l],
                           rel_bias)
        h = layer_norm(ALPHA * h + mix, ln_g[l, 0], ln_b[l, 0])
        xa = memory_cross_attention(h, mem, xa_wq[l], xa_wkv[l], xa_wo[l])
        h = layer_norm(ALPHA * h + xa, ln_g[l, 1], ln_b[l, 1])
        ff = conv_ffn(h, ffn_w_up[l], ffn_conv_w[l], ffn_conv_b[l], ffn_w_down[l])
        h = layer_norm(ALPHA * h + ff, ln_g[l, 2], ln_b[l, 2])
    return h


def setup_inputs(seed=0):
    out = dict(first_inputs(seed))
    for name, value in second_inputs(seed + 1).items():
        if name != "x":
            out[name + "_2"] = value
    return out


def reference(
    x, w_in, b_gate, g_mix_pre, g_mix_post, g_ffn_pre, g_ffn_post, da_lambda_q, da_lambda_k,
    da_subln_g, rw_mu, rw_w0, rw_w_up, rw_a0, rw_a_up, rw_g_up, rw_k_k, rw_k_a, rw_r_k, rw_ln_w,
    rw_ln_b, w_branch_a, w_branch_b, w_out, w_ffn_in, w_ffn_out, mem_2, w_in_2, w_out_2,
    s5_lambda_re_2, s5_lambda_im_2, s5_log_dt_2, s5_b_re_2, s5_b_im_2, s5_c_re_2, s5_c_im_2,
    s5_d_2, s5_w_glu_2, s5_b_glu_2, nsa_cmp_pos_2, nsa_cmp_w1_2, nsa_cmp_w2_2, rel_bias_2,
    xa_wq_2, xa_wkv_2, xa_wo_2, ffn_w_up_2, ffn_conv_w_2, ffn_conv_b_2, ffn_w_down_2, ln_g_2,
    ln_b_2,
):
    x = first_block(
        x, w_in, b_gate, g_mix_pre, g_mix_post, g_ffn_pre, g_ffn_post, da_lambda_q, da_lambda_k,
        da_subln_g, rw_mu, rw_w0, rw_w_up, rw_a0, rw_a_up, rw_g_up, rw_k_k, rw_k_a, rw_r_k,
        rw_ln_w, rw_ln_b, w_branch_a, w_branch_b, w_out, w_ffn_in, w_ffn_out,
    )
    return second_block(
        x, mem_2, w_in_2, w_out_2, s5_lambda_re_2, s5_lambda_im_2, s5_log_dt_2, s5_b_re_2,
        s5_b_im_2, s5_c_re_2, s5_c_im_2, s5_d_2, s5_w_glu_2, s5_b_glu_2, nsa_cmp_pos_2,
        nsa_cmp_w1_2, nsa_cmp_w2_2, rel_bias_2, xa_wq_2, xa_wkv_2, xa_wo_2, ffn_w_up_2,
        ffn_conv_w_2, ffn_conv_b_2, ffn_w_down_2, ln_g_2, ln_b_2,
    )


_drawn_inputs = setup_inputs


def setup_inputs(seed=0):
    import zlib

    import numpy as np

    out = dict(_drawn_inputs(seed))
    spreads = {}
    factors = {'b_gate': 8.0,
     'rw_w_up': 4.356,
     'rw_k_k': 8.106,
     'rw_ln_b': 8.0,
     's5_lambda_re_2': 64.0,
     's5_lambda_im_2': 64.0,
     's5_log_dt_2': 64.0,
     's5_b_re_2': 64.0,
     's5_b_im_2': 64.0,
     's5_c_re_2': 64.0,
     's5_c_im_2': 64.0,
     's5_b_glu_2': 64.0,
     'nsa_cmp_pos_2': 35.389,
     'rel_bias_2': 6.234,
     'ffn_conv_b_2': 34.545,
     'ln_g_2': 8.275,
     'ln_b_2': 8.452}
    for name, (base, spread) in spreads.items():
        noise = np.random.default_rng([zlib.crc32(name.encode()), seed]).standard_normal(out[name].shape)
        drawn = base * np.exp(spread * noise) if base else spread * noise
        out[name] = __import__('jax').numpy.asarray(drawn.astype(out[name].dtype))
    for name, factor in factors.items():
        out[name] = (out[name] * factor).astype(out[name].dtype)
    return out
```

```python
import math
from contextlib import ExitStack

import numpy as np

import concourse.bass as bass
from concourse import mybir

F32 = mybir.dt.float32
ALU = mybir.AluOpType
ACT = mybir.ActivationFunctionType
AX = mybir.AxisListType

P = 128
D = 2048
T = 256
DB = D // P
D_FF = 5632
FB = D_FF // P
DA_HEADS = 8
DA_W = 2048
LORA = 96
GATE_RANK = 256
RW_HEADS = 32
RW_TILES = RW_HEADS // 2
C = 64
NCH = T // C
EPS = 1e-6
DA_EPS = 1e-5
GN_EPS = 1e-5 * 64
LN_EPS = 1e-5
LAMBDA_INIT = 0.8 - 0.6 * math.exp(-0.3 * 0)
ALPHA = 2.0 ** 0.25
NEG = -1e30
ARENA = 19328

RING = 4
SLOT = 16 * 256
STAGES = [
    ("rkv", 24, 1, 16, "T"), ("lora", 2, 1, 16, "T"), ("qk", 16, 1, 16, "T"), ("v", 8, 1, 16, "R"),
    ("gates", 16, 1, 16, "T"),
    ("branch_a", 8, 1, 16, "T"), ("branch_b", 8, 1, 16, "T"), ("out", 8, 1, 16, "T"),
    ("ffn_in", 44, 1, 16, "T"), ("ffn_out", 8, 4, 11, "T"),
    ("u5", 2, 1, 16, "T"), ("sqk", 4, 1, 16, "T"), ("sv", 2, 1, 16, "R"), ("nq", 4, 1, 16, "T"),
    ("nkc", 2, 1, 16, "T"), ("nk", 2, 1, 16, "T"), ("nv", 2, 1, 16, "R"), ("ng", 1, 1, 16, "R"),
    ("mem_k", 2, 1, 16, "T"), ("mem_v", 2, 1, 16, "R"),
    ("out2", 8, 1, 16, "T"), ("xq", 2, 1, 16, "T"), ("xo", 8, 0.25, 4, "T"),
    ("up2", 44, 1, 16, "T"), ("down2", 8, 4, 11, "T"),
]
STORED = ("rkv", "lora", "qk", "v", "gates", "mem_k", "mem_v", "u5", "sqk", "sv", "nq", "nkc", "nk", "nv", "ng", "xq")


class Stage:

    def __init__(self, name, units, slots, blocks, layout, slot, bank, store):
        self.name, self.units, self.slots, self.blocks, self.layout = name, units, slots, blocks, layout
        self.slot, self.bank, self.store = slot, bank, store


def plan():
    slot = bank = store = 0
    out = {}
    for name, units, slots, blocks, layout in STAGES:
        out[name] = Stage(name, units, slots, blocks, layout, slot, bank, store)
        slot += int(units * slots)
        bank += units
        store += units if name in STORED else 0
    return out, slot, store


PLAN, N_SLOTS, N_STORED = plan()


RW_PACK = ["mu_r", "mu_k", "mu_v", "w0", "a0", "k_k", "k_a", "r_k", "ln_w", "ln_b"]
RW_PW = 4 * P + len(RW_PACK)
KEEP = {"AR": 512, "rows": 768, "GK": 512, "GBR": 256, "bonus": 256, "g": 256, "PC": 4}
KEEP_AT, _at = {}, 0
for _n, _w in KEEP.items():
    KEEP_AT[_n] = (_at, _at + _w)
    _at += _w
KEEP_W = _at

CONSTS = [("identity", P), ("ones", P), ("ones_mean", P), ("head_ones", P), ("head_mean", P), ("rotate", P),
          ("cos", T), ("sin", T), ("chunk_keep", T), ("gram_mask", P), ("chunk_mask", 384),
          ("later", P), ("past_mask", 384)]
CONST_AT, _at = {}, 0
for _n, _w in CONSTS:
    CONST_AT[_n] = (_at, _at + _w)
    _at += _w
CONST_W = _at

NORMS = ["g_mix_pre", "g_mix_post", "g_ffn_pre", "g_ffn_post", "ln_w", "ln_b", "b_gate_a", "b_gate_b",
         "ln_g0", "ln_g1", "ln_g2", "ln_b0", "ln_b1", "ln_b2"]
MISC = [("mu_wl", 1), ("mu_al", 1), ("mu_gl0", 1), ("mu_gl1", 1), ("lam_q", 2), ("lam_k", 2), ("subln", 2),
        ("s5_d", 4), ("s5_b_glu", 4), ("lam_re", 16), ("lam_im", 16), ("log_dt", 16)]
MISC_AT, _at = {}, 0
for _n, _w in MISC:
    MISC_AT[_n] = (_at, _at + _w)
    _at += _w
MISC_W = _at


def constants():
    c = np.zeros((P, CONST_W), np.float32)
    i = np.arange(P)

    def put(name, value):
        a, b = CONST_AT[name]
        c[:, a:b] = value

    put("identity", np.eye(P))
    put("ones", 1.0)
    put("ones_mean", 1.0 / D)
    same = (i[:, None] // 64 == i[None, :] // 64).astype(np.float32)
    put("head_ones", same)
    put("head_mean", same / 64)
    rot = np.zeros((P, P), np.float32)
    rot[i[64:], i[:64]] = -1.0
    rot[i[:64], i[64:]] = 1.0
    put("rotate", rot)
    half = 64
    inv = np.float32(10000.0) ** (-np.arange(half, dtype=np.float32) / np.float32(half))
    ang = (np.arange(T, dtype=np.float32)[None, :] * inv[:, None].astype(np.float32)).astype(np.float64)
    put("cos", np.concatenate([np.cos(ang)] * 2))
    put("sin", np.concatenate([np.sin(ang)] * 2))
    put("chunk_keep", (np.arange(T) % C != 0)[None, :].astype(np.float32))
    s, t = (i % 64)[:, None], np.arange(64)[None, :]
    put("gram_mask", np.concatenate([s < t, s <= t], 1))
    q, k = i[:, None], i[None, :]
    diag = np.where(k // 64 <= q // 64, 0.0, NEG)
    put("chunk_mask", np.concatenate([np.zeros((P, P)), diag, diag], 1))
    put("later", i[:, None] > i[None, :])
    kk, qq = i[:, None], np.arange(T)[None, :]
    put("past_mask", np.concatenate([kk < qq, (kk < qq)[:, 0:P]], 1))
    return c


N_BUCKETS, MAX_DIST = 32, 1024
NSA_CONSTS = [("onehot_cmp", 2 * 15 * P), ("onehot_rows", T), ("cmp_add", 30), ("cmp_mul", 30),
              ("tab", 16), ("w2", 128), ("pos", 32), ("flip", P)]
NSA_AT, _at = {}, 0
for _n, _w in NSA_CONSTS:
    NSA_AT[_n] = (_at, _at + _w)
    _at += _w
NSA_CONST_W = _at


def bucket(dist):
    n = np.maximum(dist, 0)
    exact = N_BUCKETS // 2
    nf = np.maximum(n, 1).astype(np.float32)
    large = exact + (np.log(nf / np.float32(exact)) / np.float32(math.log(MAX_DIST / exact))
                     * np.float32(N_BUCKETS - exact)).astype(np.int32)
    return np.where(n < exact, n, np.minimum(large, N_BUCKETS - 1))


def nsa_constants(c):
    def put(name, value):
        a, b = NSA_AT[name]
        c[:value.shape[0], a:b] = value

    q = np.arange(T).reshape(2, 1, P)
    end = 16 * np.arange(15).reshape(1, 15, 1) + 31
    put("onehot_cmp", (bucket(q - end)[None] == np.arange(N_BUCKETS)[:, None, None, None]).reshape(N_BUCKETS, -1))
    put("onehot_rows", bucket(T - 1 - np.arange(T))[None, :] == np.arange(N_BUCKETS)[:, None])
    seen = (q >= end).transpose(2, 0, 1).reshape(P, 30)
    put("cmp_add", np.where(seen, 0.0, NEG))
    put("cmp_mul", seen)
    put("flip", 8.0 * np.eye(P)[::-1])


def build(nc, t_in, t_out):
    ctx = ExitStack()
    with ctx:
        def sb(name, shape):
            return ctx.enter_context(nc.sbuf_tensor(name, shape, F32))

        def scratch(name, shape):
            return nc.dram_tensor(name, shape, F32).ap()

        sems = {}

        def sem(name):
            if name not in sems:
                sems[name] = ctx.enter_context(nc.semaphore(name))
            return sems[name]

        ring = sb("weight_ring", [P, RING, SLOT])
        xT = sb("xT", [P, DB, T])
        hT = sb("hT", [P, DB, T])
        yT = sb("yT", [P, DB, T])
        ostage = sb("out_stage", [P, RING, 512])
        arena = sb("arena", [P, ARENA])
        consts = sb("consts", [P, CONST_W])
        params = sb("params", [P, 16 * len(NORMS) + MISC_W])
        small = sb("small", [P, 64])
        psg = [ctx.enter_context(nc.psum_tensor(f"product_bank{i}", [P, 512], F32)) for i in range(4)]
        pm = [ctx.enter_context(nc.psum_tensor(f"mixer_bank{i}", [P, 512], F32)) for i in range(4)]

        def const(name):
            a, b = CONST_AT[name]
            return consts[:, a:b]

        def norm_param(name):
            n = NORMS.index(name)
            return params[:, 16 * n:16 * n + 16]

        def misc(name):
            a, b = MISC_AT[name]
            return params[:, 16 * len(NORMS) + a:16 * len(NORMS) + b]

        def carve(*widths, at=0):
            out = []
            for w in widths:
                out.append(arena[:, at:at + w])
                at += w
            assert at <= ARENA, at
            return out

        units = scratch("units", [N_STORED, P, 512])
        keep = scratch("rwkv_keep", [RW_TILES, P, KEEP_W])
        l_units = scratch("l_units", [P, C * C])
        m_units = scratch("m_units", [P, C * C])
        bias_rows = scratch("bias_rows", [16, 384])
        kc_dram = scratch("kc_dram", [4, C, 16])

        weights = t_in["weights"]

        w_ready = [sem(f"weight_slot{s}_ready") for s in range(RING)]
        w_used = sem("weight_slots_used")
        bank_free = [sem(f"product_bank{s}_free") for s in range(4)]
        stored = [sem(f"out_stage{s}_stored") for s in range(RING)]

        def stream_weights(sp):
            for s in range(RING):
                sp.dma_start(ring[:, s, :], weights[s, :, :]).then_inc(w_ready[s], 16)
            turns = N_SLOTS // RING
            with sp.Fori(1, turns) as i:
                for s in range(RING):
                    g = sp.snap(i * RING + s)
                    used = sp.snap(i * RING + (s - RING + 1))
                    sp.wait_ge(w_used, used)
                    sp.dma_start(ring[:, s, :], weights[bass.ds(g, 1), :, :].rearrange("o p n -> p (o n)"))\
                        .then_inc(w_ready[s], 16)
            for g in range(turns * RING, N_SLOTS):
                sp.wait_ge(w_used, g - RING + 1)
                sp.dma_start(ring[:, g % RING, :], weights[g, :, :]).then_inc(w_ready[g % RING], 16)

        def run(steps):
            for _ in steps:
                pass

        def weave(products_, mixer, every):
            for n, _ in enumerate(mixer):
                for _ in range(every(n) if callable(every) else every):
                    next(products_, None)
            run(products_)

        def chain(*parts):
            for part in parts:
                yield from part

        def groups(eng, st):
            def over(body):
                first = 1 if (st.bank < 4 or st.slot < RING) else 0
                if st.units % 4 or st.units // 4 - first < 2 or st.slots < 1:
                    for u in range(st.units):
                        body(0, u)
                    return
                for u in range(4 * first):
                    body(0, u)
                with eng.Fori(first, st.units // 4) as i:
                    for j in range(4):
                        body(i, j)
            return over

        def wait(eng, s, value):
            if not isinstance(value, int) or value > 0:
                eng.wait_ge(s, value)

        def products(pe, name, src, ready=None, count=1):
            st = PLAN[name]
            if ready:
                pe.wait_ge(sem(ready), count)
            per_slot = max(1, int(1 / st.slots))
            slots = int(max(1, st.slots))

            def unit(i, j):
                b = (st.bank + j) % 4
                bank = psg[b]
                wait(pe, bank_free[b], i + (st.bank + j) // 4)
                for n in range(slots):
                    q = st.slot + (j // per_slot) * slots + n
                    s = q % RING
                    if j % per_slot == 0:
                        pe.wait_ge(w_ready[s], 16 * slots * i + 16 * (q // RING + 1))
                    cols = 256 * per_slot
                    w = ring[:, s, 0:st.blocks * cols].rearrange("p (k n) -> p k n", n=cols)
                    w = w[:, :, (j % per_slot) * 256:(j % per_slot) * 256 + 256]
                    for half in range(2):
                        for k in range(st.blocks):
                            kk = n * st.blocks + k
                            if st.layout == "T":
                                lhs, rhs = w[:, k, half * P:half * P + P], src[:, kk, :]
                            else:
                                lhs, rhs = src[:, kk, half * P:half * P + P], w[:, k, :]
                            out = bank[:, half * T:half * T + T]
                            first = kk == 0 and (slots == 1 or half == 0)
                            mm = pe.matmul(out, lhs, rhs, start=first, stop=kk == slots * st.blocks - 1,
                                           skip_group_check=slots > 1)
                    if j % per_slot == per_slot - 1:
                        mm.then_inc(w_used, 1)
            groups(pe, st)(unit)

        def quarters(pe, name, src, ready=None, count=1):
            st = PLAN[name]
            if ready:
                pe.wait_ge(sem(ready), count)
            for u in range(st.units):
                b, s = (st.bank + u) % 4, (st.slot + u) % RING
                wait(pe, bank_free[b], (st.bank + u) // 4)
                pe.wait_ge(w_ready[s], 16 * ((st.slot + u) // RING + 1))
                w = ring[:, s, :].rearrange("p (k n) -> p k n", n=256)
                for half in range(2):
                    for k in range(16):
                        if st.layout == "T":
                            lhs, rhs = w[:, k, half * P:half * P + P], src[:, k, :]
                        else:
                            lhs, rhs = src[:, k, half * P:half * P + P], w[:, k, :]
                        mm = pe.matmul(psg[b][:, half * T:half * T + T], lhs, rhs, start=k == 0, stop=k == 15)
                        if k == 7 or (k == 15 and half == 0):
                            yield
                mm.then_inc(w_used, 1)
                yield

        def unit_done(eng, st, i, j):
            slots, per_slot = int(max(1, st.slots)), max(1, int(1 / st.slots))
            eng.wait_ge(w_used, i * 4 * slots + st.slot + (j // per_slot + 1) * slots)

        def store_units(act, name):
            st = PLAN[name]

            def unit(i, j):
                b, o = (st.bank + j) % 4, (st.store + j) % RING
                unit_done(act, st, i, j)
                wait(act, stored[o], 16 * i + 16 * ((st.store + j) // RING))
                act.activation(ostage[:, o, :], psg[b][:, :], ACT.Copy).then_inc(bank_free[b], 1)
                act.wait_ge(bank_free[b], i + (st.bank + j) // 4 + 1)
                row = i * 4 + (st.store + j)
                act.dma_start(units[bass.ds(row, 1), :, :].rearrange("o p n -> p (o n)") if not isinstance(row, int)
                              else units[row, :, :], ostage[:, o, :]).then_inc(stored[o], 16)
            groups(act, st)(unit)

        def store_quarters(act, name):
            st = PLAN[name]
            for u in range(st.units):
                yield
                yield
                yield
                b, o = (st.bank + u) % 4, (st.store + u) % RING
                unit_done(act, st, 0, u)
                wait(act, stored[o], 16 * ((st.store + u) // RING))
                act.activation(ostage[:, o, :], psg[b][:, :], ACT.Copy).then_inc(bank_free[b], 1)
                act.wait_ge(bank_free[b], (st.bank + u) // 4 + 1)
                act.dma_start(units[st.store + u, :, :], ostage[:, o, :]).then_inc(stored[o], 16)
                yield

        def stage_stored(eng, name):
            st = PLAN[name]
            end = st.store + st.units
            for o in range(RING):
                wait(eng, stored[o], 16 * ((end - o + RING - 1) // RING))

        def load_inputs(pool):
            pool.dma_start(xT[:, :, :], t_in["xT"]).then_inc(sem("x_loaded"), 16)
            pool.dma_start(consts[:, :], t_in["consts"]).then_inc(sem("consts_loaded"), 16)
            pool.dma_start(params[:, :], t_in["params"]).then_inc(sem("params_loaded"), 16)
            pool.memset(small[:, 0:1], EPS)
            pool.memset(small[:, 1:2], DA_EPS)
            pool.memset(small[:, 2:3], GN_EPS)
            pool.memset(small[:, 3:4], LN_EPS)
            pool.memset(small[:, 4:5], math.pi / 2).then_inc(sem("small_set"), 1)
        eps_col = {EPS: 0, DA_EPS: 1, GN_EPS: 2}

        def norm_space():
            sq, r = carve(DB * T, T, at=11264)
            return sq.rearrange("p (b t) -> p b t", b=DB), r

        def bc_b(v):
            return v.unsqueeze(1).to_broadcast([P, DB, T])

        def bc_t(v):
            return v.unsqueeze(2).to_broadcast([P, DB, T])

        TURN = {n: k + 1 for k, n in enumerate(["mix_pre", "mix_post", "ffn_pre", "ffn_post", "norm1", "norm2", "norm3"])}

        def rms_act(act, tag, src, ready=None):
            sq, r = norm_space()
            if ready:
                act.wait_ge(sem(ready), 1)
            act.activation(sq, src, ACT.Square).then_inc(sem("norm_squares"), 1)
            act.wait_ge(sem("norm_sum"), TURN[tag])
            act.activation(r, pm[0][:, 0:T], ACT.Sqrt, bias=small[:, 0:1]).then_inc(sem("norm_root"), 1)

        def rms_pe(pe, tag):
            sq, r = norm_space()
            pe.wait_ge(sem("norm_squares"), TURN[tag])
            for b in range(DB):
                mm = pe.matmul(pm[0][:, 0:T], const("ones_mean"), sq[:, b, :], start=b == 0, stop=b == DB - 1)
            mm.then_inc(sem("norm_sum"), 1)

        def rms_dve(dve, tag, src, gain, dst, add_to=None, done=None):
            sq, r = norm_space()
            dve.wait_ge(sem("norm_root"), TURN[tag])
            dve.reciprocal(r, r)
            dve.drain()
            dve.tensor_tensor(dst, src, bc_b(r), ALU.mult)
            dve.drain()
            last = dve.tensor_tensor(dst, dst, bc_t(norm_param(gain)), ALU.mult)
            if add_to is not None:
                dve.drain()
                last = dve.tensor_tensor(add_to, add_to, dst, ALU.add)
            last.then_inc(sem(done), 1)

        def ln_act(act, n):
            sq, r = norm_space()
            act.wait_ge(sem("ln_centred"), n)
            act.activation(sq, yT[:, :, :], ACT.Square).then_inc(sem("norm_squares"), 1)
            act.wait_ge(sem("norm_sum"), 4 + n)
            act.activation(r, pm[1][:, 0:T], ACT.Sqrt, bias=small[:, 3:4]).then_inc(sem("norm_root"), 1)

        def ln_pe(pe, n):
            sq, r = norm_space()
            pe.wait_ge(sem("ln_added"), n)
            for b in range(DB):
                mm = pe.matmul(pm[0][:, 0:T], const("ones_mean"), yT[:, b, :], start=b == 0, stop=b == DB - 1)
            mm.then_inc(sem("ln_mean"), 1)
            pe.wait_ge(sem("norm_squares"), 4 + n)
            for b in range(DB):
                mm = pe.matmul(pm[1][:, 0:T], const("ones_mean"), sq[:, b, :], start=b == 0, stop=b == DB - 1)
            mm.then_inc(sem("norm_sum"), 1)

        def ln_dve(dve, n):
            sq, r = norm_space()
            dve.wait_ge(sem("y_ready"), 2 + n)
            dve.scalar_tensor_tensor(yT[:, :, :], xT[:, :, :], ALPHA, yT[:, :, :], ALU.mult, ALU.add)\
                .then_inc(sem("ln_added"), 1)
            dve.wait_ge(sem("ln_mean"), n)
            dve.tensor_copy(r, pm[0][:, 0:T])
            dve.drain()
            dve.tensor_tensor(yT[:, :, :], yT[:, :, :], bc_b(r), ALU.subtract).then_inc(sem("ln_centred"), 1)
            dve.wait_ge(sem("norm_root"), 4 + n)
            dve.reciprocal(r, r)
            dve.drain()
            dve.tensor_tensor(yT[:, :, :], yT[:, :, :], bc_b(r), ALU.mult)
            dve.drain()
            dve.tensor_tensor(yT[:, :, :], yT[:, :, :], bc_t(norm_param(f"ln_g{n - 1}")), ALU.mult)
            dve.drain()
            dve.tensor_tensor(xT[:, :, :], yT[:, :, :], bc_t(norm_param(f"ln_b{n - 1}")), ALU.add)\
                .then_inc(sem("ln_done"), 1)

        def into_y(act, name):
            st = PLAN[name]

            def unit(i, j):
                b = (st.bank + j) % 4
                unit_done(act, st, i, j)
                act.activation(yT[:, 2 * j:2 * j + 2, :], psg[b][:, :].rearrange("p (h t) -> p h t", h=2),
                               ACT.Copy).then_inc(bank_free[b], 1)
            for u in range(st.units):
                unit(0, u)
            act.drain().then_inc(sem("y_ready"), 1)

        rw = {}
        (rw["wl"], rw["al"], rw["gl"], rw["pack"], rw["p"], rw["x"], rw["sg"], rw["a"], rw["g"], rw["kk"],
         rw["sq"], rw["nrm"], rw["cum"], rw["cumex"], rw["Pex"], rw["Pin"], rw["Pinv"], rw["kka"], rw["Bt"],
         rw["kp"], rw["Kt"], rw["AR"], rw["rk"], rw["bonus"], rw["rows"], rw["GB"], rw["GK"], rw["d"]) = carve(
            256, 256, 512, 2 * RW_PW, 2 * 3 * 257, 768, 256, 256, 256, 256,
            256, 256, 256, 256, 256, 256, 256, 256, 256,
            256, 256, 512, 256, 256, 768, 512, 512, 256, at=4096)
        rwp = rw["pack"].rearrange("p (s n) -> p s n", s=2)
        rwx = rw["p"].rearrange("p (s c n) -> p s c n", s=2, c=3)
        PC_out = small[:, 8:12]
        KEPT = 16 * 9

        def rwkv_unit(u):
            st = PLAN["rkv"]
            return units[st.store + u, :, :]

        def rw1_pool(pool):
            pool.memset(rwx[:, :, :, 0:1], 0.0).then_inc(sem("rw_prev_zero"), 1)
            stage_stored(pool, "lora")
            lo = PLAN["lora"].store
            pool.dma_start(arena[:, 4096:4096 + 512], units[lo, :, :]).then_inc(sem("lora_loaded"), 16)
            pool.dma_start(rw["gl"], units[lo + 1, :, :]).then_inc(sem("lora_loaded"), 16)
            for b in range(RW_TILES):
                s = b % 2
                if b >= 2:
                    pool.wait_ge(sem("rw1_tile_done"), b - 1)
                got = sem(f"rw1_in{s}")
                pool.dma_start(rwp[:, s, :], t_in["rw_pack"][b, :, :]).then_inc(got, 16)
                for c in range(3):
                    j = 16 * c + b
                    pool.dma_start(rwx[:, s, c, 1:257], rwkv_unit(j // 2)[:, (j % 2) * T:(j % 2) * T + T])\
                        .then_inc(got, 16)

        def pcol(s, name):
            c = 4 * P + RW_PACK.index(name)
            return rwp[:, s, c:c + 1]

        xr, xk, xv = (rw["x"][:, 256 * c:256 * c + 256] for c in range(3))

        def rw1_dve(dve):
            dve.wait_ge(sem("lora_loaded"), 32)
            dve.wait_ge(sem("consts_loaded"), 16)
            dve.wait_ge(sem("params_loaded"), 16)
            for n, (buf, mu) in enumerate([(rw["wl"], "mu_wl"), (rw["al"], "mu_al"),
                                           (rw["gl"][:, 0:256], "mu_gl0"), (rw["gl"][:, 256:512], "mu_gl1")]):
                if n:
                    dve.drain()
                dve.tensor_tensor(rw["d"][:, 1:256], buf[:, 0:255], buf[:, 1:256], ALU.subtract)
                dve.tensor_scalar(rw["d"][:, 0:1], buf[:, 0:1], -1.0, None, ALU.mult)
                dve.drain()
                last = dve.scalar_tensor_tensor(buf, rw["d"], misc(mu), buf, ALU.mult, ALU.add)
            last.then_inc(sem("lora_mixed"), 1)
            dve.wait_ge(sem("rw_prev_zero"), 1)
            dve.wait_ge(sem("lora_ready"), 1)

            def tile(i, s):
                b1 = 2 * i + s + 1
                dve.wait_ge(sem(f"rw1_in{s}"), 64 * i + 64)
                if not (isinstance(i, int) and i == 0 and s == 0):
                    dve.wait_ge(sem("rw1_keeps"), KEPT * (b1 - 1))
                dx = rw["GB"]
                for c, (x, mu) in enumerate([(xr, "mu_r"), (xk, "mu_k"), (xv, "mu_v")]):
                    t = [rw["d"], rw["kka"], rw["kp"]][c]
                    dve.tensor_tensor(t, rwx[:, s, c, 0:256], rwx[:, s, c, 1:257], ALU.subtract)
                dve.drain()
                for c, (x, mu) in enumerate([(xr, "mu_r"), (xk, "mu_k"), (xv, "mu_v")]):
                    t = [rw["d"], rw["kka"], rw["kp"]][c]
                    last = dve.scalar_tensor_tensor(x, t, pcol(s, mu), rwx[:, s, c, 1:257], ALU.mult, ALU.add)
                dve.drain()
                dve.tensor_scalar(rw["kk"], xk, pcol(s, "k_k"), None, ALU.mult).then_inc(sem("rw1_kk_raw"), 1)
                yield
                dve.wait_ge(sem("rw1_sigmoids"), b1)
                dve.tensor_scalar(rw["sg"], rw["sg"], -math.exp(-0.5), None, ALU.mult)
                dve.tensor_scalar(rw["kp"], rw["a"], -1.0, pcol(s, "k_a"), ALU.add, ALU.mult)
                dve.drain()
                dve.tensor_tensor_scan(rw["cum"], const("chunk_keep"), rw["sg"], 0.0, ALU.mult, ALU.add)
                dve.scalar_tensor_tensor(rw["kp"], rw["kp"], 1.0, xk, ALU.add, ALU.mult)
                dve.drain()
                dve.tensor_tensor(rw["cumex"], rw["cum"], rw["sg"], ALU.subtract)
                dve.scalar_tensor_tensor(rw["rk"], xr, pcol(s, "r_k"), rw["kp"], ALU.mult, ALU.mult)\
                    .then_inc(sem("rw1_cum"), 1)
                dve.wait_ge(sem("rw1_norm"), b1)
                dve.tensor_scalar(rw["nrm"], rw["nrm"], 1e-12, None, ALU.max)
                dve.drain()
                dve.reciprocal(rw["nrm"], rw["nrm"])
                dve.drain()
                dve.tensor_tensor(rw["kk"], rw["kk"], rw["nrm"], ALU.mult)
                dve.drain()
                dve.tensor_tensor(rw["kka"], rw["kk"], rw["a"], ALU.mult)
                dve.wait_ge(sem("rw1_powers"), b1)
                ar = rw["AR"].rearrange("p (c w t) -> p c w t", c=NCH, w=2)
                v3 = lambda v: v.rearrange("p (c t) -> p c t", c=NCH)
                dve.scalar_tensor_tensor(ar[:, :, 0, :], v3(rw["kk"]), -1.0, v3(rw["Pex"]), ALU.mult, ALU.mult)
                dve.drain()
                dve.tensor_tensor(ar[:, :, 1, :], v3(xr), v3(rw["Pin"]), ALU.mult)
                dve.tensor_tensor(rw["Bt"], rw["kka"], rw["Pinv"], ALU.mult)
                dve.tensor_tensor(rw["Kt"], rw["kp"], rw["Pinv"], ALU.mult)
                dve.tensor_copy(PC_out, rw["Pin"][:, C - 1:T:C]).then_inc(sem("rw1_operands"), 1)
                yield
                dve.wait_ge(sem("rw1_bonus_sum"), b1)
                dve.tensor_tensor(rw["bonus"], pm[0][:, 256:512], xv, ALU.mult).then_inc(sem("rw1_bonus"), 1)
                dve.wait_ge(sem("rw1_grams"), b1)
                m = const("gram_mask").unsqueeze(1).to_broadcast([P, 2, 128])
                for head in range(2):
                    for kind, dst in enumerate([rw["GB"], rw["GK"]]):
                        two = lambda v: v.rearrange("p (u n) -> p u n", u=2)
                        last = dve.tensor_tensor(two(dst[:, 256 * head:256 * head + 256]),
                                                 two(pm[1 + head][:, 256 * kind:256 * kind + 256]), m, ALU.mult)
                last.then_inc(sem("rw1_tile_done"), 1)
                yield

            for b in range(RW_TILES):
                yield from tile(b // 2, b % 2)

        def rw1_act(act):
            act.wait_ge(sem("lora_mixed"), 1)
            act.activation(rw["wl"], rw["wl"], ACT.Tanh)
            act.activation(rw["gl"], rw["gl"], ACT.Sigmoid).then_inc(sem("lora_ready"), 1)

            def keep_tile(i, s):
                b1 = 2 * i + s + 1
                act.wait_ge(sem("rw1_tile_done"), b1)
                act.wait_ge(sem("rw1_rows"), b1)
                row = 2 * i + s
                dst = keep[row, :, :] if isinstance(i, int) else keep[bass.ds(row, 1), :, :].rearrange("o p n -> p (o n)")
                for name, src in [("AR", rw["AR"]), ("rows", rw["rows"]), ("GK", rw["GK"]),
                                  ("bonus", rw["bonus"]), ("g", rw["g"]), ("PC", PC_out)]:
                    a, z = KEEP_AT[name]
                    act.dma_start(dst[:, a:z], src).then_inc(sem("rw1_keeps"), 16)
                a, z = KEEP_AT["GBR"]
                gb = rw["GB"].rearrange("p (u w t) -> p u w t", u=4, w=2)
                act.dma_start(dst[:, a:z].rearrange("p (u t) -> p u t", u=4), gb[:, :, 1, :]).then_inc(sem("rw1_keeps"), 16)
                for par in range(2):
                    base = 8 * row if isinstance(i, int) else 8 * row
                    src = gb[64 * par:64 * par + 64, :, 0, :]
                    lu = l_units.rearrange("(b u par) (s t) -> b par s u t", u=4, par=2, s=C)
                    d = lu[row, par, :, :, :] if isinstance(i, int) else \
                        lu[bass.ds(row, 1), par, :, :, :].rearrange("o s u t -> s (o u) t")
                    act.dma_start(d, src).then_inc(sem("rw1_keeps"), 16)

            def tile(i, s):
                b1 = 2 * i + s + 1
                if b1 > 1:
                    act.wait_ge(sem("rw1_keeps"), KEPT * (b1 - 1))
                act.wait_ge(sem("rw1_lora_w"), b1)
                act.activation(rw["sg"], pm[3][:, 0:256], ACT.Sigmoid, bias=pcol(s, "w0"))
                act.activation(rw["a"], pm[3][:, 256:512], ACT.Sigmoid, bias=pcol(s, "a0"))
                act.wait_ge(sem("rw1_lora_g"), b1)
                act.activation(rw["g"], pm[1][:, 0:256], ACT.Copy).then_inc(sem("rw1_sigmoids"), 1)
                act.wait_ge(sem("rw1_kk_raw"), b1)
                act.activation(rw["sq"], rw["kk"], ACT.Square).then_inc(sem("rw1_kk_sq"), 1)
                yield
                act.wait_ge(sem("rw1_kk_sum"), b1)
                act.activation(rw["nrm"], pm[0][:, 0:256], ACT.Sqrt).then_inc(sem("rw1_norm"), 1)
                act.wait_ge(sem("rw1_cum"), b1)
                act.activation(rw["Pex"], rw["cumex"], ACT.Exp)
                act.activation(rw["Pin"], rw["cum"], ACT.Exp)
                act.activation(rw["Pinv"], rw["cum"], ACT.Exp, scale=-1.0).then_inc(sem("rw1_powers"), 1)
                yield
                act.wait_ge(sem("rw1_turned"), b1)
                r = rw["rows"].rearrange("p (q n) -> p q n", q=6)
                act.activation(r[:, 0:4, :], pm[3][:, 0:512].rearrange("p (q n) -> p q n", q=4), ACT.Copy)
                act.activation(r[:, 4:6, :], pm[0][:, 0:256].rearrange("p (q n) -> p q n", q=2), ACT.Copy)\
                    .then_inc(sem("rw1_rows"), 1)
                keep_tile(i, s)
                yield

            for b in range(RW_TILES):
                yield from tile(b // 2, b % 2)

        def rw1_pe(pe):
            pe.wait_ge(sem("lora_ready"), 1)

            def tile(i, s):
                b1 = 2 * i + s + 1
                pe.wait_ge(sem(f"rw1_in{s}"), 64 * i + 64)
                if not (isinstance(i, int) and i == 0 and s == 0):
                    pe.wait_ge(sem("rw1_rows"), b1 - 1)
                    pe.wait_ge(sem("rw1_tile_done"), b1 - 1)
                    pe.wait_ge(sem("rw1_bonus"), b1 - 1)
                pe.matmul(pm[3][:, 0:256], rwp[0:LORA, s, 0:P], rw["wl"][0:LORA, :], start=True, stop=True)
                pe.matmul(pm[3][:, 256:512], rwp[0:LORA, s, P:2 * P], rw["al"][0:LORA, :], start=True, stop=True)\
                    .then_inc(sem("rw1_lora_w"), 1)
                pe.matmul(pm[1][:, 0:256], rwp[:, s, 2 * P:3 * P], rw["gl"][:, 0:256], start=True, stop=False)
                pe.matmul(pm[1][:, 0:256], rwp[:, s, 3 * P:4 * P], rw["gl"][:, 256:512], start=False, stop=True)\
                    .then_inc(sem("rw1_lora_g"), 1)
                yield
                pe.wait_ge(sem("rw1_kk_sq"), b1)
                pe.matmul(pm[0][:, 0:256], const("head_ones"), rw["sq"], start=True, stop=True)\
                    .then_inc(sem("rw1_kk_sum"), 1)
                pe.wait_ge(sem("rw1_norm"), b1)
                pe.wait_ge(sem("rw1_cum"), b1)
                pe.matmul(pm[0][:, 256:512], const("head_ones"), rw["rk"], start=True, stop=True)\
                    .then_inc(sem("rw1_bonus_sum"), 1)
                yield
                pe.wait_ge(sem("rw1_operands"), b1)
                for q, src in enumerate([rw["Bt"], rw["Kt"], xv]):
                    for half in range(2):
                        n = 2 * q + half
                        if n == 4:
                            pe.wait_ge(sem("rw1_bonus"), b1)
                        out = pm[3][:, n * P:n * P + P] if n < 4 else pm[0][:, (n - 4) * P:(n - 4) * P + P]
                        mm = pe.transpose(out, src[:, half * P:half * P + P], const("identity"))
                mm.then_inc(sem("rw1_turned"), 1)
                for kind, src in enumerate([rw["Bt"], rw["Kt"]]):
                    for c in range(NCH):
                        for head in range(2):
                            j = slice(64 * head, 64 * head + 64)
                            u = 2 * kind + c // 2
                            mm = pe.matmul(pm[1 + head][64 * (c % 2):64 * (c % 2) + 64, u * 128:u * 128 + 128],
                                           src[j, c * C:c * C + C], rw["AR"][j, c * 128:c * 128 + 128],
                                           start=True, stop=True)
                mm.then_inc(sem("rw1_grams"), 1)
                yield

            for b in range(RW_TILES):
                yield from tile(b // 2, b % 2)

        inv_L, inv_M = carve(C * C, C * C, at=4096)
        inv_tmp = yT[:, :, :].rearrange("p b t -> p (b t)")

        def inv_pool(pool):
            pool.wait_ge(sem("rw1_keeps"), KEPT * RW_TILES)
            pool.dma_start(inv_L, l_units).then_inc(sem("inv_in"), 16)

        def inv_dve(dve):
            dve.wait_ge(sem("rw1_keeps"), KEPT * RW_TILES)
            L = inv_L.rearrange("p (s t) -> p s t", s=C)
            M = inv_M.rearrange("p (c t) -> p c t", c=C)
            dve.memset(inv_M, 0.0)
            dve.drain()
            dve.memset(inv_M[:, 0:C * C:C + 1], 1.0)
            dve.wait_ge(sem("inv_in"), 16)
            dve.drain()
            for t in range(1, C):
                tmp = inv_tmp[:, 0:t * t].rearrange("p (c s) -> p c s", c=t)
                dve.tensor_tensor(tmp, M[:, 0:t, 0:t],
                                  L[:, 0:t, t:t + 1].rearrange("p s o -> p o s").to_broadcast([P, t, t]), ALU.mult)
                dve.drain()
                last = dve.reduce_sum(M[:, 0:t, t:t + 1], tmp, AX.X)
                dve.drain()
                yield
            dve.nop().then_inc(sem("inv_done"), 1)

        def inv_act(act):
            act.wait_ge(sem("inv_done"), 1)
            act.dma_start(m_units, inv_M).then_inc(sem("inv_stored"), 16)

        GT = 4
        r2_keep, r2_M, r2_X, r2_U, r2_S, r2_Y, r2_d, r2_sq = carve(
            GT * KEEP_W, GT * 256, 512, 512, 256, GT * 256, 512, 512, at=4096)
        r2k = r2_keep.rearrange("p (g n) -> p g n", g=GT)
        r2m = r2_M.rearrange("p (g u t) -> p g u t", g=GT, u=4)
        obT = yT

        def kept(name, g):
            a, z = KEEP_AT[name]
            return r2k[:, g, a:z]

        def rw2_pool(pool):
            pool.wait_ge(sem("inv_stored"), 16)
            pool.wait_ge(sem("attn_head_done"), DA_HEADS)
            for n in range(RW_TILES // GT):
                if n:
                    pool.wait_ge(sem("rw2_group_done"), n)
                for g in range(GT):
                    b = GT * n + g
                    pool.dma_start(r2k[:, g, :], keep[b, :, :]).then_inc(sem("rw2_in"), 16)
                    for par in range(2):
                        mu = m_units.rearrange("(b u par) (s t) -> b par s u t", u=4, par=2, s=C)
                        pool.dma_start(r2m[64 * par:64 * par + 64, g, :, :], mu[b, par, :, :, :])\
                            .then_inc(sem("rw2_in"), 16)

        def rw2_steps(n):
            return 16 * 3 * GT * (n + 1)

        def rw2_pe(pe):
            def group(n):
                pe.wait_ge(sem("rw2_in"), rw2_steps(n))
                for c in range(NCH):
                    k = NCH * n + c
                    tb = slice(64 * (c % 2), 64 * (c % 2) + 64)
                    pe.wait_ge(sem("rw2_S"), k + 1)
                    par = c % 2
                    row = lambda q, g, head: kept("rows", g)[tb, q * 256 + (c // 2) * P + 64 * head:
                                                            q * 256 + (c // 2) * P + 64 * head + 64]
                    heads = [(g, head) for g in range(GT) for head in range(2)]

                    def by_rows(terms):
                        seen = set()
                        for rows in (0, 1):
                            if rows:
                                pe.drain()
                            for r, quadrant, out, lhs, rhs in terms:
                                if r == rows:
                                    last = pe.matmul(out, lhs, rhs, start=quadrant not in seen, stop=True,
                                                     skip_group_check=True)
                                    seen.add(quadrant)
                        return last

                    terms = []
                    for g, head in heads:
                        h, j, u = 2 * g + head, slice(64 * head, 64 * head + 64), 2 * head + c // 2
                        out = pm[0][tb, h * 64:h * 64 + 64]
                        terms.append((head, par, out, kept("AR", g)[j, c * 128:c * 128 + 64], r2_S[j, g * 64:g * 64 + 64]))
                        terms.append((par, par, out, kept("GK", g)[tb, u * 128:u * 128 + 64], row(2, g, head)))
                    by_rows(terms).then_inc(sem("rw2_X_sum"), 1)
                    yield
                    pe.wait_ge(sem("rw2_X"), k + 1)
                    for g, head in heads:
                        h, u = 2 * g + head, 2 * head + c // 2
                        mm = pe.matmul(pm[1][tb, h * 64:h * 64 + 64], r2m[tb, g, u, :],
                                       r2_X[tb, h * 64:h * 64 + 64], start=True, stop=True)
                    mm.then_inc(sem("rw2_U_sum"), 1)
                    yield
                    pe.wait_ge(sem("rw2_U"), k + 1)
                    for g, head in heads:
                        h, j = 2 * g + head, slice(64 * head, 64 * head + 64)
                        out = pm[3][j, g * 64:g * 64 + 64]
                        pe.matmul(out, row(0, g, head), r2_U[tb, h * 64:h * 64 + 64], start=True, stop=False)
                        mm = pe.matmul(out, row(1, g, head), row(2, g, head), start=False, stop=True)
                    mm.then_inc(sem("rw2_S_sum"), 1)
                    if k:
                        pe.wait_ge(sem("rw2_Y"), k)
                    terms = []
                    for g, head in heads:
                        h, j, u = 2 * g + head, slice(64 * head, 64 * head + 64), 2 * head + c // 2
                        out = pm[2][j, g * 64:g * 64 + 64]
                        terms.append((head, head, out, r2_S[j, g * 64:g * 64 + 64],
                                      kept("AR", g)[j, c * 128 + 64:c * 128 + 128]))
                        terms.append((par, head, out, r2_U[tb, h * 64:h * 64 + 64], kept("GBR", g)[tb, u * 64:u * 64 + 64]))
                        terms.append((par, head, out, row(2, g, head), kept("GK", g)[tb, u * 128 + 64:u * 128 + 128]))
                    by_rows(terms).then_inc(sem("rw2_Y_sum"), 1)
                    yield
                for pair in range(GT // 2):
                    q = (GT // 2) * n + pair
                    pe.wait_ge(sem("rw2_Y"), NCH * (n + 1))
                    pe.matmul(pm[0][:, :], const("head_mean"), r2_Y[:, pair * 512:pair * 512 + 512], start=True, stop=True)\
                        .then_inc(sem("rw2_mean"), 1)
                    yield
                    pe.wait_ge(sem("rw2_sq"), q + 1)
                    pe.matmul(pm[1][:, :], const("head_mean"), r2_sq, start=True, stop=True).then_inc(sem("rw2_var"), 1)
                    yield
            for n in range(RW_TILES // GT):
                yield from group(n)

        def rw2_act(act):
            def group(n):
                for c in range(NCH):
                    k = NCH * n + c
                    tb = slice(64 * (c % 2), 64 * (c % 2) + 64)
                    act.wait_ge(sem("rw2_X_sum"), k + 1)
                    act.activation(r2_X[tb, :], pm[0][tb, :], ACT.Copy).then_inc(sem("rw2_X"), 1)
                    yield
                    act.wait_ge(sem("rw2_U_sum"), k + 1)
                    act.activation(r2_U[tb, :], pm[1][tb, :], ACT.Copy).then_inc(sem("rw2_U"), 1)
                    yield
                    act.wait_ge(sem("rw2_Y_sum"), k + 1)
                    if n and c == 0:
                        act.wait_ge(sem("rw2_group_done"), n)
                    act.activation(r2_Y.rearrange("p (g t) -> p g t", g=GT)[:, :, c * C:c * C + C],
                                   pm[2][:, 0:256].rearrange("p (g t) -> p g t", g=GT), ACT.Copy)\
                        .then_inc(sem("rw2_Y"), 1)
                    yield
                for pair in range(GT // 2):
                    q = (GT // 2) * n + pair
                    act.wait_ge(sem("rw2_centred"), q + 1)
                    act.activation(r2_sq, r2_d, ACT.Square).then_inc(sem("rw2_sq"), 1)
                    yield
                    act.wait_ge(sem("rw2_var"), q + 1)
                    act.activation(r2_sq, pm[1][:, :], ACT.Sqrt, bias=small[:, 2:3]).then_inc(sem("rw2_root"), 1)
                    yield
            for n in range(RW_TILES // GT):
                yield from group(n)

        def rw2_dve(dve):
            def group(n):
                dve.wait_ge(sem("rw2_in"), rw2_steps(n))
                if n:
                    dve.wait_ge(sem("rw2_Y_sum"), NCH * n)
                dve.memset(r2_S, 0.0).then_inc(sem("rw2_S"), 1)
                for c in range(NCH):
                    k = NCH * n + c
                    dve.wait_ge(sem("rw2_S_sum"), k + 1)
                    if c == NCH - 1:
                        continue
                    S3 = r2_S.rearrange("p (g i) -> p g i", g=GT)
                    dve.wait_ge(sem("rw2_Y_sum"), k + 1)
                    dve.tensor_tensor(S3, S3, pm[3][:, 0:256].rearrange("p (g i) -> p g i", g=GT), ALU.add)
                    dve.drain()
                    a, z = KEEP_AT["PC"]
                    dve.tensor_tensor(S3, S3, r2k[:, :, a + c:a + c + 1].to_broadcast([P, GT, 64]), ALU.mult)\
                        .then_inc(sem("rw2_S"), 1)
                for pair in range(GT // 2):
                    q = (GT // 2) * n + pair
                    y = r2_Y[:, pair * 512:pair * 512 + 512]
                    dve.wait_ge(sem("rw2_mean"), q + 1)
                    if q:
                        dve.drain()
                    dve.tensor_tensor(r2_d, y, pm[0][:, :], ALU.subtract).then_inc(sem("rw2_centred"), 1)
                    dve.wait_ge(sem("rw2_root"), q + 1)
                    dve.reciprocal(r2_sq, r2_sq)
                    dve.drain()
                    dve.tensor_tensor(r2_d, r2_d, r2_sq, ALU.mult)
                    dve.drain()
                    for h in range(2):
                        g = 2 * pair + h
                        b = GT * n + g
                        d = r2_d[:, h * 256:h * 256 + 256]
                        dve.tensor_scalar(d, d, norm_param("ln_w")[:, b:b + 1], norm_param("ln_b")[:, b:b + 1],
                                          ALU.mult, ALU.add)
                        dve.drain()
                        dve.tensor_tensor(d, d, kept("bonus", g), ALU.add)
                        dve.drain()
                        last = dve.tensor_tensor(obT[:, b, :], d, kept("g", g), ALU.mult)
                last.then_inc(sem("rw2_group_done"), 1)
                yield
            for n in range(RW_TILES // GT):
                yield from group(n)

        SB_AT, NSA_AT_HEAD, XA_AT = DA_HEADS, DA_HEADS + 8, DA_HEADS + 8 + 16
        NSA_SOFT_AT, XA_SOFT_AT = DA_HEADS, DA_HEADS + 16
        oaT = arena[:, 0:4096].rearrange("p (b t) -> p b t", b=DB)
        DA_AT = 12288
        (da_in, da_q, da_k, da_t, da_s, da_p, da_pt, da_sq, da_r, da_st) = carve(
            2 * 1536, 512, 512, 512, 768, 384, 384, 512, 256, 16, at=DA_AT)
        dain = da_in.rearrange("p (s c n) -> p s c n", s=2, c=3)
        LAM = small[:, 20:22]

        def da_pool(pool):
            stage_stored(pool, "v")
            for h in range(DA_HEADS):
                s = h % 2
                if h >= 2:
                    pool.wait_ge(sem("attn_head_done"), h - 1)
                elif h == 0:
                    pool.wait_ge(sem("rw1_keeps"), KEPT * RW_TILES)
                for c, row in enumerate([PLAN["qk"].store + h, PLAN["qk"].store + 8 + h, PLAN["v"].store + h]):
                    pool.dma_start(dain[:, s, c, :], units[row, :, :]).then_inc(sem(f"da_in{s}"), 16)

        def da_pe(pe):
            pe.wait_ge(sem("lam_in"), 1)
            pe.wait_ge(sem("rw1_rows"), RW_TILES)
            pe.wait_ge(sem("rw1_tile_done"), RW_TILES)
            pe.matmul(pm[0][:, 0:2], const("ones"), da_st[:, 0:2], start=True, stop=True).then_inc(sem("lam_sum"), 1)
            pe.wait_ge(sem("lam_done"), 1)

            def head(i, s):
                h1 = 2 * i + s + 1
                pe.wait_ge(sem(f"da_in{s}"), 48 * i + 48)
                pe.matmul(pm[0][:, :], const("rotate"), dain[:, s, 0, :], start=True, stop=True)
                pe.matmul(pm[1][:, :], const("rotate"), dain[:, s, 1, :], start=True, stop=True)\
                    .then_inc(sem("da_rotated"), 1)
                yield
                pe.wait_ge(sem("da_roped"), h1)
                for m in range(2):
                    q, k = da_q[:, m * T:m * T + T], da_k[:, m * T:m * T + T]
                    pe.matmul(pm[m][:, 0:256], q[:, P:T], k, start=True, stop=True)
                    mm = pe.matmul(pm[m][:, 256:384], q[:, 0:P], k[:, 0:P], start=True, stop=True)
                mm.then_inc(sem("attn_scores"), 1)
                yield
                pe.wait_ge(sem("attn_probs"), h1)
                pe.transpose(pm[2][:, 0:128], da_p[:, 256:384], const("identity"))
                pe.transpose(pm[2][:, 128:256], da_p[:, 0:128], const("identity"))
                pe.transpose(pm[2][:, 256:384], da_p[:, 128:256], const("identity")).then_inc(sem("attn_turned"), 1)
                yield
                pe.wait_ge(sem("attn_pt"), h1)
                for e in range(2):
                    v = dain[:, s, 2, :].rearrange("p (h e) -> p h e", h=2)
                    pe.matmul(pm[3][:, e * T:e * T + T], v[:, 0, e * P:e * P + P], da_pt[:, 0:256], start=True, stop=False)
                    mm = pe.matmul(pm[3][:, e * T + P:e * T + T], v[:, 1, e * P:e * P + P], da_pt[:, 256:384],
                                   start=False, stop=True)
                mm.then_inc(sem("attn_out"), 1)
                yield
                pe.wait_ge(sem("da_sq"), h1)
                pe.matmul(pm[2][:, 0:256], const("ones"), da_sq[:, 0:256], start=True, stop=False)
                pe.matmul(pm[2][:, 0:256], const("ones"), da_sq[:, 256:512], start=False, stop=True)\
                    .then_inc(sem("da_sq_sum"), 1)
                yield
                pe.wait_ge(sem("attn_head_done"), h1)
            for h in range(DA_HEADS):
                yield from head(h // 2, h % 2)

        def da_dve(dve):
            dve.wait_ge(sem("rw1_keeps"), KEPT * RW_TILES)
            dve.tensor_tensor(da_st[:, 0:2], misc("lam_q"), misc("lam_k"), ALU.mult).then_inc(sem("lam_in"), 1)
            dve.wait_ge(sem("lam_exp"), 1)
            dve.tensor_tensor(LAM[:, 0:1], da_st[:, 3:4], da_st[:, 2:3], ALU.subtract)
            dve.drain()
            dve.tensor_scalar(LAM[:, 1:2], LAM[:, 0:1], -LAMBDA_INIT, None, ALU.add)
            dve.tensor_scalar(da_st[:, 14:16], misc("subln"), 1.0 - LAMBDA_INIT, None, ALU.mult)
            dve.drain().then_inc(sem("lam_done"), 1)

            def head(i, s):
                h1 = 2 * i + s + 1
                h = 2 * i + s
                dve.wait_ge(sem(f"da_in{s}"), 48 * i + 48)
                two = lambda v: v.rearrange("p (m t) -> p m t", m=2)
                rep = lambda n: const(n).unsqueeze(1).to_broadcast([P, 2, T])
                dve.tensor_tensor(two(da_q), two(dain[:, s, 0, :]), rep("cos"), ALU.mult)
                dve.tensor_tensor(two(da_k), two(dain[:, s, 1, :]), rep("cos"), ALU.mult)
                dve.wait_ge(sem("da_rotated"), h1)
                dve.tensor_tensor(two(da_t), two(pm[0][:, :]), rep("sin"), ALU.mult)
                dve.tensor_tensor(two(da_sq), two(pm[1][:, :]), rep("sin"), ALU.mult)
                dve.drain()
                dve.tensor_tensor(da_q, da_q, da_t, ALU.add)
                dve.tensor_tensor(da_k, da_k, da_sq, ALU.add).then_inc(sem("da_roped"), 1)
                yield
                dve.wait_ge(sem("attn_scores"), h1)
                S = da_s.rearrange("p (m n) -> p m n", m=2)
                for m in range(2):
                    dve.tensor_tensor(S[:, m, :], pm[m][:, 0:384], const("chunk_mask"), ALU.add)
                dve.drain()
                dve.reduce_max(da_st[:, 0:2], S[:, :, 0:256], AX.X)
                dve.reduce_max(da_st[:, 2:4], S[:, :, 256:384], AX.X)
                dve.drain()
                dve.tensor_scalar(da_st[:, 4:8], da_st[:, 0:4], -float(P) ** -0.5, None, ALU.mult)\
                    .then_inc(sem("attn_max"), 1)
                dve.wait_ge(sem("attn_exp"), h1)
                dve.reciprocal(da_st[:, 8:12], da_st[:, 8:12])
                dve.drain()
                dve.tensor_scalar(da_st[:, 12:13], da_st[:, 9:10], LAM[:, 1:2], None, ALU.mult)
                dve.tensor_scalar(da_st[:, 13:14], da_st[:, 11:12], LAM[:, 1:2], None, ALU.mult)
                dve.drain()
                for qb, (a, z) in enumerate([(0, 256), (256, 384)]):
                    dve.tensor_scalar(da_t[:, a:z], S[:, 0, a:z], da_st[:, 8 + 2 * qb:9 + 2 * qb], None, ALU.mult)
                dve.drain()
                for qb, (a, z) in enumerate([(0, 256), (256, 384)]):
                    last = dve.scalar_tensor_tensor(da_p[:, a:z], S[:, 1, a:z], da_st[:, 12 + qb:13 + qb], da_t[:, a:z],
                                                    ALU.mult, ALU.add)
                last.then_inc(sem("attn_probs"), 1)
                yield
                yield
                yield
                dve.wait_ge(sem("da_root"), h1)
                dve.reciprocal(da_r, da_r)
                dve.drain()
                for e in range(2):
                    o = oaT[:, 2 * h + e, :] if isinstance(h, int) else \
                        arena[:, bass.ds(h * 512 + e * 256, 256)]
                    last = dve.scalar_tensor_tensor(o, pm[3][:, e * T:e * T + T], da_st[:, 14 + e:15 + e], da_r,
                                                    ALU.mult, ALU.mult)
                last.then_inc(sem("attn_head_done"), 1)
                yield
            for h in range(DA_HEADS):
                yield from head(h // 2, h % 2)

        def da_act(act):
            act.wait_ge(sem("lam_sum"), 1)
            act.activation(da_st[:, 2:4], pm[0][:, 0:2], ACT.Exp).then_inc(sem("lam_exp"), 1)

            def head(i, s):
                h1 = 2 * i + s + 1
                yield
                act.wait_ge(sem("attn_max"), h1)
                S = da_s.rearrange("p (m n) -> p m n", m=2)
                for qb, (a, z) in enumerate([(0, 256), (256, 384)]):
                    for m in range(2):
                        n = 2 * qb + m
                        act.activation(S[:, m, a:z], S[:, m, a:z], ACT.Exp, scale=float(P) ** -0.5,
                                       bias=da_st[:, 4 + n:5 + n], accum_out=da_st[:, 8 + n:9 + n])
                act.drain().then_inc(sem("attn_exp"), 1)
                yield
                act.wait_ge(sem("attn_turned"), h1)
                act.activation(da_pt, pm[2][:, 0:384], ACT.Copy).then_inc(sem("attn_pt"), 1)
                yield
                act.wait_ge(sem("attn_out"), h1)
                act.activation(da_sq, pm[3][:, :], ACT.Square).then_inc(sem("da_sq"), 1)
                yield
                act.wait_ge(sem("da_sq_sum"), h1)
                act.activation(da_r, pm[2][:, 0:256], ACT.Sqrt, scale=1.0 / 256, bias=small[:, 1:2])\
                    .then_inc(sem("da_root"), 1)
                yield
            for h in range(DA_HEADS):
                yield from head(h // 2, h % 2)

        gates = arena[:, 4096:4096 + 8192].rearrange("p (b t) -> p b t", b=32)
        mixT = hT[:, :, :]

        def gates_pool(pool):
            stage_stored(pool, "gates")
            pool.wait_ge(sem("rw2_group_done"), RW_TILES // GT)
            st = PLAN["gates"]
            for n in range(16):
                pool.dma_start(gates[:, 2 * n:2 * n + 2, :].rearrange("p b t -> p (b t)"), units[st.store + n, :, :])\
                    .then_inc(sem(f"gates_in{n // 8}"), 16)

        def branch_a_act(act):
            st = PLAN["branch_a"]
            act.wait_ge(w_used, PLAN["gates"].slot + 16)
            for u in range(8):
                yield
                yield
                yield
                b = (st.bank + u) % 4
                unit_done(act, st, 0, u)
                act.activation(mixT[:, 2 * u:2 * u + 2, :], psg[b][:, :].rearrange("p (h t) -> p h t", h=2), ACT.Copy)\
                    .then_inc(bank_free[b], 1)
                yield
            act.drain().then_inc(sem("branch_a_ready"), 1)

        def gates_dve(dve):
            b = params[:, 16 * NORMS.index("b_gate_a"):16 * NORMS.index("b_gate_a") + 32]
            for w in range(2):
                g = gates[:, 16 * w:16 * w + 16, :]
                dve.wait_ge(sem(f"gates_in{w}"), 128)
                dve.tensor_tensor(g, g, b[:, 16 * w:16 * w + 16].unsqueeze(2).to_broadcast([P, 16, T]), ALU.add)\
                    .then_inc(sem("gates_biased"), 1)
            dve.wait_ge(sem("gates_open"), 1)
            dve.wait_ge(sem("branch_a_ready"), 1)
            dve.tensor_tensor(mixT, mixT, gates[:, 0:16, :], ALU.mult)
            dve.wait_ge(sem("gates_open"), 2)
            st = PLAN["branch_b"]
            for u in range(8):
                b = (st.bank + u) % 4
                unit_done(dve, st, 0, u)
                mix = mixT[:, 2 * u:2 * u + 2, :]
                g = gates[:, 16 + 2 * u:16 + 2 * u + 2, :]
                dve.tensor_tensor(g, psg[b][:, :].rearrange("p (h t) -> p h t", h=2), g, ALU.mult).then_inc(bank_free[b], 1)
                dve.drain()
                dve.tensor_tensor(mix, mix, g, ALU.add)
            dve.drain().then_inc(sem("mix_ready"), 1)

        def gates_act(act):
            for w in range(2):
                g = gates[:, 16 * w:16 * w + 16, :]
                act.wait_ge(sem("gates_biased"), w + 1)
                act.activation(g, g, ACT.Sigmoid).then_inc(sem("gates_open"), 1)

        fT = arena[:, 0:FB * T].rearrange("p (b t) -> p b t", b=FB)
        silu = carve(4 * T, at=16384)[0].rearrange("p (s t) -> p s t", s=4)

        def ffn_act(act):
            st = PLAN["ffn_in"]

            def unit(i, j):
                b = (st.bank + j) % 4
                unit_done(act, st, i, j)
                u = 4 * i + j
                if not (isinstance(u, int) and u < 4):
                    act.wait_ge(sem("ffn_mul"), u - 3)
                act.activation(silu[:, j % 4, :], psg[b][:, 0:T], ACT.Silu).then_inc(sem("ffn_silu"), 1)
            for u in range(4):
                unit(0, u)
            with act.Fori(1, st.units // 4) as i:
                for j in range(4):
                    unit(i, j)

        def ffn_dve(dve):
            st = PLAN["ffn_in"]

            def unit(i, j):
                b = (st.bank + j) % 4
                dve.wait_ge(sem("ffn_silu"), 4 * i + j + 1)
                u = 4 * i + j
                dst = fT[:, u, :] if isinstance(u, int) else arena[:, bass.ds(u * T, T)]
                dve.tensor_tensor(dst, silu[:, j % 4, :], psg[b][:, T:2 * T], ALU.mult)
                dve.drain().then_inc(bank_free[b], 1)
                dve.nop().then_inc(sem("ffn_mul"), 1)
            for u in range(4):
                unit(0, u)
            with dve.Fori(1, st.units // 4) as i:
                for j in range(4):
                    unit(i, j)
            dve.drain().then_inc(sem("ffn_ready"), 1)

        def mem_pool(pool):
            pool.wait_ge(w_used, PLAN["ffn_in"].slot + PLAN["ffn_in"].units)
            pool.dma_start(hT[:, :, :], t_in["memT"]).then_inc(sem("mem_loaded"), 16)

        ST = 16
        (s5_u, s5_Er, s5_Ei, s5_x, s5_z, s5_y) = carve(1024, 4096, 4096, 2048, 1024, 1024)
        s5_t = yT.rearrange("p b t -> p (b t)")
        s5q = arena[:, 14080:14080 + 16 * 24].rearrange("p (n b) -> p n b", b=16)
        s5_BC = s5_t[:, 2048:2048 + 2 * 512].rearrange("p (s n) -> p s n", s=2)
        s5_wglu = arena[:, 14592:14592 + 2048].rearrange("p (k n) -> p k n", k=4)
        uT = s5_u.rearrange("p (b t) -> p b t", b=4)
        s5yT = s5_y.rearrange("p (b t) -> p b t", b=4)
        s5zT = s5_z.rearrange("p (b t) -> p b t", b=4)
        Er, Ei = s5_Er.rearrange("p (b t) -> p b t", b=ST), s5_Ei.rearrange("p (b t) -> p b t", b=ST)
        SQ = ["delta", "mag", "th", "k", "r", "rc", "sin", "cos", "ar1", "ai", "den", "cr", "ci", "nci", "a", "b",
              "pr", "pi"]

        def q5(name):
            return s5q[:, SQ.index(name), :]

        def s5_pool(pool):
            pool.wait_ge(sem("block1_done"), 1)
            pool.dma_start(s5_wglu, t_in["w_glu"]).then_inc(sem("s5_glu_in"), 16)
            stage_stored(pool, "u5")
            for n in range(2):
                pool.dma_start(s5_u[:, 512 * n:512 * n + 512], units[PLAN["u5"].store + n, :, :]).then_inc(sem("s5_u_in"), 16)
            for i in range(ST):
                if i >= 2:
                    pool.wait_ge(sem("s5_tile_read"), i - 1)
                pool.dma_start(s5_BC[:, i % 2, :], t_in["s5_bc"][i, :, :]).then_inc(sem(f"s5_bc_in{i % 2}"), 16)

        def s5_act(act):
            act.wait_ge(sem("block1_done"), 1)
            act.activation(q5("delta"), misc("log_dt"), ACT.Exp).then_inc(sem("s5_delta"), 1)
            act.wait_ge(sem("s5_th"), 1)
            act.activation(q5("mag"), q5("a"), ACT.Exp)
            act.activation(q5("sin"), q5("r"), ACT.Sin)
            act.activation(q5("cos"), q5("rc"), ACT.Sin).then_inc(sem("s5_trig"), 1)
            for ct in range(4):
                act.wait_ge(sem("s5_y"), ct + 1)
                act.activation(s5zT[:, ct, :], s5yT[:, ct, :], ACT.Gelu_apprx_tanh)
            act.drain().then_inc(sem("s5_gelu"), 1)
            for n in range(4):
                act.wait_ge(sem("s5_glu_sum"), n + 1)
                act.activation(s5yT[:, n, :], pm[n % 2][:, 0:T], ACT.Sigmoid, bias=misc("s5_b_glu")[:, n:n + 1])\
                    .then_inc(sem("s5_glu"), 1)

        def s5_dve(dve):
            dr = dve.drain
            tt, ts, stt = dve.tensor_tensor, dve.tensor_scalar, dve.scalar_tensor_tensor
            two_pi = 2 * math.pi
            C1, C2 = 6.28125, float(np.float32(two_pi - 6.28125))
            C3 = two_pi - 6.28125 - C2
            ROUND = 1.5 * 2.0 ** 23
            dve.wait_ge(sem("s5_delta"), 1)
            ts(q5("cr"), misc("lam_re"), 0.0, None, ALU.add)
            tt(q5("a"), misc("lam_re"), q5("delta"), ALU.mult)
            tt(q5("th"), misc("lam_im"), q5("delta"), ALU.mult)
            dr()
            ts(q5("k"), q5("th"), 1 / two_pi, ROUND, ALU.mult, ALU.add)
            dr()
            ts(q5("k"), q5("k"), -ROUND, None, ALU.add)
            dr()
            stt(q5("r"), q5("k"), -C1, q5("th"), ALU.mult, ALU.add)
            dr()
            stt(q5("r"), q5("k"), -C2, q5("r"), ALU.mult, ALU.add)
            dr()
            stt(q5("r"), q5("k"), -C3, q5("r"), ALU.mult, ALU.add)
            dr()
            PI = 3.1415925
            ts(q5("r"), q5("r"), PI, -PI, ALU.min, ALU.max)
            dr()
            ts(q5("rc"), q5("r"), math.pi / 2, None, ALU.add)
            dr()
            ts(q5("b"), q5("rc"), PI, -two_pi, ALU.is_gt, ALU.mult)
            dr()
            tt(q5("rc"), q5("rc"), q5("b"), ALU.add)
            dr()
            ts(q5("rc"), q5("rc"), PI, -PI, ALU.min, ALU.max).then_inc(sem("s5_th"), 1)
            dve.wait_ge(sem("s5_trig"), 1)
            tt(q5("ar1"), q5("mag"), q5("cos"), ALU.mult)
            tt(q5("ai"), q5("mag"), q5("sin"), ALU.mult)
            tt(q5("a"), misc("lam_re"), misc("lam_re"), ALU.mult)
            tt(q5("b"), misc("lam_im"), misc("lam_im"), ALU.mult)
            dr()
            ts(q5("ar1"), q5("ar1"), -1.0, None, ALU.add)
            tt(q5("den"), q5("a"), q5("b"), ALU.add)
            dr()
            dve.reciprocal(q5("den"), q5("den"))
            tt(q5("cr"), q5("ar1"), misc("lam_re"), ALU.mult)
            tt(q5("a"), q5("ai"), misc("lam_im"), ALU.mult)
            tt(q5("ci"), q5("ai"), misc("lam_re"), ALU.mult)
            tt(q5("b"), q5("ar1"), misc("lam_im"), ALU.mult)
            dr()
            tt(q5("cr"), q5("cr"), q5("a"), ALU.add)
            tt(q5("ci"), q5("ci"), q5("b"), ALU.subtract)
            dr()
            tt(q5("cr"), q5("cr"), q5("den"), ALU.mult)
            tt(q5("ci"), q5("ci"), q5("den"), ALU.mult)
            dr()
            ts(q5("nci"), q5("ci"), -1.0, None, ALU.mult)
            dve.tensor_copy(Er[:, :, 0], q5("cos"))
            dve.tensor_copy(Ei[:, :, 0], q5("sin"))
            dr()
            tmp = s5_t[:, 0:2048].rearrange("p (b t) -> p b t", b=ST)
            m = 1
            while m < T:
                br = Er[:, :, m - 1:m].to_broadcast([P, ST, m])
                bi = Ei[:, :, m - 1:m].to_broadcast([P, ST, m])
                a, b = Er[:, :, 0:m], Ei[:, :, 0:m]
                cr_, ci_ = Er[:, :, m:2 * m], Ei[:, :, m:2 * m]
                t0 = tmp[:, :, 0:m]
                tt(t0, b, bi, ALU.mult)
                tt(cr_, a, br, ALU.mult)
                dr()
                tt(cr_, cr_, t0, ALU.subtract)
                dr()
                tt(t0, b, br, ALU.mult)
                tt(ci_, a, bi, ALU.mult)
                dr()
                tt(ci_, ci_, t0, ALU.add)
                dr()
                m *= 2
            X = [s5_x[:, 256 * n:256 * n + 256] for n in range(8)]
            xr5, xi5, wr, wi, t1, t2, zr, zi = X
            for i in range(ST):
                er, ei = Er[:, i, :], Ei[:, i, :]
                col = lambda n: q5(n)[:, i:i + 1]
                dve.wait_ge(sem("s5_in_sum"), i + 1)
                pr, pi = pm[i % 2][:, 0:T], pm[i % 2][:, T:2 * T]
                ts(xr5, pr, col("cr"), None, ALU.mult)
                ts(xi5, pr, col("ci"), None, ALU.mult)
                dr()
                stt(xr5, pi, col("nci"), xr5, ALU.mult, ALU.add)
                stt(xi5, pi, col("cr"), xi5, ALU.mult, ALU.add).then_inc(sem("s5_in_read"), 1)
                dr()
                tt(wr, xr5, er, ALU.mult)
                tt(wi, xi5, er, ALU.mult)
                tt(t1, xi5, ei, ALU.mult)
                tt(t2, xr5, ei, ALU.mult)
                dr()
                tt(wr, wr, t1, ALU.add)
                tt(wi, wi, t2, ALU.subtract)
                dr()
                mag = col("mag").to_broadcast([P, T])
                dve.tensor_tensor_scan(zr, mag, wr, 0.0, ALU.mult, ALU.add)
                dve.tensor_tensor_scan(zi, mag, wi, 0.0, ALU.mult, ALU.add)
                dr()
                S = s5_t[:, 3072 + 512 * (i % 2):3072 + 512 * (i % 2) + 512]
                if i >= 2:
                    dve.wait_ge(sem("s5_tile_read"), i - 1)
                tt(t1, zi, ei, ALU.mult)
                tt(t2, zr, ei, ALU.mult)
                tt(S[:, 0:T], zr, er, ALU.mult)
                tt(S[:, T:2 * T], zi, er, ALU.mult)
                dr()
                tt(S[:, 0:T], S[:, 0:T], t1, ALU.subtract)
                stt(S[:, T:2 * T], S[:, T:2 * T], -1.0, t2, ALU.mult, ALU.subtract).then_inc(sem("s5_states"), 1)
                if i % 4 == 3:
                    ct = i // 4
                    dve.wait_ge(sem("s5_out_sum"), ct + 1)
                    stt(s5yT[:, ct, :], uT[:, ct, :], misc("s5_d")[:, ct:ct + 1], pm[2 + ct % 2][:, 0:T],
                        ALU.mult, ALU.add).then_inc(sem("s5_y"), 1)
            for n in range(4):
                dve.wait_ge(sem("s5_glu"), n + 1)
                last = tt(hT[:, n, :], s5zT[:, n, :], s5yT[:, n, :], ALU.mult)
            last.then_inc(sem("s5_done"), 1)

        def s5_pe(pe):
            pe.wait_ge(sem("s5_u_in"), 32)

            def inputs(i):
                pe.wait_ge(sem(f"s5_bc_in{i % 2}"), 16 * (i // 2 + 1))
                if i >= 2:
                    pe.wait_ge(sem("s5_in_read"), i - 1)
                pe.matmul(pm[i % 2][:, 0:T], s5_BC[:, i % 2, 0:P], uT[:, i // 4, :], start=True, stop=True)
                pe.matmul(pm[i % 2][:, T:2 * T], s5_BC[:, i % 2, P:2 * P], uT[:, i // 4, :], start=True, stop=True)\
                    .then_inc(sem("s5_in_sum"), 1)

            inputs(0)
            for i in range(ST):
                if i + 1 < ST:
                    inputs(i + 1)
                ct = i // 4
                pe.wait_ge(sem("s5_states"), i + 1)
                if i % 4 == 0 and ct >= 2:
                    pe.wait_ge(sem("s5_y"), ct - 1)
                S = s5_t[:, 3072 + 512 * (i % 2):3072 + 512 * (i % 2) + 512]
                out = pm[2 + ct % 2][:, 0:T]
                pe.matmul(out, s5_BC[:, i % 2, 2 * P:3 * P], S[:, 0:T], start=i % 4 == 0, stop=False)
                mm = pe.matmul(out, s5_BC[:, i % 2, 3 * P:4 * P], S[:, T:2 * T], start=False, stop=i % 4 == 3)
                mm.then_inc(sem("s5_tile_read"), 1)
                if i % 4 == 3:
                    pe.wait_ge(sem("s5_tile_read"), i + 1)
                    pe.nop().then_inc(sem("s5_out_sum"), 1)
            pe.wait_ge(sem("s5_gelu"), 1)
            pe.wait_ge(sem("s5_glu_in"), 16)
            for n in range(4):
                if n >= 2:
                    pe.wait_ge(sem("s5_glu"), n - 1)
                for k in range(4):
                    mm = pe.matmul(pm[n % 2][:, 0:T], s5_wglu[:, k, n * P:n * P + P], s5zT[:, k, :],
                                   start=k == 0, stop=k == 3)
                mm.then_inc(sem("s5_glu_sum"), 1)

        SB_HEADS = 8
        sb_in, sb_v, sb_z, sb_e, sb_l, sb_w = carve(2048, 1024, 384, 384, 384, 384)
        sbqk = sb_in.rearrange("p (w b t) -> p w b t", w=2, b=4)
        sbv = sb_v.rearrange("p (n h e) -> p n h e", n=2, h=2)
        HSCALE = 64.0 ** -0.5

        def sb_pool(pool):
            stage_stored(pool, "sv")
            pool.wait_ge(sem("s5_done"), 1)
            for n in range(4):
                pool.dma_start(sb_in[:, 512 * n:512 * n + 512], units[PLAN["sqk"].store + n, :, :]).then_inc(sem("sb_in"), 16)
            for n in range(2):
                pool.dma_start(sb_v[:, 512 * n:512 * n + 512], units[PLAN["sv"].store + n, :, :]).then_inc(sem("sb_in"), 16)

        def sb_pe(pe):
            pe.wait_ge(sem("sb_in"), 96)
            pe.wait_ge(sem("s5_done"), 1)
            for h in range(SB_HEADS):
                r, b = slice(64 * (h % 2), 64 * (h % 2) + 64), h // 2
                q, k = sbqk[r, 0, b, :], sbqk[r, 1, b, :]
                pe.matmul(pm[0][:, 0:256], k[:, 0:P], q, start=True, stop=True)
                pe.matmul(pm[0][:, 256:384], k[:, P:T], q[:, P:T], start=True, stop=True).then_inc(sem("attn_scores"), 1)
                pe.wait_ge(sem("sb_stay"), h + 1)
                pe.matmul(pm[1][:, 0:256], const("later"), sb_l[:, 0:256], start=True, stop=False)
                pe.matmul(pm[1][:, P:256], const("ones"), sb_l[:, 256:384], start=False, stop=True)
                pe.matmul(pm[1][:, 256:384], const("later"), sb_l[:, 256:384], start=True, stop=True)\
                    .then_inc(sem("sb_left"), 1)
                pe.wait_ge(sem("attn_probs"), SB_AT + h + 1)
                v = sbv[:, h // 4, :, 64 * (h % 4):64 * (h % 4) + 64]
                out = pm[2][r, 0:256]
                pe.matmul(out, v[:, 0, :], sb_w[:, 0:256], start=True, stop=False)
                pe.matmul(out[:, P:256], v[:, 1, :], sb_w[:, 256:384], start=False, stop=True).then_inc(sem("attn_out"), 1)
                pe.wait_ge(sem("attn_head_done"), SB_AT + h + 1)

        def sb_act(act):
            for h in range(SB_HEADS):
                r, b = slice(64 * (h % 2), 64 * (h % 2) + 64), h // 2
                act.wait_ge(sem("attn_scores"), SB_AT + h + 1)
                act.activation(sb_e, pm[0][:, 0:384], ACT.Abs, scale=HSCALE)
                act.drain()
                act.activation(sb_e, sb_e, ACT.Exp, scale=-1.0)
                act.drain()
                act.activation(sb_e, sb_e, ACT.Ln, bias=1.0).then_inc(sem("sb_ln"), 1)
                act.wait_ge(sem("sb_expo"), h + 1)
                act.activation(sb_w, sb_z, ACT.Exp).then_inc(sem("sb_exp"), 1)
                act.wait_ge(sem("attn_out"), SB_AT + h + 1)
                act.activation(hT[r, 4 + b, :], pm[2][r, 0:256], ACT.Copy).then_inc(sem("attn_head_done"), 1)

        def sb_dve(dve):
            for h in range(SB_HEADS):
                dve.wait_ge(sem("sb_ln"), h + 1)
                dve.tensor_scalar(sb_z, pm[0][:, 0:384], HSCALE, 0.0, ALU.mult, ALU.max)
                dve.drain()
                dve.tensor_tensor(sb_e, sb_e, sb_z, ALU.add)
                dve.drain()
                dve.scalar_tensor_tensor(sb_l, sb_e, -1.0, const("past_mask"), ALU.mult, ALU.mult)\
                    .then_inc(sem("sb_stay"), 1)
                dve.scalar_tensor_tensor(sb_z, pm[0][:, 0:384], HSCALE, sb_e, ALU.mult, ALU.subtract)
                dve.drain()
                dve.wait_ge(sem("sb_left"), h + 1)
                dve.tensor_tensor(sb_z, sb_z, pm[1][:, 0:384], ALU.add).then_inc(sem("sb_expo"), 1)
                dve.wait_ge(sem("sb_exp"), h + 1)
                dve.tensor_tensor(sb_w, sb_w, const("past_mask"), ALU.mult).then_inc(sem("attn_probs"), 1)

        NH, NG, NCMP = 16, 4, 15
        (n_q, n_kd, n_v, n_kcs, n_bias, n_BC, n_g, n_oc) = carve(2048, 2048, 1024, 2 * 1028, 768, 480, 96, NSA_CONST_W)
        at = 2048 + 2048 + 1024 + 2056 + 768 + 480 + 96 + NSA_CONST_W
        (n_s, n_pt, n_cs, n_ct, n_st, n_H, n_kc, n_vc, n_pos) = carve(768, 768, 32, 256, 32, 120, 64, 256, 2, at=at)
        n_w1 = s5_t[:, 0:4096].rearrange("p (j m n) -> p j m n", j=2, m=16)
        nqT = n_q.rearrange("p (b t) -> p b t", b=8)
        nkd = n_kd.rearrange("p (w g t) -> p w g t", w=2, g=NG)
        nv = n_v.rearrange("p (w h e) -> p w h e", w=2, h=2)
        nkcs = n_kcs.rearrange("p (j g t) -> p j g t", j=2, g=NG)
        nbias = n_bias.rearrange("p (s n) -> p s n", s=2)
        nBC = n_BC.rearrange("p (q h n) -> p q h n", q=2, h=NH)
        ng = n_g.rearrange("p (q h) -> p q h", q=2)

        def nc_(name):
            a, b = NSA_AT[name]
            return n_oc[:, a:b]

        def nsa_pool(pool):
            stage_stored(pool, "ng")
            pool.wait_ge(sem("attn_head_done"), SB_AT + SB_HEADS)
            load = lambda d, s, name="nsa_in": pool.dma_start(d, s).then_inc(sem(name), 16)
            load(n_oc, t_in["nsa_const"])
            load(n_w1, t_in["cmp_w1"])
            for n in range(4):
                load(n_q[:, 512 * n:512 * n + 512], units[PLAN["nq"].store + n, :, :])
            for j in range(2):
                u = units[PLAN["nkc"].store + j, :, :]
                for par in range(2):
                    src = u[64 * par:64 * par + 64, :].rearrange("p (g t) -> p g t", g=2)
                    load(nkcs[0:64, j, par:NG:2, 0:256], src)
                    load(nkcs[64:128, j, par:NG:2, 0:255], src[:, :, 1:256])
                u = units[PLAN["nk"].store + j, :, :]
                for par in range(2):
                    src = u[64 * par:64 * par + 64, :].rearrange("p (g t) -> p g t", g=2)
                    for base in (0, 64):
                        load(nkd[base:base + 64, j, par:NG:2, :], src)
                load(n_v[:, 512 * j:512 * j + 512], units[PLAN["nv"].store + j, :, :])
            load(ng, units[PLAN["ng"].store, :, :].rearrange("p (q n) -> p q n", q=2)[:, :, 0:48])
            pool.wait_ge(sem("bias_rows_ready"), 1)
            pool.dma_start(bias_rows, n_s[0:16, 0:384]).then_inc(sem("bias_rows_stored"), 16)
            pool.wait_ge(sem("bias_rows_stored"), 16)
            for h in range(NH):
                if h >= 2:
                    pool.wait_ge(sem("attn_head_done"), NSA_AT_HEAD + h - 1)
                row = bias_rows[h, :]
                tile_ = bass.AP(row.tensor, row.offset, [[1, P], [1, 256]])
                diag = bass.AP(row.tensor, row.offset + 128, [[1, P], [1, 128]])
                pool.dma_start(nbias[:, h % 2, 0:256], tile_).then_inc(sem(f"nsa_bias{h % 2}"), 16)
                pool.dma_start(nbias[:, h % 2, 256:384], diag).then_inc(sem(f"nsa_bias{h % 2}"), 16)

        N_LOADS = 16 * (2 + 4 + 2 * (4 + 4 + 1) + 1)

        def nsa_pe(pe):
            pe.wait_ge(sem("nsa_in"), N_LOADS)
            tab = nc_("tab")[0:32, :]
            pe.matmul(pm[0][0:16, 0:256], tab, nc_("onehot_rows")[0:32, :], start=True, stop=True)
            oc = nc_("onehot_cmp")
            for qb in range(2):
                for n in range(NCMP):
                    u = qb * NCMP + n
                    pe.matmul(pm[1][:, u * 16:u * 16 + 16], oc[0:32, u * P:u * P + P], tab, start=True, stop=True)
            for j in range(2):
                for m in range(16):
                    pe.matmul(pm[2][:, j:j + 1], n_w1[:, j, m, :], nc_("pos")[:, 16 * j + m:16 * j + m + 1],
                              start=m == 0, stop=m == 15)
                for m in range(16):
                    rhs = nkcs[:, j, :, 2 * m:2 * m + 16 * (NCMP - 1) + 1:16]
                    mm = pe.matmul(pm[3][:, 64 * j:64 * j + 60], n_w1[:, j, m, :], rhs, start=m == 0, stop=m == 15)
            mm.then_inc(sem("nsa_hidden_sum"), 1)
            pe.wait_ge(sem("nsa_hidden"), 1)
            w2k, w2v = nc_("w2")[:, 0:64], nc_("w2")[:, 64:128]
            for half in range(2):
                pe.matmul(pm[2][64 * half:64 * half + 64, 0:60], w2k, n_H[:, 0:60], start=True, stop=True)
            for g in range(NG):
                mm = pe.matmul(pm[3][0:NCMP, 64 * g:64 * g + 64], n_H[:, 60 + 15 * g:75 + 15 * g], w2v, start=True, stop=True)
            mm.then_inc(sem("nsa_kvc_sum"), 1)
            pe.wait_ge(sem("nsa_kvc"), 1)
            pe.wait_ge(sem("bias_rows_ready"), 1)
            for h in range(NH):
                r, b, g = slice(64 * (h % 2), 64 * (h % 2) + 64), h // 2, h // 4
                q = nqT[r, b, :]
                pe.wait_ge(sem(f"nsa_bias{h % 2}"), 32 * (h // 2 + 1))
                for w in range(2):
                    k = nkd[r, w, g, :]
                    pe.matmul(pm[w][:, 0:384], nc_("flip"), nbias[:, h % 2, :], start=True, stop=False)
                    pe.matmul(pm[w][:, 0:256], q[:, P:T], k, start=False, stop=False)
                    pe.matmul(pm[w][:, 256:384], q[:, 0:P], k[:, 0:P], start=False, stop=True)
                for qb in range(2):
                    mm = pe.matmul(pm[0][:, 384 + 16 * qb:384 + 16 * qb + 15], q[:, qb * P:qb * P + P],
                                   n_kc[r, 15 * g:15 * g + 15], start=True, stop=True)
                mm.then_inc(sem("attn_scores"), 1)
                pe.wait_ge(sem("attn_probs"), NSA_AT_HEAD + h + 1)
                for w in range(2):
                    p = n_s[:, 384 * w:384 * w + 384]
                    pe.transpose(pm[2 + w][:, 0:128], p[:, 256:384], const("identity"))
                    pe.transpose(pm[2 + w][:, 128:256], p[:, 0:128], const("identity"))
                    pe.transpose(pm[2 + w][:, 256:384], p[:, 128:256], const("identity"))
                for qb in range(2):
                    mm = pe.transpose(pm[1][0:NCMP, qb * P:qb * P + P], n_cs[:, 16 * qb:16 * qb + 15], const("identity"))
                mm.then_inc(sem("attn_turned"), 1)
                pe.wait_ge(sem("attn_pt"), NSA_SOFT_AT + h + 1)
                out = pm[0][r, 0:256]
                pe.matmul(out, n_vc[0:NCMP, 64 * g:64 * g + 64], n_ct[0:NCMP, :], start=True, stop=False)
                for w in range(2):
                    v = nv[:, w, :, 64 * g:64 * g + 64]
                    pt = n_pt[:, 384 * w:384 * w + 384]
                    pe.matmul(out, v[:, 0, :], pt[:, 0:256], start=False, stop=False)
                    mm = pe.matmul(out[:, P:256], v[:, 1, :], pt[:, 256:384], start=False, stop=w == 1)
                mm.then_inc(sem("attn_out"), 1)
                pe.wait_ge(sem("attn_head_done"), NSA_AT_HEAD + h + 1)

        def nsa_act(act):
            act.wait_ge(sem("nsa_in"), N_LOADS)
            act.wait_ge(sem("nsa_hidden_sum"), 1)
            act.activation(n_pos, pm[2][:, 0:2], ACT.Copy)
            act.drain()
            for j in range(2):
                act.activation(n_H[:, 60 * j:60 * j + 60], pm[3][:, 64 * j:64 * j + 60], ACT.Gelu_apprx_tanh,
                               bias=n_pos[:, j:j + 1])
            act.drain().then_inc(sem("nsa_hidden"), 1)
            act.activation(ng, ng, ACT.Sigmoid).then_inc(sem("nsa_gates"), 1)
            act.wait_ge(sem("nsa_kvc_sum"), 1)
            act.activation(n_kc[:, 0:60], pm[2][:, 0:60], ACT.Copy)
            act.activation(n_vc[0:NCMP, :], pm[3][0:NCMP, 0:256], ACT.Copy)
            act.drain().then_inc(sem("nsa_kvc"), 1)
            for h in range(NH):
                r, b = slice(64 * (h % 2), 64 * (h % 2) + 64), h // 2
                act.wait_ge(sem("attn_max"), NSA_SOFT_AT + h + 1)
                for w in range(2):
                    for qb, (a, z) in enumerate([(256, 384), (0, 256)]):
                        n = 2 * w + qb
                        s = n_s[:, 384 * w + a:384 * w + z]
                        act.activation(s, pm[w][:, a:z], ACT.Exp, scale=HSCALE, bias=n_st[:, 8 + n:9 + n],
                                       accum_out=n_st[:, 16 + n:17 + n])
                for qb in range(2):
                    s = n_cs[:, 16 * qb:16 * qb + 15]
                    act.activation(s, s, ACT.Exp, bias=n_st[:, 12 + qb:13 + qb])
                act.drain().then_inc(sem("attn_exp"), 1)
                act.wait_ge(sem("attn_turned"), NSA_SOFT_AT + h + 1)
                for w in range(2):
                    act.activation(n_pt[:, 384 * w:384 * w + 384], pm[2 + w][:, 0:384], ACT.Copy)
                act.activation(n_ct[0:NCMP, :], pm[1][0:NCMP, 0:256], ACT.Copy)
                act.drain().then_inc(sem("attn_pt"), 1)
                act.wait_ge(sem("attn_out"), NSA_AT_HEAD + h + 1)
                act.activation(hT[r, 8 + b, :], pm[0][r, 0:256], ACT.Copy).then_inc(sem("attn_head_done"), 1)

        def nsa_dve(dve):
            dve.wait_ge(sem("nsa_in"), N_LOADS)
            dve.wait_ge(sem("nsa_hidden_sum"), 1)
            dve.memset(n_s[0:16, 256:384], NEG)
            dve.tensor_copy(n_s[0:16, 0:256], pm[0][0:16, 0:256])
            dve.tensor_copy(nBC, pm[1][:, 0:480].rearrange("p (q n h) -> p q h n", q=2, h=NH))
            dve.drain().then_inc(sem("bias_rows_ready"), 1)
            dve.wait_ge(sem("bias_rows_stored"), 16)
            dve.wait_ge(sem("nsa_gates"), 1)
            cadd = nc_("cmp_add").rearrange("p (q n) -> p q n", q=2)
            cmul = nc_("cmp_mul").rearrange("p (q n) -> p q n", q=2)
            cs = n_cs.rearrange("p (q n) -> p q n", q=2)[:, :, 0:15]
            for h in range(NH):
                dve.wait_ge(sem("attn_scores"), NSA_AT_HEAD + h + 1)
                dve.scalar_tensor_tensor(cs, pm[0][:, 384:416].rearrange("p (q n) -> p q n", q=2)[:, :, 0:15], HSCALE,
                                         nBC[:, :, h, :], ALU.mult, ALU.add)
                dve.drain()
                dve.tensor_tensor(cs, cs, cadd, ALU.add)
                for w in range(2):
                    dve.reduce_max(n_st[:, 2 * w:2 * w + 1], pm[w][:, 256:384], AX.X)
                    dve.reduce_max(n_st[:, 2 * w + 1:2 * w + 2], pm[w][:, 0:256], AX.X)
                dve.drain()
                dve.reduce_max(n_st[:, 4:6], cs, AX.X)
                dve.drain()
                dve.tensor_scalar(n_st[:, 8:12], n_st[:, 0:4], -HSCALE, None, ALU.mult)
                dve.tensor_scalar(n_st[:, 12:14], n_st[:, 4:6], -1.0, None, ALU.mult).then_inc(sem("attn_max"), 1)
                dve.wait_ge(sem("attn_exp"), NSA_SOFT_AT + h + 1)
                dve.tensor_tensor(cs, cs, cmul, ALU.mult)
                dve.drain()
                dve.reduce_sum(n_st[:, 20:22], cs, AX.X)
                dve.drain()
                dve.tensor_scalar(n_st[:, 16:22], n_st[:, 16:22], 1e-30, None, ALU.max)
                dve.drain()
                dve.reciprocal(n_st[:, 16:22], n_st[:, 16:22])
                dve.drain()
                f = n_st[:, 24:30].rearrange("p (w q) -> p q w", w=3)
                s = n_st[:, 16:22].rearrange("p (w q) -> p q w", w=3)
                dve.tensor_tensor(f[:, :, 0:2], s[:, :, 0:2], ng[:, :, 3 * h + 1:3 * h + 3], ALU.mult)
                dve.tensor_tensor(f[:, :, 2:3], s[:, :, 2:3], ng[:, :, 3 * h:3 * h + 1], ALU.mult)
                dve.drain()
                for w in range(2):
                    for qb, (a, z) in enumerate([(256, 384), (0, 256)]):
                        v = n_s[:, 384 * w + a:384 * w + z]
                        dve.tensor_scalar(v, v, n_st[:, 24 + 2 * w + qb:25 + 2 * w + qb], None, ALU.mult)
                for qb in range(2):
                    v = n_cs[:, 16 * qb:16 * qb + 15]
                    last = dve.tensor_scalar(v, v, n_st[:, 28 + qb:29 + qb], None, ALU.mult)
                last.then_inc(sem("attn_probs"), 1)

        XH = 4
        (x_q, x_k, x_v, x_s, x_pt, x_st) = carve(1024, 1024, 1024, 512, 512, 8)
        xoT = arena[:, 5120:5120 + 1024].rearrange("p (b t) -> p b t", b=XH)

        def xa_pool(pool):
            stage_stored(pool, "xq")
            pool.wait_ge(sem("ln_done"), 1)
            for n in range(2):
                for dst, name in ((x_q, "xq"), (x_k, "mem_k"), (x_v, "mem_v")):
                    pool.dma_start(dst[:, 512 * n:512 * n + 512], units[PLAN[name].store + n, :, :]).then_inc(sem("xa_in"), 16)

        def xa_pe(pe):
            pe.wait_ge(sem("xa_in"), 96)
            for h in range(XH):
                q, k = x_q[:, h * T:h * T + T], x_k[:, h * T:h * T + T]
                for qb in range(2):
                    mm = pe.matmul(pm[0][:, qb * T:qb * T + T], q[:, qb * P:qb * P + P], k, start=True, stop=True)
                mm.then_inc(sem("attn_scores"), 1)
                pe.wait_ge(sem("attn_probs"), XA_AT + h + 1)
                for kb in range(2):
                    for qb in range(2):
                        mm = pe.transpose(pm[1][:, kb * T + qb * P:kb * T + qb * P + P],
                                          x_s[:, qb * T + kb * P:qb * T + kb * P + P], const("identity"))
                mm.then_inc(sem("attn_turned"), 1)
                pe.wait_ge(sem("attn_pt"), XA_SOFT_AT + h + 1)
                v = x_v.rearrange("p (n k e) -> p n k e", n=2, k=2)
                for kb in range(2):
                    mm = pe.matmul(pm[2][:, 0:T], v[:, h // 2, kb, (h % 2) * P:(h % 2) * P + P],
                                   x_pt[:, kb * T:kb * T + T], start=kb == 0, stop=kb == 1)
                mm.then_inc(sem("attn_out"), 1)
                pe.wait_ge(sem("attn_head_done"), XA_AT + h + 1)

        def xa_act(act):
            sc = float(P) ** -0.5
            for h in range(XH):
                act.wait_ge(sem("attn_max"), XA_SOFT_AT + h + 1)
                for qb in range(2):
                    act.activation(x_s[:, qb * T:qb * T + T], pm[0][:, qb * T:qb * T + T], ACT.Exp, scale=sc,
                                   bias=x_st[:, 2 + qb:3 + qb], accum_out=x_st[:, 4 + qb:5 + qb])
                act.drain().then_inc(sem("attn_exp"), 1)
                act.wait_ge(sem("attn_turned"), XA_SOFT_AT + h + 1)
                act.activation(x_pt, pm[1][:, :], ACT.Copy).then_inc(sem("attn_pt"), 1)
                act.wait_ge(sem("attn_out"), XA_AT + h + 1)
                act.activation(xoT[:, h, :], pm[2][:, 0:T], ACT.Copy).then_inc(sem("attn_head_done"), 1)

        def xa_dve(dve):
            for h in range(XH):
                dve.wait_ge(sem("attn_scores"), XA_AT + h + 1)
                dve.reduce_max(x_st[:, 0:2], pm[0][:, :].rearrange("p (q k) -> p q k", q=2), AX.X)
                dve.drain()
                dve.tensor_scalar(x_st[:, 2:4], x_st[:, 0:2], -float(P) ** -0.5, None, ALU.mult).then_inc(sem("attn_max"), 1)
                dve.wait_ge(sem("attn_exp"), XA_SOFT_AT + h + 1)
                dve.reciprocal(x_st[:, 4:6], x_st[:, 4:6])
                dve.drain()
                for qb in range(2):
                    v = x_s[:, qb * T:qb * T + T]
                    last = dve.tensor_scalar(v, v, x_st[:, 4 + qb:5 + qb], None, ALU.mult)
                last.then_inc(sem("attn_probs"), 1)

        CV_AT = FB * T
        (cv_p, cv_u, cv_t, cv_g) = carve(352, 4 * 516, 2 * 512, 2 * 256, at=CV_AT)
        cvu = cv_u.rearrange("p (s h t) -> p s h t", s=4, h=2)
        cvt = cv_t.rearrange("p (s h t) -> p s h t", s=2, h=2)
        cvg = cv_g.rearrange("p (s t) -> p s t", s=2)

        def conv_pool(pool):
            pool.wait_ge(sem("ln_done"), 2)
            pool.dma_start(cv_p, t_in["conv"]).then_inc(sem("conv_in"), 16)

        def conv_act(act):
            st = PLAN["up2"]
            act.wait_ge(sem("conv_zero"), 1)

            def unit(i, j):
                u = 4 * i + j
                b = (st.bank + j) % 4
                unit_done(act, st, i, j)
                if not (isinstance(u, int) and u < 4):
                    act.wait_ge(sem("conv_read"), u - 3)
                act.activation(cvu[:, j % 4, :, 2:258], psg[b][:, :].rearrange("p (h t) -> p h t", h=2), ACT.Copy)\
                    .then_inc(bank_free[b], 1)
                act.wait_ge(sem("conv_done"), u + 1)
                act.activation(cvg[:, j % 2, :], cvt[:, j % 2, 1, :], ACT.Gelu_apprx_tanh).then_inc(sem("conv_gelu"), 1)
            for u in range(4):
                unit(0, u)
            with act.Fori(1, st.units // 4) as i:
                for j in range(4):
                    unit(i, j)

        def conv_dve(dve):
            st = PLAN["up2"]
            dve.wait_ge(sem("ln_done"), 2)
            dve.memset(cvu[:, :, :, 0:2], 0.0).then_inc(sem("conv_zero"), 1)
            dve.wait_ge(sem("conv_in"), 16)

            def unit(i, j):
                u = 4 * i + j
                b = (st.bank + j) % 4
                dve.wait_ge(bank_free[b], i + (st.bank + j) // 4 + 1)
                col = lambda h, k: cv_p[:, 8 * u + 4 * h + k:8 * u + 4 * h + k + 1] if isinstance(u, int) else \
                    arena[:, bass.ds(u * 8 + (CV_AT + 4 * h + k), 1)]
                U, V = cvu[:, j % 4, :, :], cvt[:, j % 2, :, :]
                for h in range(2):
                    dve.tensor_scalar(V[:, h, :], U[:, h, 2:258], col(h, 2), col(h, 3), ALU.mult, ALU.add)
                dve.drain()
                for h in range(2):
                    dve.scalar_tensor_tensor(V[:, h, :], U[:, h, 1:257], col(h, 1), V[:, h, :], ALU.mult, ALU.add)
                dve.drain()
                for h in range(2):
                    last = dve.scalar_tensor_tensor(V[:, h, :], U[:, h, 0:256], col(h, 0), V[:, h, :], ALU.mult, ALU.add)
                dve.drain().then_inc(sem("conv_done"), 1)
                dve.nop().then_inc(sem("conv_read"), 1)
                dve.wait_ge(sem("conv_gelu"), u + 1)
                dst = fT[:, u, :] if isinstance(u, int) else arena[:, bass.ds(u * T, T)]
                dve.tensor_tensor(dst, V[:, 0, :], cvg[:, j % 2, :], ALU.mult)
                dve.drain()
            for u in range(4):
                unit(0, u)
            with dve.Fori(1, st.units // 4) as i:
                for j in range(4):
                    unit(i, j)
            dve.drain().then_inc(sem("conv_ready"), 1)

        block = ctx.enter_context(nc.Block())

        def beside_da(n):
            return 1 + (n % 5 in (1, 3, 4))

        def beside_rw2(n):
            return n % 2

        def inverse_steps(n):
            share = lambda m: round((C - 1) * (m / (5 * DA_HEADS)) ** (1 / 3))
            return share(n + 1) - share(n)

        @block.sync
        def _(sp):
            stream_weights(sp)

        @block.gpsimd
        def _(pool):
            load_inputs(pool)
            rw1_pool(pool)
            inv_pool(pool)
            da_pool(pool)
            rw2_pool(pool)
            gates_pool(pool)
            mem_pool(pool)
            s5_pool(pool)
            sb_pool(pool)
            nsa_pool(pool)
            xa_pool(pool)
            conv_pool(pool)
            pool.wait_ge(sem("ln_done"), 3)
            pool.dma_start(t_out, xT[:, :, :]).then_inc(sem("out_written"), 16)
            pool.wait_ge(sem("out_written"), 16)

        @block.tensor
        def _(pe):
            pe.wait_ge(sem("consts_loaded"), 16)
            rms_pe(pe, "mix_pre")
            products(pe, "rkv", hT, ready="mix_in")
            products(pe, "lora", hT)
            weave(chain(quarters(pe, "qk", hT), quarters(pe, "v", hT)), rw1_pe(pe), 2)
            weave(quarters(pe, "gates", hT), da_pe(pe), beside_da)
            weave(quarters(pe, "branch_a", oaT, ready="attn_head_done", count=DA_HEADS), rw2_pe(pe), beside_rw2)
            products(pe, "branch_b", obT, ready="rw2_group_done", count=RW_TILES // GT)
            products(pe, "out", mixT, ready="mix_ready")
            rms_pe(pe, "mix_post")
            rms_pe(pe, "ffn_pre")
            products(pe, "ffn_in", hT, ready="ffn_in")
            products(pe, "ffn_out", fT, ready="ffn_ready")
            rms_pe(pe, "ffn_post")
            products(pe, "u5", xT, ready="block1_done")
            for name in ("sqk", "sv", "nq", "nkc", "nk", "nv", "ng"):
                products(pe, name, xT)
            pe.wait_ge(sem("mem_loaded"), 16)
            products(pe, "mem_k", hT)
            products(pe, "mem_v", hT)
            s5_pe(pe)
            sb_pe(pe)
            nsa_pe(pe)
            products(pe, "out2", hT)
            ln_pe(pe, 1)
            products(pe, "xq", xT, ready="ln_done", count=1)
            xa_pe(pe)
            products(pe, "xo", xoT)
            ln_pe(pe, 2)
            products(pe, "up2", xT, ready="ln_done", count=2)
            products(pe, "down2", fT, ready="conv_ready")
            ln_pe(pe, 3)

        @block.scalar
        def _(act):
            act.wait_ge(sem("small_set"), 1)
            act.wait_ge(sem("x_loaded"), 16)
            rms_act(act, "mix_pre", xT[:, :, :])
            store_units(act, "rkv")
            store_units(act, "lora")
            weave(chain(store_quarters(act, "qk"), store_quarters(act, "v")), rw1_act(act), 2)
            weave(store_quarters(act, "gates"), da_act(act), beside_da)
            inv_act(act)
            weave(branch_a_act(act), rw2_act(act), beside_rw2)
            gates_act(act)
            into_y(act, "out")
            rms_act(act, "mix_post", yT[:, :, :])
            rms_act(act, "ffn_pre", xT[:, :, :], ready="x_mixed")
            ffn_act(act)
            into_y(act, "ffn_out")
            rms_act(act, "ffn_post", yT[:, :, :])
            for name in ("u5", "sqk", "sv", "nq", "nkc", "nk", "nv", "ng", "mem_k", "mem_v"):
                store_units(act, name)
            s5_act(act)
            sb_act(act)
            nsa_act(act)
            into_y(act, "out2")
            ln_act(act, 1)
            store_units(act, "xq")
            xa_act(act)
            into_y(act, "xo")
            ln_act(act, 2)
            conv_act(act)
            into_y(act, "down2")
            ln_act(act, 3)

        @block.vector
        def _(dve):
            dve.wait_ge(sem("params_loaded"), 16)
            rms_dve(dve, "mix_pre", xT[:, :, :], "g_mix_pre", hT[:, :, :], done="mix_in")
            run(rw1_dve(dve))
            weave(inv_dve(dve), da_dve(dve), inverse_steps)
            run(rw2_dve(dve))
            gates_dve(dve)
            rms_dve(dve, "mix_post", yT[:, :, :], "g_mix_post", yT[:, :, :], add_to=xT[:, :, :], done="x_mixed")
            rms_dve(dve, "ffn_pre", xT[:, :, :], "g_ffn_pre", hT[:, :, :], done="ffn_in")
            ffn_dve(dve)
            rms_dve(dve, "ffn_post", yT[:, :, :], "g_ffn_post", yT[:, :, :], add_to=xT[:, :, :], done="block1_done")
            s5_dve(dve)
            sb_dve(dve)
            nsa_dve(dve)
            ln_dve(dve, 1)
            xa_dve(dve)
            ln_dve(dve, 2)
            conv_dve(dve)
            ln_dve(dve, 3)


def slots_of(w, blocks, cols=256):
    rows, n = w.shape
    parts = rows // (P * blocks)
    s = w.reshape(parts, blocks, P, n // cols, cols).transpose(3, 0, 2, 1, 4)
    s = s.reshape(parts * (n // cols), P, blocks * cols)
    if s.shape[2] < SLOT:
        s = np.concatenate([s, np.zeros((s.shape[0], P, SLOT - s.shape[2]), np.float32)], 2)
    return s


def columns(v):
    return v.reshape(-1, P).T


def padded(w, n):
    return np.concatenate([w, np.zeros((w.shape[0], n - w.shape[1]), w.dtype)], 1)


def second_parts(i, interleave):
    w = i["w_in_2"][0]
    cols = {"u5": (0, 512), "sqk": (512, 1536), "sv": (1536, 2048), "nq": (2048, 3072), "nkc": (3072, 3584)}
    parts = {n: slots_of(w[:, a:b], 16) for n, (a, b) in cols.items()}
    ksl, vsl, ksw, vsw = (w[:, 3584 + 256 * n:3840 + 256 * n] for n in range(4))
    parts["nk"] = slots_of(np.concatenate([ksl, ksw], 1), 16)
    parts["nv"] = slots_of(np.concatenate([vsl, vsw], 1), 16)
    parts["ng"] = slots_of(padded(w[:, 4608:4656], 256), 16)
    parts["mem_k"] = slots_of(i["xa_wkv_2"][0][:, :512], 16)
    parts["mem_v"] = slots_of(i["xa_wkv_2"][0][:, 512:], 16)
    parts["out2"] = slots_of(i["w_out_2"][0], 16)
    parts["xq"] = slots_of(i["xa_wq_2"][0], 16)
    parts["xo"] = slots_of(i["xa_wo_2"][0], 4, 1024)
    parts["up2"] = slots_of(interleave(i["ffn_w_up_2"][0]), 16)
    parts["down2"] = slots_of(i["ffn_w_down_2"][0], 11)
    return parts


def second_arrays(i, put, arrays):
    for n in range(3):
        put(f"ln_g{n}", i["ln_g_2"][0, n])
        put(f"ln_b{n}", i["ln_b_2"][0, n])
    put("s5_d", columns(i["s5_d_2"][0]))
    put("s5_b_glu", columns(i["s5_b_glu_2"][0]))
    put("lam_re", columns(i["s5_lambda_re_2"][0].reshape(-1)))
    put("lam_im", columns(i["s5_lambda_im_2"][0].reshape(-1)))
    put("log_dt", columns(np.repeat(i["s5_log_dt_2"][0], 64)))
    bc = np.zeros((16, P, 4 * P), np.float32)
    for g in range(32):
        n, s, ch = g // 2, slice(64 * (g % 2), 64 * (g % 2) + 64), 16 * (g % 8)
        for w, name in enumerate(["s5_b_re_2", "s5_b_im_2"]):
            bc[n, ch:ch + 16, w * P + s.start:w * P + s.stop] = i[name][0, g].T
        for w, name in enumerate(["s5_c_re_2", "s5_c_im_2"]):
            bc[n, s, (2 + w) * P + ch:(2 + w) * P + ch + 16] = i[name][0, g].T
    arrays["s5_bc"] = bc
    arrays["w_glu"] = i["s5_w_glu_2"][0].reshape(4, P, 512).transpose(1, 0, 2)
    arrays["memT"] = i["mem_2"][0].T.reshape(DB, P, T).transpose(1, 0, 2)
    nsa = np.zeros((P, NSA_CONST_W), np.float32)
    nsa_constants(nsa)
    for name, v in [("tab", i["rel_bias_2"]), ("w2", np.concatenate(list(i["nsa_cmp_w2_2"][0]), 1)),
                    ("pos", i["nsa_cmp_pos_2"][0].reshape(32, P).T)]:
        a, b = NSA_AT[name]
        nsa[:v.shape[0], a:b] = v
    arrays["nsa_const"] = nsa
    arrays["cmp_w1"] = i["nsa_cmp_w1_2"][0].reshape(2, 16, P, P).transpose(2, 0, 1, 3)
    conv = np.zeros((P, FB, 2, 4), np.float32)
    conv[:, :, :, 0:3] = i["ffn_conv_w_2"][0].reshape(3, 2, FB, P).transpose(3, 2, 1, 0)
    conv[:, :, :, 3] = i["ffn_conv_b_2"][0].reshape(2, FB, P).transpose(2, 1, 0)
    arrays["conv"] = conv.reshape(P, FB * 8)


def lay_out(i):
    w_in = i["w_in"][0]
    da_q, da_k, da_v, rwkv = w_in[:, 0:2048], w_in[:, 2048:4096], w_in[:, 4096:6144], w_in[:, 6144:12288]
    lora, gate_cols = w_in[:, 12288:12736], w_in[:, 12736:16832]
    lora = np.concatenate([padded(lora[:, 0:96], P), padded(lora[:, 96:192], P), lora[:, 192:448]], 1)
    interleave = lambda w: np.stack([w[:, :D_FF].reshape(D, FB, P), w[:, D_FF:].reshape(D, FB, P)], 2).reshape(D, 2 * D_FF)
    parts = {
        "rkv": slots_of(rwkv, 16), "lora": slots_of(lora, 16),
        "qk": slots_of(np.concatenate([da_q, da_k], 1), 16), "v": slots_of(da_v, 16),
        "gates": slots_of(gate_cols, 16), "branch_a": slots_of(i["w_branch_a"][0], 16),
        "branch_b": slots_of(i["w_branch_b"][0], 16), "out": slots_of(i["w_out"][0], 16),
        "ffn_in": slots_of(interleave(i["w_ffn_in"][0]), 16), "ffn_out": slots_of(i["w_ffn_out"][0], 11),
    }
    parts.update(second_parts(i, interleave) if "mem_k" in PLAN else {})
    weights = np.concatenate([parts[s[0]] for s in STAGES])
    assert weights.shape[0] == N_SLOTS

    mu = i["rw_mu"][0]
    params = np.zeros((P, 16 * len(NORMS) + MISC_W), np.float32)

    def put(name, v):
        if name in NORMS:
            params[:, 16 * NORMS.index(name):16 * NORMS.index(name) + 16] = columns(v)
        else:
            a, b = MISC_AT[name]
            params[:v.shape[0], 16 * len(NORMS) + a:16 * len(NORMS) + b] = v

    for name in ("g_mix_pre", "g_mix_post", "g_ffn_pre", "g_ffn_post"):
        put(name, i[name][0])
    put("ln_w", i["rw_ln_w"][0])
    put("ln_b", i["rw_ln_b"][0])
    put("b_gate_a", i["b_gate"][0, :D])
    put("b_gate_b", i["b_gate"][0, D:])
    put("mu_wl", mu[6144:6240][:, None])
    put("mu_al", mu[6240:6336][:, None])
    put("mu_gl0", mu[6336:6464][:, None])
    put("mu_gl1", mu[6464:6592][:, None])
    put("lam_q", i["da_lambda_q"][0].T)
    put("lam_k", i["da_lambda_k"][0].T)
    put("subln", columns(i["da_subln_g"][0]))

    rw_pack = np.zeros((RW_TILES, P, RW_PW), np.float32)
    tiles = lambda w: w.reshape(w.shape[0], RW_TILES, P).transpose(1, 0, 2)
    rw_pack[:, :LORA, 0:P] = tiles(i["rw_w_up"][0])
    rw_pack[:, :LORA, P:2 * P] = tiles(i["rw_a_up"][0])
    rw_pack[:, :, 2 * P:3 * P] = tiles(i["rw_g_up"][0][:P])
    rw_pack[:, :, 3 * P:4 * P] = tiles(i["rw_g_up"][0][P:])
    cols = {"mu_r": mu[:2048], "mu_k": mu[2048:4096], "mu_v": mu[4096:6144], "w0": i["rw_w0"][0], "a0": i["rw_a0"][0],
            "k_k": i["rw_k_k"][0], "k_a": i["rw_k_a"][0], "r_k": i["rw_r_k"][0].reshape(-1),
            "ln_w": i["rw_ln_w"][0], "ln_b": i["rw_ln_b"][0]}
    for n, name in enumerate(RW_PACK):
        rw_pack[:, :, 4 * P + n] = cols[name].reshape(RW_TILES, P)

    arrays = {"weights": weights, "consts": constants(), "rw_pack": rw_pack,
              "xT": i["x"][0].T.reshape(DB, P, T).transpose(1, 0, 2)}
    if "mem_k" in PLAN:
        second_arrays(i, put, arrays)
    arrays["params"] = params
    return {"in_" + k: np.ascontiguousarray(v, dtype=np.float32) for k, v in arrays.items()}


def program(nc, arrays):
    t_in = {n[3:]: nc.dram_tensor(n, a.shape, F32, kind="ExternalInput").ap() for n, a in arrays.items()}
    t_out = nc.dram_tensor("outT", (P, DB, T), F32, kind="ExternalOutput").ap()
    build(nc, t_in, t_out)


def kernel(**inputs):
    import concourse.bacc as bacc
    from concourse.bass_utils import run_bass_kernel_spmd

    arrays = lay_out({k: np.asarray(v) for k, v in inputs.items()})
    nc = bacc.Bacc("TRN2", target_bir_lowering=False, num_devices=1)
    program(nc, arrays)
    r = run_bass_kernel_spmd(nc, [arrays], core_ids=[0])
    out = r.results[0]["outT"]
    return np.ascontiguousarray(out.transpose(2, 1, 0).reshape(1, T, D))
```

```python
import math
from contextlib import ExitStack

import numpy as np

import concourse.bass as bass
from concourse import mybir

F32 = mybir.dt.float32
ALU = mybir.AluOpType
ACT = mybir.ActivationFunctionType
AX = mybir.AxisListType

P = 128
D = 2048
T = 256
DB = D // P
D_FF = 5632
FB = D_FF // P
DA_HEADS = 8
DA_W = 2048
LORA = 96
GATE_RANK = 256
RW_HEADS = 32
RW_TILES = RW_HEADS // 2
C = 64
NCH = T // C
EPS = 1e-6
DA_EPS = 1e-5
GN_EPS = 1e-5 * 64
LN_EPS = 1e-5
LAMBDA_INIT = 0.8 - 0.6 * math.exp(-0.3 * 0)
ALPHA = 2.0 ** 0.25
NEG = -1e30
ARENA = 19328

RING = 4
SLOT = 16 * 256
STAGES = [
    ("rkv", 24, 1, 16, "T"), ("lora", 2, 1, 16, "T"), ("qk", 16, 1, 16, "T"), ("v", 8, 1, 16, "R"),
    ("gates", 16, 1, 16, "T"),
    ("branch_a", 8, 1, 16, "T"), ("branch_b", 8, 1, 16, "T"), ("out", 8, 1, 16, "T"),
    ("ffn_in", 44, 1, 16, "T"), ("ffn_out", 8, 4, 11, "T"),
    ("mem_k", 2, 1, 16, "T"), ("mem_v", 2, 1, 16, "R"),
    ("u5", 2, 1, 16, "T"), ("sqk", 4, 1, 16, "T"), ("sv", 2, 1, 16, "R"), ("nq", 4, 1, 16, "T"),
    ("nkc", 2, 1, 16, "T"), ("nk", 2, 1, 16, "T"), ("nv", 2, 1, 16, "R"), ("ng", 1, 1, 16, "R"),
    ("out2", 8, 1, 16, "T"), ("xq", 2, 1, 16, "T"), ("xo", 8, 0.25, 4, "T"),
    ("up2", 44, 1, 16, "T"), ("down2", 8, 4, 11, "T"),
]
STORED = ("rkv", "lora", "qk", "v", "gates", "mem_k", "mem_v", "u5", "sqk", "sv", "nq", "nkc", "nk", "nv", "ng", "xq")


class Stage:

    def __init__(self, name, units, slots, blocks, layout, slot, bank, store):
        self.name, self.units, self.slots, self.blocks, self.layout = name, units, slots, blocks, layout
        self.slot, self.bank, self.store = slot, bank, store


def plan():
    slot = bank = store = 0
    out = {}
    for name, units, slots, blocks, layout in STAGES:
        out[name] = Stage(name, units, slots, blocks, layout, slot, bank, store)
        slot += int(units * slots)
        bank += units
        store += units if name in STORED else 0
    return out, slot, store


PLAN, N_SLOTS, N_STORED = plan()


RW_PACK = ["mu_r", "mu_k", "mu_v", "w0", "a0", "k_k", "k_a", "r_k", "ln_w", "ln_b"]
RW_PW = 4 * P + len(RW_PACK)
HALF_AT = {"AR": 0, "rows": 256, "GK": 640, "GBR": 896}
HALF_W = 1024
KEEP_AT = {"bonus": (2 * HALF_W, 2 * HALF_W + T), "g": (2 * HALF_W + T, 2 * HALF_W + 2 * T),
           "PC": (2 * HALF_W + 2 * T, 2 * HALF_W + 2 * T + NCH)}
KEEP_W = KEEP_AT["PC"][1]

CONSTS = [("identity", P), ("ones", P), ("ones_mean", P), ("head_ones", P), ("head_mean", P), ("rotate", P),
          ("cos", T), ("sin", T), ("chunk_keep", T), ("gram_mask", P), ("chunk_mask", 384),
          ("later", P), ("past_mask", 384)]
CONST_AT, _at = {}, 0
for _n, _w in CONSTS:
    CONST_AT[_n] = (_at, _at + _w)
    _at += _w
CONST_W = _at

NORMS = ["g_mix_pre", "g_mix_post", "g_ffn_pre", "g_ffn_post", "ln_w", "ln_b", "b_gate_a", "b_gate_b",
         "ln_g0", "ln_g1", "ln_g2", "ln_b0", "ln_b1", "ln_b2"]
MISC = [("mu_wl", 1), ("mu_al", 1), ("mu_gl0", 1), ("mu_gl1", 1), ("lam_q", 2), ("lam_k", 2), ("subln", 2),
        ("s5_d", 4), ("s5_b_glu", 4), ("lam_re", 16), ("lam_im", 16), ("log_dt", 16)]
MISC_AT, _at = {}, 0
for _n, _w in MISC:
    MISC_AT[_n] = (_at, _at + _w)
    _at += _w
MISC_W = _at


def constants():
    c = np.zeros((P, CONST_W), np.float32)
    i = np.arange(P)

    def put(name, value):
        a, b = CONST_AT[name]
        c[:, a:b] = value

    put("identity", np.eye(P))
    put("ones", 1.0)
    put("ones_mean", 1.0 / D)
    same = (i[:, None] // 64 == i[None, :] // 64).astype(np.float32)
    put("head_ones", same)
    put("head_mean", same / 64)
    rot = np.zeros((P, P), np.float32)
    rot[i[64:], i[:64]] = -1.0
    rot[i[:64], i[64:]] = 1.0
    put("rotate", rot)
    half = 64
    inv = np.float32(10000.0) ** (-np.arange(half, dtype=np.float32) / np.float32(half))
    ang = (np.arange(T, dtype=np.float32)[None, :] * inv[:, None].astype(np.float32)).astype(np.float64)
    put("cos", np.concatenate([np.cos(ang)] * 2))
    put("sin", np.concatenate([np.sin(ang)] * 2))
    put("chunk_keep", (np.arange(T) % C != 0)[None, :].astype(np.float32))
    s, t = (i % 64)[:, None], np.arange(64)[None, :]
    put("gram_mask", np.concatenate([s < t, s <= t], 1))
    q, k = i[:, None], i[None, :]
    diag = np.where(k // 64 <= q // 64, 0.0, NEG)
    put("chunk_mask", np.concatenate([np.zeros((P, P)), diag, diag], 1))
    put("later", i[:, None] > i[None, :])
    kk, qq = i[:, None], np.arange(T)[None, :]
    put("past_mask", np.concatenate([kk < qq, (kk < qq)[:, 0:P]], 1))
    return c


N_BUCKETS, MAX_DIST = 32, 1024
NSA_CONSTS = [("onehot_cmp", 2 * 15 * P), ("onehot_rows", T), ("cmp_add", 30), ("cmp_mul", 30),
              ("tab", 16), ("w2", 128), ("pos", 32), ("flip", P)]
NSA_AT, _at = {}, 0
for _n, _w in NSA_CONSTS:
    NSA_AT[_n] = (_at, _at + _w)
    _at += _w
NSA_CONST_W = _at


def bucket(dist):
    n = np.maximum(dist, 0)
    exact = N_BUCKETS // 2
    nf = np.maximum(n, 1).astype(np.float32)
    large = exact + (np.log(nf / np.float32(exact)) / np.float32(math.log(MAX_DIST / exact))
                     * np.float32(N_BUCKETS - exact)).astype(np.int32)
    return np.where(n < exact, n, np.minimum(large, N_BUCKETS - 1))


def nsa_constants(c):
    def put(name, value):
        a, b = NSA_AT[name]
        c[:value.shape[0], a:b] = value

    q = np.arange(T).reshape(2, 1, P)
    end = 16 * np.arange(15).reshape(1, 15, 1) + 31
    put("onehot_cmp", (bucket(q - end)[None] == np.arange(N_BUCKETS)[:, None, None, None]).reshape(N_BUCKETS, -1))
    put("onehot_rows", bucket(T - 1 - np.arange(T))[None, :] == np.arange(N_BUCKETS)[:, None])
    seen = (q >= end).transpose(2, 0, 1).reshape(P, 30)
    put("cmp_add", np.where(seen, 0.0, NEG))
    put("cmp_mul", seen)
    put("flip", 8.0 * np.eye(P)[::-1])


def build(nc, t_in, t_out):
    ctx = ExitStack()
    with ctx:
        def sb(name, shape):
            return ctx.enter_context(nc.sbuf_tensor(name, shape, F32))

        def scratch(name, shape):
            return nc.dram_tensor(name, shape, F32).ap()

        sems = {}

        def sem(name):
            if name not in sems:
                sems[name] = ctx.enter_context(nc.semaphore(name))
            return sems[name]

        ring = sb("weight_ring", [P, RING, SLOT])
        xT = sb("xT", [P, DB, T])
        hT = sb("hT", [P, DB, T])
        yT = sb("yT", [P, DB, T])
        ostage = sb("out_stage", [P, RING, 512])
        arena = sb("arena", [P, ARENA])
        consts = sb("consts", [P, CONST_W])
        params = sb("params", [P, 16 * len(NORMS) + MISC_W])
        small = sb("small", [P, 64])
        psg = [ctx.enter_context(nc.psum_tensor(f"product_bank{i}", [P, 512], F32)) for i in range(4)]
        pm = [ctx.enter_context(nc.psum_tensor(f"mixer_bank{i}", [P, 512], F32)) for i in range(4)]

        def const(name):
            a, b = CONST_AT[name]
            return consts[:, a:b]

        def norm_param(name):
            n = NORMS.index(name)
            return params[:, 16 * n:16 * n + 16]

        def misc(name):
            a, b = MISC_AT[name]
            return params[:, 16 * len(NORMS) + a:16 * len(NORMS) + b]

        def carve(*widths, at=0):
            out = []
            for w in widths:
                out.append(arena[:, at:at + w])
                at += w
            assert at <= ARENA, at
            return out

        units = scratch("units", [N_STORED, P, 512])
        keep = scratch("rwkv_keep", [RW_TILES, P, KEEP_W])
        l_units = scratch("l_units", [P, C * C])
        m_units = scratch("m_units", [P, C * C])
        bias_rows = scratch("bias_rows", [16, 384])
        kc_dram = scratch("kc_dram", [4, C, 16])

        weights = t_in["weights"]

        w_ready = [sem(f"weight_slot{s}_ready") for s in range(RING)]
        w_used = sem("weight_slots_used")
        bank_free = [sem(f"product_bank{s}_free") for s in range(4)]
        stored = [sem(f"out_stage{s}_stored") for s in range(RING)]

        def stream_weights(sp):
            for s in range(RING):
                sp.dma_start(ring[:, s, :], weights[s, :, :]).then_inc(w_ready[s], 16)
            turns = N_SLOTS // RING
            with sp.Fori(1, turns) as i:
                for s in range(RING):
                    g = sp.snap(i * RING + s)
                    used = sp.snap(i * RING + (s - RING + 1))
                    sp.wait_ge(w_used, used)
                    sp.dma_start(ring[:, s, :], weights[bass.ds(g, 1), :, :].rearrange("o p n -> p (o n)"))\
                        .then_inc(w_ready[s], 16)
            for g in range(turns * RING, N_SLOTS):
                sp.wait_ge(w_used, g - RING + 1)
                sp.dma_start(ring[:, g % RING, :], weights[g, :, :]).then_inc(w_ready[g % RING], 16)

        def run(steps):
            for _ in steps:
                pass

        def weave(products_, mixer, every):
            for n, _ in enumerate(mixer):
                for _ in range(every(n) if callable(every) else every):
                    next(products_, None)
            run(products_)

        def chain(*parts):
            for part in parts:
                yield from part

        def groups(eng, st, peel=False):
            def over(body):
                first = 1 if (st.bank < 4 or st.slot < RING or peel) else 0
                if st.units % 4 or st.units // 4 - first < 2 or st.slots < 1:
                    for u in range(st.units):
                        body(0, u)
                    return
                for u in range(4 * first):
                    body(0, u)
                with eng.Fori(first, st.units // 4) as i:
                    for j in range(4):
                        body(i, j)
            return over

        def wait(eng, s, value):
            if not isinstance(value, int) or value > 0:
                eng.wait_ge(s, value)

        def products(pe, name, src, ready=None, count=1, chunks=1, after=None):
            st = PLAN[name]
            if ready and chunks == 1:
                pe.wait_ge(sem(ready), count)
            per_slot = max(1, int(1 / st.slots))
            slots = int(max(1, st.slots))

            def unit(i, j):
                b = (st.bank + j) % 4
                bank = psg[b]
                wait(pe, bank_free[b], i + (st.bank + j) // 4)
                for n in range(slots):
                    q = st.slot + (j // per_slot) * slots + n
                    s = q % RING
                    if j % per_slot == 0:
                        pe.wait_ge(w_ready[s], 16 * slots * i + 16 * (q // RING + 1))
                    cols = 256 * per_slot
                    w = ring[:, s, 0:st.blocks * cols].rearrange("p (k n) -> p k n", n=cols)
                    w = w[:, :, (j % per_slot) * 256:(j % per_slot) * 256 + 256]
                    for half in range(2):
                        for k in range(st.blocks):
                            kk = n * st.blocks + k
                            if chunks > 1 and isinstance(i, int) and i == j == half == 0 and k % (DB // chunks) == 0:
                                pe.wait_ge(sem(ready), count - chunks + 1 + k // (DB // chunks))
                            if st.layout == "T":
                                lhs, rhs = w[:, k, half * P:half * P + P], src[:, kk, :]
                            else:
                                lhs, rhs = src[:, kk, half * P:half * P + P], w[:, k, :]
                            out = bank[:, half * T:half * T + T]
                            first = kk == 0 and (slots == 1 or half == 0)
                            mm = pe.matmul(out, lhs, rhs, start=first, stop=kk == slots * st.blocks - 1,
                                           skip_group_check=slots > 1)
                    if j % per_slot == per_slot - 1:
                        mm.then_inc(w_used, 1)
                if after:
                    after(j)
            groups(pe, st, peel=chunks > 1 or after is not None)(unit)

        def quarters(pe, name, src, ready=None, count=1):
            st = PLAN[name]
            if ready:
                pe.wait_ge(sem(ready), count)
            for u in range(st.units):
                b, s = (st.bank + u) % 4, (st.slot + u) % RING
                wait(pe, bank_free[b], (st.bank + u) // 4)
                pe.wait_ge(w_ready[s], 16 * ((st.slot + u) // RING + 1))
                w = ring[:, s, :].rearrange("p (k n) -> p k n", n=256)
                for half in range(2):
                    for k in range(16):
                        if st.layout == "T":
                            lhs, rhs = w[:, k, half * P:half * P + P], src[:, k, :]
                        else:
                            lhs, rhs = src[:, k, half * P:half * P + P], w[:, k, :]
                        mm = pe.matmul(psg[b][:, half * T:half * T + T], lhs, rhs, start=k == 0, stop=k == 15)
                        if k == 7 or (k == 15 and half == 0):
                            yield
                mm.then_inc(w_used, 1)
                yield

        def unit_done(eng, st, i, j):
            slots, per_slot = int(max(1, st.slots)), max(1, int(1 / st.slots))
            eng.wait_ge(w_used, i * 4 * slots + st.slot + (j // per_slot + 1) * slots)

        def store_units(act, name):
            st = PLAN[name]

            def unit(i, j):
                b, o = (st.bank + j) % 4, (st.store + j) % RING
                unit_done(act, st, i, j)
                wait(act, stored[o], 16 * i + 16 * ((st.store + j) // RING))
                act.activation(ostage[:, o, :], psg[b][:, :], ACT.Copy).then_inc(bank_free[b], 1)
                act.wait_ge(bank_free[b], i + (st.bank + j) // 4 + 1)
                row = i * 4 + (st.store + j)
                act.dma_start(units[bass.ds(row, 1), :, :].rearrange("o p n -> p (o n)") if not isinstance(row, int)
                              else units[row, :, :], ostage[:, o, :]).then_inc(stored[o], 16)
            groups(act, st)(unit)

        def store_quarters(act, name):
            st = PLAN[name]
            for u in range(st.units):
                yield
                yield
                yield
                b, o = (st.bank + u) % 4, (st.store + u) % RING
                unit_done(act, st, 0, u)
                wait(act, stored[o], 16 * ((st.store + u) // RING))
                act.activation(ostage[:, o, :], psg[b][:, :], ACT.Copy).then_inc(bank_free[b], 1)
                act.wait_ge(bank_free[b], (st.bank + u) // 4 + 1)
                act.dma_start(units[st.store + u, :, :], ostage[:, o, :]).then_inc(stored[o], 16)
                yield

        def stage_stored(eng, name):
            st = PLAN[name]
            end = st.store + st.units
            for o in range(RING):
                wait(eng, stored[o], 16 * ((end - o + RING - 1) // RING))

        def load_inputs(pool):
            pool.dma_start(xT[:, :, :], t_in["xT"]).then_inc(sem("x_loaded"), 16)
            pool.dma_start(consts[:, :], t_in["consts"]).then_inc(sem("consts_loaded"), 16)
            pool.dma_start(params[:, :], t_in["params"]).then_inc(sem("params_loaded"), 16)
            pool.memset(small[:, 0:1], EPS)
            pool.memset(small[:, 1:2], DA_EPS)
            pool.memset(small[:, 2:3], GN_EPS)
            pool.memset(small[:, 3:4], LN_EPS)
            pool.memset(small[:, 4:5], math.pi / 2).then_inc(sem("small_set"), 1)

        NCK = 4
        NB = DB // NCK
        chunks_of = [slice(NB * c, NB * c + NB) for c in range(NCK)]

        def norm_space():
            sq, r = carve(DB * T, T, at=11264)
            return sq.rearrange("p (b t) -> p b t", b=DB), r

        def bc_b(v, n=NB):
            return v.unsqueeze(1).to_broadcast([P, n, T])

        TURN = {n: k + 1 for k, n in enumerate(["mix_pre", "mix_post", "ffn_pre", "ffn_post", "ln1", "ln2", "ln3"])}
        SQUARES_AT = {n: NCK * k for k, n in enumerate(["mix_pre", "ffn_pre", "ln1", "ln2", "ln3"])}

        def squares_act(act, tag, src, ready, count):
            sq, r = norm_space()
            for c, ck in enumerate(chunks_of):
                act.wait_ge(sem(ready), count - NCK + 1 + c if ready != "x_loaded" else 16)
                act.activation(sq[:, ck, :], src[:, ck, :], ACT.Square).then_inc(sem("norm_squares"), 1)

        def root_act(act, tag, bank, eps_col):
            sq, r = norm_space()
            act.wait_ge(sem("norm_sum"), TURN[tag])
            act.activation(r, bank[:, 0:T], ACT.Sqrt, bias=small[:, eps_col:eps_col + 1]).then_inc(sem("norm_root"), 1)

        def squares_pe(pe, tag, bank):
            sq, r = norm_space()
            for b in range(DB):
                if b % NB == 0:
                    pe.wait_ge(sem("norm_squares"), SQUARES_AT[tag] + b // NB + 1)
                mm = pe.matmul(bank[:, 0:T], const("ones_mean"), sq[:, b, :], start=b == 0, stop=b == DB - 1)
            mm.then_inc(sem("norm_sum"), 1)

        def unit_sums(pe, name, src, done):
            st = PLAN[name]
            per_slot = max(1, int(1 / st.slots))

            def add(u):
                b = (st.bank + u) % 4
                pe.wait_ge(bank_free[b], (st.bank + u) // 4 + 1)
                for n in (2 * u, 2 * u + 1):
                    mm = pe.matmul(pm[0][:, 0:T], const("ones_mean"), src[:, n, :], start=n == 0, stop=n == DB - 1)
                return mm

            def after(u):
                released = u // per_slot * per_slot
                for v in range(max(0, released - per_slot), released) if u % per_slot == 0 else ():
                    add(v)
                if u == st.units - 1:
                    for v in range(released, st.units):
                        last = add(v)
                    last.then_inc(sem(done), 1)
            return after

        def post_norm_pe(pe, name, src, ready):
            sq, r = norm_space()
            products(pe, name, src, ready=ready, after=unit_sums(pe, name, sq, "norm_sum"))

        def scaled_into_y(act, name, gain):
            st = PLAN[name]
            sq, r = norm_space()
            for u in range(st.units):
                b = (st.bank + u) % 4
                unit_done(act, st, 0, u)
                for h in range(2):
                    n = 2 * u + h
                    act.activation(yT[:, n, :], psg[b][:, h * T:h * T + T], ACT.Identity,
                                   scale=norm_param(gain)[:, n:n + 1])
                act.activation(sq[:, 2 * u:2 * u + 2, :], psg[b][:, :].rearrange("p (h t) -> p h t", h=2),
                               ACT.Square).then_inc(bank_free[b], 1)

        def reciprocal_dve(dve, tag):
            sq, r = norm_space()
            dve.wait_ge(sem("norm_root"), TURN[tag])
            dve.reciprocal(r, r)
            dve.drain()
            return r

        def pre_norm_dve(dve, tag, gain, done):
            r = reciprocal_dve(dve, tag)
            for ck in chunks_of:
                for b in range(ck.start, ck.stop):
                    last = dve.scalar_tensor_tensor(hT[:, b, :], xT[:, b, :], norm_param(gain)[:, b:b + 1], r,
                                                    ALU.mult, ALU.mult)
                last.then_inc(sem(done), 1)

        def post_norm_dve(dve, tag, done):
            r = reciprocal_dve(dve, tag)
            dve.tensor_tensor(yT[:, chunks_of[0], :], yT[:, chunks_of[0], :], bc_b(r), ALU.mult)
            for c, ck in enumerate(chunks_of):
                if c + 1 < NCK:
                    nx = chunks_of[c + 1]
                    dve.tensor_tensor(yT[:, nx, :], yT[:, nx, :], bc_b(r), ALU.mult)
                dve.drain()
                dve.tensor_tensor(xT[:, ck, :], xT[:, ck, :], yT[:, ck, :], ALU.add).then_inc(sem(done), 1)

        def ln_product_pe(pe, name, src, n, **kw):
            products(pe, name, src, after=unit_sums(pe, name, yT, "ln_mean"), **kw)
            squares_pe(pe, f"ln{n}", pm[1])

        def ln_act(act, n):
            squares_act(act, f"ln{n}", yT, "ln_centred", NCK * n)
            root_act(act, f"ln{n}", pm[1], 3)
            for c, ck in enumerate(chunks_of):
                act.wait_ge(sem("ln_scaled"), NCK * (n - 1) + c + 1)
                for b in range(ck.start, ck.stop):
                    last = act.activation(xT[:, b, :], yT[:, b, :], ACT.Identity, bias=norm_param(f"ln_b{n - 1}")[:, b:b + 1],
                                          scale=norm_param(f"ln_g{n - 1}")[:, b:b + 1])
                last.then_inc(sem("ln_done"), 1)

        def ln_dve(dve, n, name):
            st = PLAN[name]
            sq, r = norm_space()
            for u in range(st.units):
                b = (st.bank + u) % 4
                two = slice(2 * u, 2 * u + 2)
                unit_done(dve, st, 0, u)
                dve.scalar_tensor_tensor(yT[:, two, :], xT[:, two, :], ALPHA,
                                         psg[b][:, :].rearrange("p (h t) -> p h t", h=2), ALU.mult, ALU.add)\
                    .then_inc(bank_free[b], 1)
            dve.wait_ge(sem("ln_mean"), n)
            dve.tensor_copy(r, pm[0][:, 0:T])
            dve.drain()
            for ck in chunks_of:
                dve.tensor_tensor(yT[:, ck, :], yT[:, ck, :], bc_b(r), ALU.subtract).then_inc(sem("ln_centred"), 1)
            reciprocal_dve(dve, f"ln{n}")
            for ck in chunks_of:
                dve.tensor_tensor(yT[:, ck, :], yT[:, ck, :], bc_b(r), ALU.mult).then_inc(sem("ln_scaled"), 1)

        rw = {}
        (rw["wl"], rw["al"], rw["gl"], rw["pack"], rw["p"], rw["x"], rw["sg"], rw["a"], rw["kk"],
         rw["sq"], rw["nrm"], rw["cum"], rw["cumex"], rw["Pex"], rw["Pin"], rw["Pinv"], rw["kka"], rw["Bt"],
         rw["kp"], rw["Kt"], rw["rk"], rw["d"], rw["keep1"], rw["L1"]) = carve(
            256, 256, 512, 2 * RW_PW, 2 * 3 * 257, 768, 256, 256, 256,
            256, 256, 256, 256, 256, 256, 256, 256, 256,
            256, 256, 256, 256, KEEP_W, 256, at=4096)
        rw["keep0"], rw["L0"], rw["x1"] = carve(KEEP_W, 256, 768)
        rw_keep = [rw["keep0"], rw["keep1"]]
        rw_L = [rw["L0"], rw["L1"]]
        rw_halves = [k[:, 0:2 * HALF_W].rearrange("p (h n) -> p h n", h=2) for k in rw_keep]
        rwp = rw["pack"].rearrange("p (s n) -> p s n", s=2)
        rwx = rw["p"].rearrange("p (s c n) -> p s c n", s=2, c=3)
        KEPT = 16 * 3

        def all_kept(eng):
            for s in range(2):
                eng.wait_ge(sem(f"rw1_keeps{s}"), KEPT * RW_TILES // 2)

        def rwkv_unit(u):
            st = PLAN["rkv"]
            return units[st.store + u, :, :]

        def rw1_pool(pool):
            pool.memset(rwx[:, :, :, 0:1], 0.0).then_inc(sem("rw_prev_zero"), 1)
            stage_stored(pool, "lora")
            lo = PLAN["lora"].store
            pool.dma_start(arena[:, 4096:4096 + 512], units[lo, :, :]).then_inc(sem("lora_loaded"), 16)
            pool.dma_start(rw["gl"], units[lo + 1, :, :]).then_inc(sem("lora_loaded"), 16)
            for b in range(RW_TILES):
                s = b % 2
                if b >= 2:
                    pool.wait_ge(sem("rw1_tile_done"), b - 1)
                got = sem(f"rw1_in{s}")
                pool.dma_start(rwp[:, s, :], t_in["rw_pack"][b, :, :]).then_inc(got, 16)
                for c in range(3):
                    j = 16 * c + b
                    pool.dma_start(rwx[:, s, c, 1:257], rwkv_unit(j // 2)[:, (j % 2) * T:(j % 2) * T + T])\
                        .then_inc(got, 16)

        def pcol(s, name):
            c = 4 * P + RW_PACK.index(name)
            return rwp[:, s, c:c + 1]

        rw_x = [[x[:, 256 * c:256 * c + 256] for c in range(3)] for x in (rw["x"], rw["x1"])]

        def rw1_dve(dve):
            dve.wait_ge(sem("lora_loaded"), 32)
            dve.wait_ge(sem("consts_loaded"), 16)
            dve.wait_ge(sem("params_loaded"), 16)
            for n, (buf, mu) in enumerate([(rw["wl"], "mu_wl"), (rw["al"], "mu_al"),
                                           (rw["gl"][:, 0:256], "mu_gl0"), (rw["gl"][:, 256:512], "mu_gl1")]):
                if n:
                    dve.drain()
                dve.tensor_tensor(rw["d"][:, 1:256], buf[:, 0:255], buf[:, 1:256], ALU.subtract)
                dve.tensor_scalar(rw["d"][:, 0:1], buf[:, 0:1], -1.0, None, ALU.mult)
                dve.drain()
                last = dve.scalar_tensor_tensor(buf, rw["d"], misc(mu), buf, ALU.mult, ALU.add)
            last.then_inc(sem("lora_mixed"), 1)
            dve.wait_ge(sem("rw_prev_zero"), 1)
            dve.wait_ge(sem("lora_ready"), 1)

            def shift(b):
                s = b % 2
                dve.wait_ge(sem(f"rw1_in{s}"), 64 * (b // 2) + 64)
                steps = list(zip(rw_x[s], ["mu_r", "mu_k", "mu_v"], [rw["d"], rw["kka"], rw["kp"]]))
                for c, (x, mu, t) in enumerate(steps):
                    dve.tensor_tensor(t, rwx[:, s, c, 0:256], rwx[:, s, c, 1:257], ALU.subtract)
                dve.drain()
                for c, (x, mu, t) in enumerate(steps):
                    dve.scalar_tensor_tensor(x, t, pcol(s, mu), rwx[:, s, c, 1:257], ALU.mult, ALU.add)
                dve.drain()
                dve.tensor_scalar(rw["kk"], rw_x[s][1], pcol(s, "k_k"), None, ALU.mult).then_inc(sem("rw1_kk_raw"), 1)

            def tile(b, s):
                b1 = b + 1
                xr, xk, xv = rw_x[s]
                if b >= 2:
                    dve.wait_ge(sem(f"rw1_keeps{s}"), KEPT * (b // 2))
                yield
                dve.wait_ge(sem("rw1_sigmoids"), b1)
                dve.tensor_scalar(rw["sg"], rw["sg"], -math.exp(-0.5), None, ALU.mult)
                dve.tensor_scalar(rw["kp"], rw["a"], -1.0, pcol(s, "k_a"), ALU.add, ALU.mult)
                dve.drain()
                dve.tensor_tensor_scan(rw["cum"], const("chunk_keep"), rw["sg"], 0.0, ALU.mult, ALU.add)
                dve.scalar_tensor_tensor(rw["kp"], rw["kp"], 1.0, xk, ALU.add, ALU.mult)
                dve.drain()
                dve.tensor_tensor(rw["cumex"], rw["cum"], rw["sg"], ALU.subtract)
                dve.scalar_tensor_tensor(rw["rk"], xr, pcol(s, "r_k"), rw["kp"], ALU.mult, ALU.mult)\
                    .then_inc(sem("rw1_cum"), 1)
                dve.wait_ge(sem("rw1_norm"), b1)
                dve.tensor_scalar(rw["nrm"], rw["nrm"], 1e-12, None, ALU.max)
                dve.drain()
                dve.reciprocal(rw["nrm"], rw["nrm"])
                dve.drain()
                dve.tensor_tensor(rw["kk"], rw["kk"], rw["nrm"], ALU.mult)
                dve.drain()
                dve.tensor_tensor(rw["kka"], rw["kk"], rw["a"], ALU.mult)
                dve.wait_ge(sem("rw1_powers"), b1)
                dve.drain()
                halves = rw_halves[s]
                for half in range(2):
                    ar = halves[:, half, 0:256].rearrange("p (c w t) -> p c w t", c=2, w=2)
                    of_half = lambda v: v[:, half * P:half * P + P].rearrange("p (c t) -> p c t", c=2)
                    dve.scalar_tensor_tensor(ar[:, :, 0, :], of_half(rw["kk"]), -1.0, of_half(rw["Pex"]),
                                             ALU.mult, ALU.mult)
                    dve.tensor_tensor(ar[:, :, 1, :], of_half(xr), of_half(rw["Pin"]), ALU.mult)
                dve.tensor_tensor(rw["Bt"], rw["kka"], rw["Pinv"], ALU.mult)
                dve.tensor_tensor(rw["Kt"], rw["kp"], rw["Pinv"], ALU.mult)
                a, z = KEEP_AT["PC"]
                dve.tensor_copy(rw_keep[s][:, a:z], rw["Pin"][:, C - 1:T:C])
                dve.drain().then_inc(sem("rw1_operands"), 1)
                yield
                if b + 1 < RW_TILES:
                    shift(b + 1)
                dve.wait_ge(sem("rw1_bonus_sum"), b1)
                a, z = KEEP_AT["bonus"]
                dve.tensor_tensor(rw_keep[s][:, a:z], pm[0][:, 256:512], xv, ALU.mult).then_inc(sem("rw1_bonus"), 1)
                dve.wait_ge(sem("rw1_grams"), b1)
                m = const("gram_mask").unsqueeze(1).to_broadcast([P, 2, 128])
                L = rw_L[s].rearrange("p (head h t) -> p head h t", head=2, h=2)
                for head in range(2):
                    gb, gk = (pm[1 + head][:, 256 * kind:256 * kind + 256].rearrange("p (h n) -> p h n", h=2)
                              for kind in range(2))
                    at_k, at_b = HALF_AT["GK"] + 128 * head, HALF_AT["GBR"] + 64 * head
                    dve.tensor_tensor(L[:, head, :, :], gb[:, :, 0:C], m[:, :, 0:C], ALU.mult)
                    dve.tensor_tensor(halves[:, :, at_b:at_b + C], gb[:, :, C:2 * C], m[:, :, C:2 * C], ALU.mult)
                    dve.tensor_tensor(halves[:, :, at_k:at_k + 128], gk, m, ALU.mult)
                dve.drain().then_inc(sem("rw1_tile_done"), 1)
                yield

            shift(0)
            for b in range(RW_TILES):
                yield from tile(b, b % 2)

        def rw1_act(act):
            act.wait_ge(sem("lora_mixed"), 1)
            act.activation(rw["wl"], rw["wl"], ACT.Tanh)
            act.activation(rw["gl"], rw["gl"], ACT.Sigmoid).then_inc(sem("lora_ready"), 1)

            def keep_tile(i, s):
                b1 = 2 * i + s + 1
                act.wait_ge(sem("rw1_tile_done"), b1)
                act.wait_ge(sem("rw1_rows"), b1)
                row = 2 * i + s
                stored_ = sem(f"rw1_keeps{s}")
                act.dma_start(keep[row, :, :], rw_keep[s]).then_inc(stored_, 16)
                lu = l_units.rearrange("(b u par) (s t) -> b par s u t", u=4, par=2, s=C)
                for par in range(2):
                    src = rw_L[s][64 * par:64 * par + 64, :].rearrange("p (u t) -> p u t", u=4)
                    act.dma_start(lu[row, par, :, :, :], src).then_inc(stored_, 16)

            def tile(i, s):
                b1 = 2 * i + s + 1
                if i:
                    act.wait_ge(sem(f"rw1_keeps{s}"), KEPT * i)
                act.wait_ge(sem("rw1_lora_w"), b1)
                act.activation(rw["sg"], pm[3][:, 0:256], ACT.Sigmoid, bias=pcol(s, "w0"))
                act.activation(rw["a"], pm[3][:, 256:512], ACT.Sigmoid, bias=pcol(s, "a0"))
                act.wait_ge(sem("rw1_lora_g"), b1)
                a, z = KEEP_AT["g"]
                act.activation(rw_keep[s][:, a:z], pm[1][:, 0:256], ACT.Copy).then_inc(sem("rw1_sigmoids"), 1)
                act.wait_ge(sem("rw1_kk_raw"), b1)
                act.activation(rw["sq"], rw["kk"], ACT.Square).then_inc(sem("rw1_kk_sq"), 1)
                yield
                act.wait_ge(sem("rw1_kk_sum"), b1)
                act.activation(rw["nrm"], pm[0][:, 0:256], ACT.Sqrt).then_inc(sem("rw1_norm"), 1)
                act.wait_ge(sem("rw1_cum"), b1)
                act.activation(rw["Pex"], rw["cumex"], ACT.Exp)
                act.activation(rw["Pin"], rw["cum"], ACT.Exp)
                act.activation(rw["Pinv"], rw["cum"], ACT.Exp, scale=-1.0).then_inc(sem("rw1_powers"), 1)
                yield
                act.wait_ge(sem("rw1_turned"), b1)
                at = HALF_AT["rows"]
                r = rw_halves[s][:, :, at:at + 3 * P].rearrange("p h (q n) -> p q h n", q=3)
                for q in range(2):
                    act.activation(r[:, q, :, :], pm[3][:, 256 * q:256 * q + 256].rearrange("p (h n) -> p h n", h=2), ACT.Copy)
                act.activation(r[:, 2, :, :], pm[0][:, 0:256].rearrange("p (h n) -> p h n", h=2), ACT.Copy)
                act.drain().then_inc(sem("rw1_rows"), 1)
                keep_tile(i, s)
                yield

            for b in range(RW_TILES):
                yield from tile(b // 2, b % 2)

        def rw1_pe(pe):
            pe.wait_ge(sem("lora_ready"), 1)

            def tile(i, s):
                b1 = 2 * i + s + 1
                pe.wait_ge(sem(f"rw1_in{s}"), 64 * i + 64)
                if not (isinstance(i, int) and i == 0 and s == 0):
                    pe.wait_ge(sem("rw1_rows"), b1 - 1)
                    pe.wait_ge(sem("rw1_tile_done"), b1 - 1)
                    pe.wait_ge(sem("rw1_bonus"), b1 - 1)
                pe.matmul(pm[3][:, 0:256], rwp[0:LORA, s, 0:P], rw["wl"][0:LORA, :], start=True, stop=True)
                pe.matmul(pm[3][:, 256:512], rwp[0:LORA, s, P:2 * P], rw["al"][0:LORA, :], start=True, stop=True)\
                    .then_inc(sem("rw1_lora_w"), 1)
                pe.matmul(pm[1][:, 0:256], rwp[:, s, 2 * P:3 * P], rw["gl"][:, 0:256], start=True, stop=False)
                pe.matmul(pm[1][:, 0:256], rwp[:, s, 3 * P:4 * P], rw["gl"][:, 256:512], start=False, stop=True)\
                    .then_inc(sem("rw1_lora_g"), 1)
                yield
                pe.wait_ge(sem("rw1_kk_sq"), b1)
                pe.matmul(pm[0][:, 0:256], const("head_ones"), rw["sq"], start=True, stop=True)\
                    .then_inc(sem("rw1_kk_sum"), 1)
                pe.wait_ge(sem("rw1_norm"), b1)
                pe.wait_ge(sem("rw1_cum"), b1)
                pe.matmul(pm[0][:, 256:512], const("head_ones"), rw["rk"], start=True, stop=True)\
                    .then_inc(sem("rw1_bonus_sum"), 1)
                yield
                pe.wait_ge(sem("rw1_operands"), b1)
                for q, src in enumerate([rw["Bt"], rw["Kt"], rw_x[s][2]]):
                    for half in range(2):
                        n = 2 * q + half
                        if n == 4:
                            pe.wait_ge(sem("rw1_bonus"), b1)
                        out = pm[3][:, n * P:n * P + P] if n < 4 else pm[0][:, (n - 4) * P:(n - 4) * P + P]
                        mm = pe.transpose(out, src[:, half * P:half * P + P], const("identity"))
                mm.then_inc(sem("rw1_turned"), 1)
                for kind, src in enumerate([rw["Bt"], rw["Kt"]]):
                    for c in range(NCH):
                        for head in range(2):
                            j = slice(64 * head, 64 * head + 64)
                            u = 2 * kind + c // 2
                            mm = pe.matmul(pm[1 + head][64 * (c % 2):64 * (c % 2) + 64, u * 128:u * 128 + 128],
                                           src[j, c * C:c * C + C],
                                           rw_halves[s][j, c // 2, c % 2 * 128:c % 2 * 128 + 128],
                                           start=True, stop=True)
                mm.then_inc(sem("rw1_grams"), 1)
                yield

            for b in range(RW_TILES):
                yield from tile(b // 2, b % 2)

        inv_L, inv_M = carve(C * C, C * C, at=4096)
        inv_tmp = yT[:, :, :].rearrange("p b t -> p (b t)")

        def inv_pool(pool):
            all_kept(pool)
            pool.dma_start(inv_L, l_units).then_inc(sem("inv_in"), 16)

        def inv_dve(dve):
            all_kept(dve)
            L = inv_L.rearrange("p (s t) -> p s t", s=C)
            M = inv_M.rearrange("p (c t) -> p c t", c=C)
            dve.memset(inv_M, 0.0)
            dve.drain()
            dve.memset(inv_M[:, 0:C * C:C + 1], 1.0)
            dve.wait_ge(sem("inv_in"), 16)
            dve.drain()
            for t in range(1, C):
                tmp = inv_tmp[:, 0:t * t].rearrange("p (c s) -> p c s", c=t)
                dve.tensor_tensor(tmp, M[:, 0:t, 0:t],
                                  L[:, 0:t, t:t + 1].rearrange("p s o -> p o s").to_broadcast([P, t, t]), ALU.mult)
                dve.drain()
                last = dve.reduce_sum(M[:, 0:t, t:t + 1], tmp, AX.X)
                dve.drain()
                yield
            dve.nop().then_inc(sem("inv_done"), 1)

        GT = 4
        r2_keep, r2_M, r2_X, r2_U, r2_S, r2_Y, r2_d, r2_sq = carve(
            GT * KEEP_W, GT * 256, 512, 512, 256, GT * 256, 512, 512, at=4096)
        r2k = r2_keep.rearrange("p (g n) -> p g n", g=GT)
        r2m = r2_M.rearrange("p (g u t) -> p g u t", g=GT, u=4)
        obT = yT

        r2_halves = r2k[:, :, 0:2 * HALF_W].rearrange("p g (h n) -> p g h n", h=2)
        r2_PC = small[:, 24:24 + 2 * GT * NCH].rearrange("p (s g c) -> p s g c", s=2, g=GT)

        def kept(name, g, c, at, width):
            a = HALF_AT[name] + at
            return r2_halves[:, g, c // 2, a:a + width]

        def kept_all(name, g):
            a, z = KEEP_AT[name]
            return r2k[:, g, a:z]

        def rw2_pool(pool):
            pool.wait_ge(sem("inv_done"), 1)
            pool.dma_start(m_units, inv_M).then_inc(sem("inv_stored"), 16)
            pool.wait_ge(sem("inv_stored"), 16)
            pool.wait_ge(sem("attn_head_done"), DA_HEADS)
            mu = m_units.rearrange("(b h u par) (s t) -> b par u s h t", u=2, par=2, h=2, s=C)
            for n in range(RW_TILES // GT):
                tiles = keep[GT * n:GT * n + GT, :, :].rearrange("g p n -> p g n")
                for half in range(2):
                    if n:
                        pool.wait_ge(sem("rw2_Y_sum"), NCH * (n - 1) + 2 * half + 2)
                    got = sem(f"rw2_in{half}")
                    pool.dma_start(r2_halves[:, :, half, :], tiles[:, :, half * HALF_W:half * HALF_W + HALF_W])\
                        .then_inc(got, 16)
                    if half == 0:
                        a, z = KEEP_AT["PC"]
                        pool.dma_start(r2_PC[:, n % 2, :, :], tiles[:, :, a:z]).then_inc(got, 16)
                    for g in range(GT):
                        for par in range(2):
                            pool.dma_start(r2m[64 * par:64 * par + 64, g, half:4:2, :], mu[GT * n + g, par, half, :, :, :])\
                                .then_inc(got, 16)
                if n:
                    pool.wait_ge(sem("rw2_group_done"), n)
                pool.dma_start(r2k[:, :, 2 * HALF_W:2 * HALF_W + 2 * T], tiles[:, :, 2 * HALF_W:2 * HALF_W + 2 * T])\
                    .then_inc(sem("rw2_in_all"), 16)

        def rw2_loads(half, n):
            return 16 * (2 * GT + 2 - half) * (n + 1)

        def rw2_pe(pe):
            def group(n):
                for c in range(NCH):
                    if c % 2 == 0:
                        pe.wait_ge(sem(f"rw2_in{c // 2}"), rw2_loads(c // 2, n))
                    k = NCH * n + c
                    tb = slice(64 * (c % 2), 64 * (c % 2) + 64)
                    pe.wait_ge(sem("rw2_S"), k + 1)
                    par = c % 2
                    row = lambda q, g, head: kept("rows", g, c, q * P + 64 * head, 64)[tb, :]
                    heads = [(g, head) for g in range(GT) for head in range(2)]

                    def by_rows(terms):
                        seen = set()
                        for rows in (0, 1):
                            if rows:
                                pe.drain()
                            for r, quadrant, out, lhs, rhs in terms:
                                if r == rows:
                                    last = pe.matmul(out, lhs, rhs, start=quadrant not in seen, stop=True,
                                                     skip_group_check=True)
                                    seen.add(quadrant)
                        return last

                    if n and c == 0:
                        pe.wait_ge(sem("rw2_root"), GT // 2 * n)
                    terms = []
                    for g, head in heads:
                        h, j, u = 2 * g + head, slice(64 * head, 64 * head + 64), 2 * head + c // 2
                        out = pm[0][tb, h * 64:h * 64 + 64]
                        terms.append((head, par, out, kept("AR", g, c, par * 128, 64)[j, :], r2_S[j, g * 64:g * 64 + 64]))
                        terms.append((par, par, out, kept("GK", g, c, head * 128, 64)[tb, :], row(2, g, head)))
                    by_rows(terms).then_inc(sem("rw2_X_sum"), 1)
                    yield
                    pe.wait_ge(sem("rw2_X"), k + 1)
                    for g, head in heads:
                        h, u = 2 * g + head, 2 * head + c // 2
                        mm = pe.matmul(pm[1][tb, h * 64:h * 64 + 64], r2m[tb, g, u, :],
                                       r2_X[tb, h * 64:h * 64 + 64], start=True, stop=True)
                    mm.then_inc(sem("rw2_U_sum"), 1)
                    yield
                    pe.wait_ge(sem("rw2_U"), k + 1)
                    for g, head in heads:
                        h, j = 2 * g + head, slice(64 * head, 64 * head + 64)
                        out = pm[3][j, g * 64:g * 64 + 64]
                        pe.matmul(out, row(0, g, head), r2_U[tb, h * 64:h * 64 + 64], start=True, stop=False)
                        mm = pe.matmul(out, row(1, g, head), row(2, g, head), start=False, stop=True)
                    mm.then_inc(sem("rw2_S_sum"), 1)
                    if k:
                        pe.wait_ge(sem("rw2_Y"), k)
                    terms = []
                    for g, head in heads:
                        h, j, u = 2 * g + head, slice(64 * head, 64 * head + 64), 2 * head + c // 2
                        out = pm[2][j, g * 64:g * 64 + 64]
                        terms.append((head, head, out, r2_S[j, g * 64:g * 64 + 64],
                                      kept("AR", g, c, par * 128 + 64, 64)[j, :]))
                        terms.append((par, head, out, r2_U[tb, h * 64:h * 64 + 64], kept("GBR", g, c, head * 64, 64)[tb, :]))
                        terms.append((par, head, out, row(2, g, head), kept("GK", g, c, head * 128 + 64, 64)[tb, :]))
                    by_rows(terms).then_inc(sem("rw2_Y_sum"), 1)
                    yield
                for pair in range(GT // 2):
                    q = (GT // 2) * n + pair
                    pe.wait_ge(sem("rw2_Y"), NCH * (n + 1))
                    pe.matmul(pm[0][:, :], const("head_mean"), r2_Y[:, pair * 512:pair * 512 + 512], start=True, stop=True)\
                        .then_inc(sem("rw2_mean"), 1)
                    yield
                    pe.wait_ge(sem("rw2_sq"), q + 1)
                    pe.matmul(pm[1][:, :], const("head_mean"), r2_sq, start=True, stop=True).then_inc(sem("rw2_var"), 1)
                    yield
            for n in range(RW_TILES // GT):
                yield from group(n)

        def rw2_act(act):
            def group(n):
                for c in range(NCH):
                    k = NCH * n + c
                    tb = slice(64 * (c % 2), 64 * (c % 2) + 64)
                    act.wait_ge(sem("rw2_X_sum"), k + 1)
                    act.activation(r2_X[tb, :], pm[0][tb, :], ACT.Copy).then_inc(sem("rw2_X"), 1)
                    yield
                    act.wait_ge(sem("rw2_U_sum"), k + 1)
                    act.activation(r2_U[tb, :], pm[1][tb, :], ACT.Copy).then_inc(sem("rw2_U"), 1)
                    yield
                    act.wait_ge(sem("rw2_Y_sum"), k + 1)
                    if n and c == 0:
                        act.wait_ge(sem("rw2_group_done"), n)
                    act.activation(r2_Y.rearrange("p (g t) -> p g t", g=GT)[:, :, c * C:c * C + C],
                                   pm[2][:, 0:256].rearrange("p (g t) -> p g t", g=GT), ACT.Copy)\
                        .then_inc(sem("rw2_Y"), 1)
                    yield
                for pair in range(GT // 2):
                    q = (GT // 2) * n + pair
                    act.wait_ge(sem("rw2_centred"), q + 1)
                    act.activation(r2_sq, r2_d, ACT.Square).then_inc(sem("rw2_sq"), 1)
                    yield
                    act.wait_ge(sem("rw2_var"), q + 1)
                    act.activation(r2_sq, pm[1][:, :], ACT.Sqrt, bias=small[:, 2:3]).then_inc(sem("rw2_root"), 1)
                    yield
            for n in range(RW_TILES // GT):
                yield from group(n)

        def rw2_dve(dve):
            def group(n):
                dve.wait_ge(sem("rw2_in0"), rw2_loads(0, n))
                if n == 0:
                    dve.memset(r2_S, 0.0).then_inc(sem("rw2_S"), 1)
                for c in range(NCH):
                    k = NCH * n + c
                    dve.wait_ge(sem("rw2_S_sum"), k + 1)
                    if c == NCH - 1:
                        continue
                    S3 = r2_S.rearrange("p (g i) -> p g i", g=GT)
                    dve.wait_ge(sem("rw2_Y_sum"), k + 1)
                    dve.tensor_tensor(S3, S3, pm[3][:, 0:256].rearrange("p (g i) -> p g i", g=GT), ALU.add)
                    dve.drain()
                    dve.tensor_tensor(S3, S3, r2_PC[:, n % 2, :, c:c + 1].to_broadcast([P, GT, 64]), ALU.mult)\
                        .then_inc(sem("rw2_S"), 1)
                if n + 1 < RW_TILES // GT:
                    dve.wait_ge(sem("rw2_Y_sum"), NCH * (n + 1))
                    dve.memset(r2_S, 0.0).then_inc(sem("rw2_S"), 1)
                dve.wait_ge(sem("rw2_in_all"), 16 * (n + 1))
                for pair in range(GT // 2):
                    q = (GT // 2) * n + pair
                    y = r2_Y[:, pair * 512:pair * 512 + 512]
                    dve.wait_ge(sem("rw2_mean"), q + 1)
                    if q:
                        dve.drain()
                    dve.tensor_tensor(r2_d, y, pm[0][:, :], ALU.subtract).then_inc(sem("rw2_centred"), 1)
                    dve.wait_ge(sem("rw2_root"), q + 1)
                    dve.reciprocal(r2_sq, r2_sq)
                    dve.drain()
                    dve.tensor_tensor(r2_d, r2_d, r2_sq, ALU.mult)
                    dve.drain()
                    for h in range(2):
                        g = 2 * pair + h
                        b = GT * n + g
                        d = r2_d[:, h * 256:h * 256 + 256]
                        dve.tensor_scalar(d, d, norm_param("ln_w")[:, b:b + 1], norm_param("ln_b")[:, b:b + 1],
                                          ALU.mult, ALU.add)
                        dve.drain()
                        dve.tensor_tensor(d, d, kept_all("bonus", g), ALU.add)
                        dve.drain()
                        last = dve.tensor_tensor(obT[:, b, :], d, kept_all("g", g), ALU.mult)
                last.then_inc(sem("rw2_group_done"), 1)
                yield
            for n in range(RW_TILES // GT):
                yield from group(n)

        SB_AT, NSA_AT_HEAD, XA_AT = DA_HEADS, DA_HEADS + 8, DA_HEADS + 8 + 16
        NSA_SOFT_AT, XA_SOFT_AT = DA_HEADS, DA_HEADS + 16
        oaT = arena[:, 0:4096].rearrange("p (b t) -> p b t", b=DB)
        DA_AT = 12288
        (da_in, da_q, da_k, da_t, da_s, da_p, da_pt, da_sq, da_r, da_st) = carve(
            2 * 1536, 512, 512, 512, 768, 384, 384, 512, 256, 16, at=DA_AT)
        dain = da_in.rearrange("p (s c n) -> p s c n", s=2, c=3)
        LAM = small[:, 20:22]

        def da_pool(pool):
            stage_stored(pool, "v")
            for h in range(DA_HEADS):
                s = h % 2
                if h >= 2:
                    pool.wait_ge(sem("attn_head_done"), h - 1)
                elif h == 0:
                    all_kept(pool)
                for c, row in enumerate([PLAN["qk"].store + h, PLAN["qk"].store + 8 + h, PLAN["v"].store + h]):
                    pool.dma_start(dain[:, s, c, :], units[row, :, :]).then_inc(sem(f"da_in{s}"), 16)

        def da_pe(pe):
            pe.wait_ge(sem("lam_in"), 1)
            pe.wait_ge(sem("rw1_rows"), RW_TILES)
            pe.wait_ge(sem("rw1_tile_done"), RW_TILES)
            pe.matmul(pm[0][:, 0:2], const("ones"), da_st[:, 0:2], start=True, stop=True).then_inc(sem("lam_sum"), 1)
            pe.wait_ge(sem("lam_done"), 1)

            def head(i, s):
                h1 = 2 * i + s + 1
                pe.wait_ge(sem(f"da_in{s}"), 48 * i + 48)
                pe.matmul(pm[0][:, :], const("rotate"), dain[:, s, 0, :], start=True, stop=True)
                pe.matmul(pm[1][:, :], const("rotate"), dain[:, s, 1, :], start=True, stop=True)\
                    .then_inc(sem("da_rotated"), 1)
                yield
                pe.wait_ge(sem("da_roped"), h1)
                for m in range(2):
                    q, k = da_q[:, m * T:m * T + T], da_k[:, m * T:m * T + T]
                    pe.matmul(pm[m][:, 0:256], q[:, P:T], k, start=True, stop=True)
                    mm = pe.matmul(pm[m][:, 256:384], q[:, 0:P], k[:, 0:P], start=True, stop=True)
                mm.then_inc(sem("attn_scores"), 1)
                yield
                pe.wait_ge(sem("attn_probs"), h1)
                pe.transpose(pm[2][:, 0:128], da_p[:, 256:384], const("identity"))
                pe.transpose(pm[2][:, 128:256], da_p[:, 0:128], const("identity"))
                pe.transpose(pm[2][:, 256:384], da_p[:, 128:256], const("identity")).then_inc(sem("attn_turned"), 1)
                yield
                pe.wait_ge(sem("attn_pt"), h1)
                for e in range(2):
                    v = dain[:, s, 2, :].rearrange("p (h e) -> p h e", h=2)
                    pe.matmul(pm[3][:, e * T:e * T + T], v[:, 0, e * P:e * P + P], da_pt[:, 0:256], start=True, stop=False)
                    mm = pe.matmul(pm[3][:, e * T + P:e * T + T], v[:, 1, e * P:e * P + P], da_pt[:, 256:384],
                                   start=False, stop=True)
                mm.then_inc(sem("attn_out"), 1)
                yield
                pe.wait_ge(sem("da_sq"), h1)
                pe.matmul(pm[2][:, 0:256], const("ones"), da_sq[:, 0:256], start=True, stop=False)
                pe.matmul(pm[2][:, 0:256], const("ones"), da_sq[:, 256:512], start=False, stop=True)\
                    .then_inc(sem("da_sq_sum"), 1)
                yield
            for h in range(DA_HEADS):
                yield from head(h // 2, h % 2)

        def da_dve(dve):
            all_kept(dve)
            dve.tensor_tensor(da_st[:, 0:2], misc("lam_q"), misc("lam_k"), ALU.mult).then_inc(sem("lam_in"), 1)
            dve.wait_ge(sem("lam_exp"), 1)
            dve.tensor_tensor(LAM[:, 0:1], da_st[:, 3:4], da_st[:, 2:3], ALU.subtract)
            dve.drain()
            dve.tensor_scalar(LAM[:, 1:2], LAM[:, 0:1], -LAMBDA_INIT, None, ALU.add)
            dve.tensor_scalar(da_st[:, 14:16], misc("subln"), 1.0 - LAMBDA_INIT, None, ALU.mult)
            dve.drain().then_inc(sem("lam_done"), 1)

            def head(i, s):
                h1 = 2 * i + s + 1
                h = 2 * i + s
                dve.wait_ge(sem(f"da_in{s}"), 48 * i + 48)
                two = lambda v: v.rearrange("p (m t) -> p m t", m=2)
                rep = lambda n: const(n).unsqueeze(1).to_broadcast([P, 2, T])
                dve.tensor_tensor(two(da_q), two(dain[:, s, 0, :]), rep("cos"), ALU.mult)
                dve.tensor_tensor(two(da_k), two(dain[:, s, 1, :]), rep("cos"), ALU.mult)
                dve.wait_ge(sem("da_rotated"), h1)
                dve.tensor_tensor(two(da_t), two(pm[0][:, :]), rep("sin"), ALU.mult)
                dve.tensor_tensor(two(da_sq), two(pm[1][:, :]), rep("sin"), ALU.mult)
                dve.drain()
                dve.tensor_tensor(da_q, da_q, da_t, ALU.add)
                dve.tensor_tensor(da_k, da_k, da_sq, ALU.add).then_inc(sem("da_roped"), 1)
                yield
                dve.wait_ge(sem("attn_scores"), h1)
                S = da_s.rearrange("p (m n) -> p m n", m=2)
                for m in range(2):
                    dve.tensor_tensor(S[:, m, :], pm[m][:, 0:384], const("chunk_mask"), ALU.add)
                dve.drain()
                dve.reduce_max(da_st[:, 0:2], S[:, :, 0:256], AX.X)
                dve.reduce_max(da_st[:, 2:4], S[:, :, 256:384], AX.X)
                dve.drain()
                dve.tensor_scalar(da_st[:, 4:8], da_st[:, 0:4], -float(P) ** -0.5, None, ALU.mult)\
                    .then_inc(sem("attn_max"), 1)
                dve.wait_ge(sem("attn_exp"), h1)
                dve.reciprocal(da_st[:, 8:12], da_st[:, 8:12])
                dve.drain()
                dve.tensor_scalar(da_st[:, 12:13], da_st[:, 9:10], LAM[:, 1:2], None, ALU.mult)
                dve.tensor_scalar(da_st[:, 13:14], da_st[:, 11:12], LAM[:, 1:2], None, ALU.mult)
                dve.drain()
                for qb, (a, z) in enumerate([(0, 256), (256, 384)]):
                    dve.tensor_scalar(da_t[:, a:z], S[:, 0, a:z], da_st[:, 8 + 2 * qb:9 + 2 * qb], None, ALU.mult)
                dve.drain()
                for qb, (a, z) in enumerate([(0, 256), (256, 384)]):
                    last = dve.scalar_tensor_tensor(da_p[:, a:z], S[:, 1, a:z], da_st[:, 12 + qb:13 + qb], da_t[:, a:z],
                                                    ALU.mult, ALU.add)
                last.then_inc(sem("attn_probs"), 1)
                yield
                yield
                yield
                dve.wait_ge(sem("da_root"), h1)
                dve.reciprocal(da_r, da_r)
                dve.drain()
                for e in range(2):
                    o = oaT[:, 2 * h + e, :] if isinstance(h, int) else \
                        arena[:, bass.ds(h * 512 + e * 256, 256)]
                    last = dve.scalar_tensor_tensor(o, pm[3][:, e * T:e * T + T], da_st[:, 14 + e:15 + e], da_r,
                                                    ALU.mult, ALU.mult)
                last.then_inc(sem("attn_head_done"), 1)
                yield
            for h in range(DA_HEADS):
                yield from head(h // 2, h % 2)

        def da_act(act):
            act.wait_ge(sem("lam_sum"), 1)
            act.activation(da_st[:, 2:4], pm[0][:, 0:2], ACT.Exp).then_inc(sem("lam_exp"), 1)

            def head(i, s):
                h1 = 2 * i + s + 1
                yield
                act.wait_ge(sem("attn_max"), h1)
                S = da_s.rearrange("p (m n) -> p m n", m=2)
                for qb, (a, z) in enumerate([(0, 256), (256, 384)]):
                    for m in range(2):
                        n = 2 * qb + m
                        act.activation(S[:, m, a:z], S[:, m, a:z], ACT.Exp, scale=float(P) ** -0.5,
                                       bias=da_st[:, 4 + n:5 + n], accum_out=da_st[:, 8 + n:9 + n])
                act.drain().then_inc(sem("attn_exp"), 1)
                yield
                act.wait_ge(sem("attn_turned"), h1)
                act.activation(da_pt, pm[2][:, 0:384], ACT.Copy).then_inc(sem("attn_pt"), 1)
                yield
                act.wait_ge(sem("attn_out"), h1)
                act.activation(da_sq, pm[3][:, :], ACT.Square).then_inc(sem("da_sq"), 1)
                yield
                act.wait_ge(sem("da_sq_sum"), h1)
                act.activation(da_r, pm[2][:, 0:256], ACT.Sqrt, scale=1.0 / 256, bias=small[:, 1:2])\
                    .then_inc(sem("da_root"), 1)
                yield
            for h in range(DA_HEADS):
                yield from head(h // 2, h % 2)

        gates = arena[:, 4096:4096 + 8192].rearrange("p (b t) -> p b t", b=32)
        mixT = hT[:, :, :]

        def gates_pool(pool):
            stage_stored(pool, "gates")
            pool.wait_ge(sem("rw2_group_done"), RW_TILES // GT)
            st = PLAN["gates"]
            for n in range(16):
                pool.dma_start(gates[:, 2 * n:2 * n + 2, :].rearrange("p b t -> p (b t)"), units[st.store + n, :, :])\
                    .then_inc(sem(f"gates_in{n // 8}"), 16)

        def branch_a_act(act):
            st = PLAN["branch_a"]
            act.wait_ge(w_used, PLAN["gates"].slot + 16)
            for u in range(8):
                yield
                yield
                yield
                b = (st.bank + u) % 4
                unit_done(act, st, 0, u)
                act.activation(mixT[:, 2 * u:2 * u + 2, :], psg[b][:, :].rearrange("p (h t) -> p h t", h=2), ACT.Copy)\
                    .then_inc(bank_free[b], 1)
                yield
            act.drain().then_inc(sem("branch_a_ready"), 1)

        def gates_dve(dve):
            b = params[:, 16 * NORMS.index("b_gate_a"):16 * NORMS.index("b_gate_a") + 32]
            for w in range(2):
                g = gates[:, 16 * w:16 * w + 16, :]
                dve.wait_ge(sem(f"gates_in{w}"), 128)
                dve.tensor_tensor(g, g, b[:, 16 * w:16 * w + 16].unsqueeze(2).to_broadcast([P, 16, T]), ALU.add)\
                    .then_inc(sem("gates_biased"), 1)
            dve.wait_ge(sem("gates_open"), 1)
            dve.wait_ge(sem("branch_a_ready"), 1)
            dve.tensor_tensor(mixT, mixT, gates[:, 0:16, :], ALU.mult)
            dve.wait_ge(sem("gates_open"), 2)
            st = PLAN["branch_b"]
            for u in range(8):
                b = (st.bank + u) % 4
                unit_done(dve, st, 0, u)
                mix = mixT[:, 2 * u:2 * u + 2, :]
                g = gates[:, 16 + 2 * u:16 + 2 * u + 2, :]
                dve.tensor_tensor(g, psg[b][:, :].rearrange("p (h t) -> p h t", h=2), g, ALU.mult).then_inc(bank_free[b], 1)
                dve.drain()
                dve.tensor_tensor(mix, mix, g, ALU.add)
            dve.drain().then_inc(sem("mix_ready"), 1)

        def gates_act(act):
            for w in range(2):
                g = gates[:, 16 * w:16 * w + 16, :]
                act.wait_ge(sem("gates_biased"), w + 1)
                act.activation(g, g, ACT.Sigmoid).then_inc(sem("gates_open"), 1)

        fT = arena[:, 0:FB * T].rearrange("p (b t) -> p b t", b=FB)
        silu = carve(4 * T, at=16384)[0].rearrange("p (s t) -> p s t", s=4)

        def ffn_act(act):
            st = PLAN["ffn_in"]

            def unit(i, j):
                b = (st.bank + j) % 4
                unit_done(act, st, i, j)
                u = 4 * i + j
                if not (isinstance(u, int) and u < 4):
                    act.wait_ge(sem("ffn_mul"), u - 3)
                act.activation(silu[:, j % 4, :], psg[b][:, 0:T], ACT.Silu).then_inc(sem("ffn_silu"), 1)
            for u in range(4):
                unit(0, u)
            with act.Fori(1, st.units // 4) as i:
                for j in range(4):
                    unit(i, j)

        def ffn_dve(dve):
            st = PLAN["ffn_in"]

            def unit(i, j):
                b = (st.bank + j) % 4
                dve.wait_ge(sem("ffn_silu"), 4 * i + j + 1)
                u = 4 * i + j
                dst = fT[:, u, :] if isinstance(u, int) else arena[:, bass.ds(u * T, T)]
                dve.tensor_tensor(dst, silu[:, j % 4, :], psg[b][:, T:2 * T], ALU.mult)
                dve.drain().then_inc(bank_free[b], 1)
                dve.nop().then_inc(sem("ffn_mul"), 1)
            for u in range(4):
                unit(0, u)
            with dve.Fori(1, st.units // 4) as i:
                for j in range(4):
                    unit(i, j)
            dve.drain().then_inc(sem("ffn_ready"), 1)

        def mem_pool(pool):
            pool.wait_ge(w_used, PLAN["ffn_in"].slot + PLAN["ffn_in"].units)
            pool.dma_start(hT[:, :, :], t_in["memT"]).then_inc(sem("mem_loaded"), 16)

        ST = 16
        (s5_u, s5_Er, s5_Ei, s5_x, s5_q, s5_w, _, s5_more) = carve(1024, 4096, 4096, 2048, 16 * 24, 2048, 4608, 1024)
        s5_t = yT.rearrange("p b t -> p (b t)")
        s5q = s5_q.rearrange("p (n b) -> p n b", b=16)
        s5_BC = [half[:, n:n + 512] for half in (s5_t[:, 2048:3072], s5_more) for n in (0, 512)]
        s5_wglu = s5_w.rearrange("p (k n) -> p k n", k=4)
        uT = s5_u.rearrange("p (b t) -> p b t", b=4)
        s5yT, s5zT = hT[:, 8:12, :], hT[:, 12:16, :]
        Er, Ei = s5_Er.rearrange("p (b t) -> p b t", b=ST), s5_Ei.rearrange("p (b t) -> p b t", b=ST)
        SQ = ["delta", "mag", "th", "k", "r", "rc", "sin", "cos", "ar1", "ai", "den", "cr", "ci", "nci", "a", "b",
              "pr", "pi"]

        def q5(name):
            return s5q[:, SQ.index(name), :]

        def s5_pool(pool):
            pool.wait_ge(sem("block1_done"), NCK)
            pool.dma_start(s5_wglu, t_in["w_glu"]).then_inc(sem("s5_glu_in"), 16)
            stage_stored(pool, "u5")
            for n in range(2):
                pool.dma_start(s5_u[:, 512 * n:512 * n + 512], units[PLAN["u5"].store + n, :, :]).then_inc(sem("s5_u_in"), 16)
            for i in range(ST):
                if i == 7:
                    sb_pool(pool)
                if i >= 4:
                    pool.wait_ge(sem("s5_tile_read"), i - 3)
                pool.dma_start(s5_BC[i % 4], t_in["s5_bc"][i, :, :]).then_inc(sem(f"s5_bc_in{i % 4}"), 16)

        def s5_angles_act(act):
            act.wait_ge(sem("block1_done"), NCK)
            act.activation(q5("delta"), misc("log_dt"), ACT.Exp).then_inc(sem("s5_delta"), 1)
            act.wait_ge(sem("s5_th"), 1)
            act.activation(q5("mag"), q5("a"), ACT.Exp)
            act.activation(q5("sin"), q5("r"), ACT.Sin)
            act.activation(q5("cos"), q5("rc"), ACT.Sin).then_inc(sem("s5_trig"), 1)

        def s5_act(act):
            for n in range(3 * ST + 2):
                yield
            for ct in range(4):
                act.wait_ge(sem("s5_y"), ct + 1)
                act.activation(s5zT[:, ct, :], s5yT[:, ct, :], ACT.Gelu_apprx_tanh)
            act.drain().then_inc(sem("s5_gelu"), 1)
            yield
            for n in range(4):
                act.wait_ge(sem("s5_glu_sum"), n + 1)
                act.activation(s5yT[:, n, :], pm[n % 2][:, 0:T], ACT.Sigmoid, bias=misc("s5_b_glu")[:, n:n + 1])\
                    .then_inc(sem("s5_glu"), 1)
            yield

        def s5_dve(dve):
            dr = dve.drain
            tt, ts, stt = dve.tensor_tensor, dve.tensor_scalar, dve.scalar_tensor_tensor
            two_pi = 2 * math.pi
            C1, C2 = 6.28125, float(np.float32(two_pi - 6.28125))
            C3 = two_pi - 6.28125 - C2
            ROUND = 1.5 * 2.0 ** 23
            dve.wait_ge(sem("s5_delta"), 1)
            ts(q5("cr"), misc("lam_re"), 0.0, None, ALU.add)
            tt(q5("a"), misc("lam_re"), q5("delta"), ALU.mult)
            tt(q5("th"), misc("lam_im"), q5("delta"), ALU.mult)
            dr()
            ts(q5("k"), q5("th"), 1 / two_pi, ROUND, ALU.mult, ALU.add)
            dr()
            ts(q5("k"), q5("k"), -ROUND, None, ALU.add)
            dr()
            stt(q5("r"), q5("k"), -C1, q5("th"), ALU.mult, ALU.add)
            dr()
            stt(q5("r"), q5("k"), -C2, q5("r"), ALU.mult, ALU.add)
            dr()
            stt(q5("r"), q5("k"), -C3, q5("r"), ALU.mult, ALU.add)
            dr()
            PI = 3.1415925
            ts(q5("r"), q5("r"), PI, -PI, ALU.min, ALU.max)
            dr()
            ts(q5("rc"), q5("r"), math.pi / 2, None, ALU.add)
            dr()
            ts(q5("b"), q5("rc"), PI, -two_pi, ALU.is_gt, ALU.mult)
            dr()
            tt(q5("rc"), q5("rc"), q5("b"), ALU.add)
            dr()
            ts(q5("rc"), q5("rc"), PI, -PI, ALU.min, ALU.max).then_inc(sem("s5_th"), 1)
            dve.wait_ge(sem("s5_trig"), 1)
            tt(q5("ar1"), q5("mag"), q5("cos"), ALU.mult)
            tt(q5("ai"), q5("mag"), q5("sin"), ALU.mult)
            tt(q5("a"), misc("lam_re"), misc("lam_re"), ALU.mult)
            tt(q5("b"), misc("lam_im"), misc("lam_im"), ALU.mult)
            dr()
            ts(q5("ar1"), q5("ar1"), -1.0, None, ALU.add)
            tt(q5("den"), q5("a"), q5("b"), ALU.add)
            dr()
            dve.reciprocal(q5("den"), q5("den"))
            tt(q5("cr"), q5("ar1"), misc("lam_re"), ALU.mult)
            tt(q5("a"), q5("ai"), misc("lam_im"), ALU.mult)
            tt(q5("ci"), q5("ai"), misc("lam_re"), ALU.mult)
            tt(q5("b"), q5("ar1"), misc("lam_im"), ALU.mult)
            dr()
            tt(q5("cr"), q5("cr"), q5("a"), ALU.add)
            tt(q5("ci"), q5("ci"), q5("b"), ALU.subtract)
            dr()
            tt(q5("cr"), q5("cr"), q5("den"), ALU.mult)
            tt(q5("ci"), q5("ci"), q5("den"), ALU.mult)
            dr()
            ts(q5("nci"), q5("ci"), -1.0, None, ALU.mult)
            dve.tensor_copy(Er[:, :, 0], q5("cos"))
            dve.tensor_copy(Ei[:, :, 0], q5("sin"))
            dr()
            tmp = s5_t[:, 0:2048].rearrange("p (b t) -> p b t", b=ST)
            m = 1
            while m < T:
                br = Er[:, :, m - 1:m].to_broadcast([P, ST, m])
                bi = Ei[:, :, m - 1:m].to_broadcast([P, ST, m])
                a, b = Er[:, :, 0:m], Ei[:, :, 0:m]
                cr_, ci_ = Er[:, :, m:2 * m], Ei[:, :, m:2 * m]
                t0 = tmp[:, :, 0:m]
                tt(t0, b, bi, ALU.mult)
                tt(cr_, a, br, ALU.mult)
                dr()
                tt(cr_, cr_, t0, ALU.subtract)
                dr()
                tt(t0, b, br, ALU.mult)
                tt(ci_, a, bi, ALU.mult)
                dr()
                tt(ci_, ci_, t0, ALU.add)
                dr()
                m *= 2
            X = [s5_x[:, 256 * n:256 * n + 256] for n in range(8)]
            xr5, xi5, wr, wi, t1, t2, zr, zi = X
            def output(ct):
                dve.wait_ge(sem("s5_out_sum"), ct + 1)
                stt(s5yT[:, ct, :], uT[:, ct, :], misc("s5_d")[:, ct:ct + 1], pm[2][:, 0:T],
                    ALU.mult, ALU.add).then_inc(sem("s5_y"), 1)

            for i in range(ST):
                er, ei = Er[:, i, :], Ei[:, i, :]
                col = lambda n: q5(n)[:, i:i + 1]
                dve.wait_ge(sem("s5_in_sum"), i + 1)
                pr, pi = pm[i % 2][:, 0:T], pm[i % 2][:, T:2 * T]
                ts(xr5, pr, col("cr"), None, ALU.mult)
                ts(xi5, pr, col("ci"), None, ALU.mult)
                dr()
                stt(xr5, pi, col("nci"), xr5, ALU.mult, ALU.add)
                stt(xi5, pi, col("cr"), xi5, ALU.mult, ALU.add).then_inc(sem("s5_in_read"), 1)
                dr()
                yield
                tt(wr, xr5, er, ALU.mult)
                tt(wi, xi5, er, ALU.mult)
                tt(t1, xi5, ei, ALU.mult)
                tt(t2, xr5, ei, ALU.mult)
                dr()
                tt(wr, wr, t1, ALU.add)
                tt(wi, wi, t2, ALU.subtract)
                dr()
                mag = col("mag").to_broadcast([P, T])
                dve.tensor_tensor_scan(zr, mag, wr, 0.0, ALU.mult, ALU.add)
                dve.tensor_tensor_scan(zi, mag, wi, 0.0, ALU.mult, ALU.add)
                dr()
                yield
                if i and i % 4 == 0:
                    output(i // 4 - 1)
                S = s5_t[:, 3072 + 512 * (i % 2):3072 + 512 * (i % 2) + 512]
                if i >= 2:
                    dve.wait_ge(sem("s5_tile_read"), i - 1)
                tt(t1, zi, ei, ALU.mult)
                tt(t2, zr, ei, ALU.mult)
                tt(S[:, 0:T], zr, er, ALU.mult)
                tt(S[:, T:2 * T], zi, er, ALU.mult)
                dr()
                tt(S[:, 0:T], S[:, 0:T], t1, ALU.subtract)
                stt(S[:, T:2 * T], S[:, T:2 * T], -1.0, t2, ALU.mult, ALU.subtract).then_inc(sem("s5_states"), 1)
                yield
            yield
            yield
            output(ST // 4 - 1)
            yield
            for n in range(4):
                dve.wait_ge(sem("s5_glu"), n + 1)
                last = tt(hT[:, n, :], s5zT[:, n, :], s5yT[:, n, :], ALU.mult)
            last.then_inc(sem("s5_done"), 1)
            yield

        def s5_pe(pe):
            pe.wait_ge(sem("s5_u_in"), 32)

            def inputs(i):
                pe.wait_ge(sem(f"s5_bc_in{i % 4}"), 16 * (i // 4 + 1))
                if i >= 2:
                    pe.wait_ge(sem("s5_in_read"), i - 1)
                bc = s5_BC[i % 4]
                pe.matmul(pm[i % 2][:, 0:T], bc[:, 0:P], uT[:, i // 4, :], start=True, stop=True)
                pe.matmul(pm[i % 2][:, T:2 * T], bc[:, P:2 * P], uT[:, i // 4, :], start=True, stop=True)\
                    .then_inc(sem("s5_in_sum"), 1)

            def outputs(i):
                pe.wait_ge(sem("s5_states"), i + 1)
                ct = i // 4
                if i % 4 == 0 and ct:
                    pe.wait_ge(sem("s5_y"), ct)
                S = s5_t[:, 3072 + 512 * (i % 2):3072 + 512 * (i % 2) + 512]
                bc = s5_BC[i % 4]
                pe.matmul(pm[2][:, 0:T], bc[:, 2 * P:3 * P], S[:, 0:T], start=i % 4 == 0, stop=False)
                mm = pe.matmul(pm[2][:, 0:T], bc[:, 3 * P:4 * P], S[:, T:2 * T], start=False, stop=i % 4 == 3)
                mm.then_inc(sem("s5_tile_read"), 1)
                if i % 4 == 3:
                    pe.wait_ge(sem("s5_tile_read"), i + 1)
                    pe.nop().then_inc(sem("s5_out_sum"), 1)

            inputs(0)
            for i in range(ST):
                if i + 1 < ST:
                    inputs(i + 1)
                yield
                if i:
                    outputs(i - 1)
                yield
                yield
            yield
            outputs(ST - 1)
            yield
            yield
            pe.wait_ge(sem("s5_gelu"), 1)
            pe.wait_ge(sem("s5_glu_in"), 16)
            for n in range(4):
                if n >= 2:
                    pe.wait_ge(sem("s5_glu"), n - 1)
                for k in range(4):
                    mm = pe.matmul(pm[n % 2][:, 0:T], s5_wglu[:, k, n * P:n * P + P], s5zT[:, k, :],
                                   start=k == 0, stop=k == 3)
                mm.then_inc(sem("s5_glu_sum"), 1)
            yield

        SB_HEADS = 8
        sb_in, sb_v, sb_z, sb_e, sb_l, sb_w = carve(2048, 1024, 384, 384, 384, 384, at=13696)
        sbqk = sb_in.rearrange("p (w b t) -> p w b t", w=2, b=4)
        sbv = sb_v.rearrange("p (n h e) -> p n h e", n=2, h=2)
        HSCALE = 64.0 ** -0.5

        def sb_pool(pool):
            stage_stored(pool, "sv")
            for n in range(4):
                pool.dma_start(sb_in[:, 512 * n:512 * n + 512], units[PLAN["sqk"].store + n, :, :]).then_inc(sem("sb_in"), 16)
            for n in range(2):
                pool.dma_start(sb_v[:, 512 * n:512 * n + 512], units[PLAN["sv"].store + n, :, :]).then_inc(sem("sb_in"), 16)

        def sb_pe(pe):
            pe.wait_ge(sem("sb_in"), 96)

            def output(h):
                pe.wait_ge(sem("attn_probs"), SB_AT + h + 1)
                r = slice(64 * (h % 2), 64 * (h % 2) + 64)
                v = sbv[:, h // 4, :, 64 * (h % 4):64 * (h % 4) + 64]
                out = pm[3][r, 0:256]
                pe.matmul(out, v[:, 0, :], sb_w[:, 0:256], start=True, stop=False)
                pe.matmul(out[:, P:256], v[:, 1, :], sb_w[:, 256:384], start=False, stop=True).then_inc(sem("attn_out"), 1)

            for h in range(SB_HEADS):
                r, b = slice(64 * (h % 2), 64 * (h % 2) + 64), h // 2
                q, k = sbqk[r, 0, b, :], sbqk[r, 1, b, :]
                if h:
                    output(h - 1)
                    pe.wait_ge(sem("attn_head_done"), SB_AT + h)
                pe.matmul(pm[3][:, 0:256], k[:, 0:P], q, start=True, stop=True)
                pe.matmul(pm[3][:, 256:384], k[:, P:T], q[:, P:T], start=True, stop=True).then_inc(sem("attn_scores"), 1)
                yield
                yield
                pe.wait_ge(sem("sb_stay"), h + 1)
                pe.matmul(pm[3][:, 0:256], const("later"), sb_l[:, 0:256], start=True, stop=False)
                pe.matmul(pm[3][:, P:256], const("ones"), sb_l[:, 256:384], start=False, stop=True)
                pe.matmul(pm[3][:, 256:384], const("later"), sb_l[:, 256:384], start=True, stop=True)\
                    .then_inc(sem("sb_left"), 1)
                yield
                yield
                yield
            output(SB_HEADS - 1)
            yield

        def sb_act(act):
            def output(h):
                r, b = slice(64 * (h % 2), 64 * (h % 2) + 64), h // 2
                act.wait_ge(sem("attn_out"), SB_AT + h + 1)
                act.activation(hT[r, 4 + b, :], pm[3][r, 0:256], ACT.Copy).then_inc(sem("attn_head_done"), 1)

            for h in range(SB_HEADS):
                if h:
                    output(h - 1)
                act.wait_ge(sem("attn_scores"), SB_AT + h + 1)
                act.activation(sb_e, pm[3][:, 0:384], ACT.Abs, scale=HSCALE)
                act.drain()
                act.activation(sb_e, sb_e, ACT.Exp, scale=-1.0)
                act.drain()
                act.activation(sb_e, sb_e, ACT.Ln, bias=1.0).then_inc(sem("sb_ln"), 1)
                yield
                yield
                yield
                yield
                act.wait_ge(sem("sb_expo"), h + 1)
                act.activation(sb_w, sb_z, ACT.Exp).then_inc(sem("sb_exp"), 1)
                yield
            output(SB_HEADS - 1)
            yield

        def sb_dve(dve):
            for h in range(SB_HEADS):
                yield
                dve.wait_ge(sem("sb_ln"), h + 1)
                dve.tensor_scalar(sb_z, pm[3][:, 0:384], HSCALE, 0.0, ALU.mult, ALU.max)
                dve.drain()
                dve.tensor_tensor(sb_e, sb_e, sb_z, ALU.add)
                dve.drain()
                dve.scalar_tensor_tensor(sb_l, sb_e, -1.0, const("past_mask"), ALU.mult, ALU.mult)
                dve.scalar_tensor_tensor(sb_z, pm[3][:, 0:384], HSCALE, sb_e, ALU.mult, ALU.subtract)
                dve.drain().then_inc(sem("sb_stay"), 1)
                yield
                yield
                dve.wait_ge(sem("sb_left"), h + 1)
                dve.tensor_tensor(sb_z, sb_z, pm[3][:, 0:384], ALU.add).then_inc(sem("sb_expo"), 1)
                yield
                dve.wait_ge(sem("sb_exp"), h + 1)
                dve.tensor_tensor(sb_w, sb_w, const("past_mask"), ALU.mult).then_inc(sem("attn_probs"), 1)
                yield
            yield

        NH, NG, NCMP = 16, 4, 15
        (n_q, n_kd, n_v, n_kcs, n_bias, n_BC, n_g, n_oc) = carve(2048, 2048, 1024, 2 * 1028, 768, 480, 96, NSA_CONST_W)
        at = 2048 + 2048 + 1024 + 2056 + 768 + 480 + 96 + NSA_CONST_W
        NSA_BUFS = (768, 768, 32, 256, 32)
        nsa_bufs = [carve(*NSA_BUFS, at=at + s * sum(NSA_BUFS)) for s in range(2)]
        n_rows = nsa_bufs[0][0]
        n_H, n_kc, n_vc, n_pos = carve(120, 64, 256, 2, at=at + 2 * sum(NSA_BUFS))
        nsa_banks = [pm, psg]
        n_w1 = s5_t[:, 0:4096].rearrange("p (j m n) -> p j m n", j=2, m=16)
        nqT = n_q.rearrange("p (b t) -> p b t", b=8)
        nkd = n_kd.rearrange("p (w g t) -> p w g t", w=2, g=NG)
        nv = n_v.rearrange("p (w h e) -> p w h e", w=2, h=2)
        nkcs = n_kcs.rearrange("p (j g t) -> p j g t", j=2, g=NG)
        nbias = n_bias.rearrange("p (s n) -> p s n", s=2)
        nBC = n_BC.rearrange("p (q h n) -> p q h n", q=2, h=NH)
        ng = n_g.rearrange("p (q h) -> p q h", q=2)

        def nc_(name):
            a, b = NSA_AT[name]
            return n_oc[:, a:b]

        def nsa_pool(pool):
            stage_stored(pool, "nk")
            pool.wait_ge(sem("s5_done"), 1)
            load = lambda d, s, name="nsa_in": pool.dma_start(d, s).then_inc(sem(name), 16)
            load(n_oc[0:N_BUCKETS, 0:ONE_HOTS], t_in["nsa_const"][0:N_BUCKETS, 0:ONE_HOTS])
            load(n_oc[:, ONE_HOTS:], t_in["nsa_const"][:, ONE_HOTS:])
            load(n_w1, t_in["cmp_w1"])
            for n in range(4):
                load(n_q[:, 512 * n:512 * n + 512], units[PLAN["nq"].store + n, :, :])
            for j in range(2):
                u = units[PLAN["nkc"].store + j, :, :]
                for par in range(2):
                    src = u[64 * par:64 * par + 64, :].rearrange("p (g t) -> p g t", g=2)
                    load(nkcs[0:64, j, par:NG:2, 0:256], src)
                    load(nkcs[64:128, j, par:NG:2, 0:255], src[:, :, 1:256])
                u = units[PLAN["nk"].store + j, :, :]
                for par in range(2):
                    src = u[64 * par:64 * par + 64, :].rearrange("p (g t) -> p g t", g=2)
                    for base in (0, 64):
                        load(nkd[base:base + 64, j, par:NG:2, :], src)
            stage_stored(pool, "ng")
            for j in range(2):
                load(n_v[:, 512 * j:512 * j + 512], units[PLAN["nv"].store + j, :, :])
            load(ng, units[PLAN["ng"].store, :, :].rearrange("p (q n) -> p q n", q=2)[:, :, 0:48])
            pool.wait_ge(sem("bias_rows_ready"), 1)
            pool.dma_start(bias_rows, n_rows[0:16, 0:384]).then_inc(sem("bias_rows_stored"), 16)
            pool.wait_ge(sem("bias_rows_stored"), 16)
            for h in range(NH):
                if h >= 2:
                    pool.wait_ge(sem("attn_scores"), NSA_AT_HEAD + h - 1)
                row = bias_rows[h, :]
                tile_ = bass.AP(row.tensor, row.offset, [[1, P], [1, 256]])
                diag = bass.AP(row.tensor, row.offset + 128, [[1, P], [1, 128]])
                pool.dma_start(nbias[:, h % 2, 0:256], tile_).then_inc(sem(f"nsa_bias{h % 2}"), 16)
                pool.dma_start(nbias[:, h % 2, 256:384], diag).then_inc(sem(f"nsa_bias{h % 2}"), 16)

        ONE_HOTS = NSA_AT["onehot_rows"][1]
        N_LOADS = 16 * (3 + 4 + 2 * (4 + 4 + 1) + 1)

        def nsa_pe(pe):
            pe.wait_ge(sem("nsa_in"), N_LOADS)
            pe.wait_ge(sem("attn_head_done"), SB_AT + SB_HEADS)
            tab = nc_("tab")[0:32, :]
            pe.matmul(pm[0][0:16, 0:256], tab, nc_("onehot_rows")[0:32, :], start=True, stop=True)
            oc = nc_("onehot_cmp")
            for qb in range(2):
                for n in range(NCMP):
                    u = qb * NCMP + n
                    pe.matmul(pm[1][:, u * 16:u * 16 + 16], oc[0:32, u * P:u * P + P], tab, start=True, stop=True)
            for j in range(2):
                for m in range(16):
                    pe.matmul(pm[2][:, j:j + 1], n_w1[:, j, m, :], nc_("pos")[:, 16 * j + m:16 * j + m + 1],
                              start=m == 0, stop=m == 15)
                for m in range(16):
                    rhs = nkcs[:, j, :, 2 * m:2 * m + 16 * (NCMP - 1) + 1:16]
                    mm = pe.matmul(pm[3][:, 64 * j:64 * j + 60], n_w1[:, j, m, :], rhs, start=m == 0, stop=m == 15)
            mm.then_inc(sem("nsa_hidden_sum"), 1)
            pe.wait_ge(sem("nsa_hidden"), 1)
            w2k, w2v = nc_("w2")[:, 0:64], nc_("w2")[:, 64:128]
            for half in range(2):
                pe.matmul(pm[2][64 * half:64 * half + 64, 0:60], w2k, n_H[:, 0:60], start=True, stop=True)
            for g in range(NG):
                mm = pe.matmul(pm[3][0:NCMP, 64 * g:64 * g + 64], n_H[:, 60 + 15 * g:75 + 15 * g], w2v, start=True, stop=True)
            mm.then_inc(sem("nsa_kvc_sum"), 1)
            pe.wait_ge(sem("nsa_kvc"), 1)
            pe.wait_ge(sem("bias_rows_ready"), 1)
            for b in range(4):
                done = PLAN["ng"].bank + 1
                pe.wait_ge(bank_free[b], (done - b + 3) // 4)

            def scores(h):
                r, b, g = slice(64 * (h % 2), 64 * (h % 2) + 64), h // 2, h // 4
                bank = nsa_banks[h % 2]
                q = nqT[r, b, :]
                if h >= 2:
                    pe.wait_ge(sem("attn_head_done"), NSA_AT_HEAD + h - 1)
                pe.wait_ge(sem(f"nsa_bias{h % 2}"), 32 * (h // 2 + 1))
                for w in range(2):
                    k = nkd[r, w, g, :]
                    pe.matmul(bank[w][:, 0:384], nc_("flip"), nbias[:, h % 2, :], start=True, stop=False)
                    pe.matmul(bank[w][:, 0:256], q[:, P:T], k, start=False, stop=False)
                    pe.matmul(bank[w][:, 256:384], q[:, 0:P], k[:, 0:P], start=False, stop=True)
                for qb in range(2):
                    mm = pe.matmul(bank[0][:, 384 + 16 * qb:384 + 16 * qb + 15], q[:, qb * P:qb * P + P],
                                   n_kc[r, 15 * g:15 * g + 15], start=True, stop=True)
                mm.then_inc(sem("attn_scores"), 1)

            def turn(h):
                n_s, n_pt, n_cs, n_ct, n_st = nsa_bufs[h % 2]
                bank = nsa_banks[h % 2]
                pe.wait_ge(sem("attn_probs"), NSA_AT_HEAD + h + 1)
                for w in range(2):
                    p = n_s[:, 384 * w:384 * w + 384]
                    pe.transpose(bank[2 + w][:, 0:128], p[:, 256:384], const("identity"))
                    pe.transpose(bank[2 + w][:, 128:256], p[:, 0:128], const("identity"))
                    pe.transpose(bank[2 + w][:, 256:384], p[:, 128:256], const("identity"))
                for qb in range(2):
                    mm = pe.transpose(bank[1][0:NCMP, qb * P:qb * P + P], n_cs[:, 16 * qb:16 * qb + 15], const("identity"))
                mm.then_inc(sem("attn_turned"), 1)

            def output(h):
                n_s, n_pt, n_cs, n_ct, n_st = nsa_bufs[h % 2]
                r, g = slice(64 * (h % 2), 64 * (h % 2) + 64), h // 4
                pe.wait_ge(sem("attn_pt"), NSA_SOFT_AT + h + 1)
                out = nsa_banks[h % 2][0][r, 0:256]
                pe.matmul(out, n_vc[0:NCMP, 64 * g:64 * g + 64], n_ct[0:NCMP, :], start=True, stop=False)
                for w in range(2):
                    v = nv[:, w, :, 64 * g:64 * g + 64]
                    pt = n_pt[:, 384 * w:384 * w + 384]
                    pe.matmul(out, v[:, 0, :], pt[:, 0:256], start=False, stop=False)
                    mm = pe.matmul(out[:, P:256], v[:, 1, :], pt[:, 256:384], start=False, stop=w == 1)
                mm.then_inc(sem("attn_out"), 1)

            scores(0)
            for h in range(NH):
                if h + 1 < NH:
                    scores(h + 1)
                turn(h)
                output(h)
            pe.wait_ge(sem("attn_head_done"), NSA_AT_HEAD + NH)

        def nsa_act(act):
            act.wait_ge(sem("nsa_in"), N_LOADS)
            act.wait_ge(sem("nsa_hidden_sum"), 1)
            act.activation(n_pos, pm[2][:, 0:2], ACT.Copy)
            act.drain()
            for j in range(2):
                act.activation(n_H[:, 60 * j:60 * j + 60], pm[3][:, 64 * j:64 * j + 60], ACT.Gelu_apprx_tanh,
                               bias=n_pos[:, j:j + 1])
            act.drain().then_inc(sem("nsa_hidden"), 1)
            act.activation(ng, ng, ACT.Sigmoid).then_inc(sem("nsa_gates"), 1)
            act.wait_ge(sem("nsa_kvc_sum"), 1)
            act.activation(n_kc[:, 0:60], pm[2][:, 0:60], ACT.Copy)
            act.activation(n_vc[0:NCMP, :], pm[3][0:NCMP, 0:256], ACT.Copy)
            act.drain().then_inc(sem("nsa_kvc"), 1)

            def exponentials(h):
                n_s, n_pt, n_cs, n_ct, n_st = nsa_bufs[h % 2]
                act.wait_ge(sem("attn_max"), NSA_SOFT_AT + h + 1)
                for w in range(2):
                    for qb, (a, z) in enumerate([(256, 384), (0, 256)]):
                        n = 2 * w + qb
                        s = n_s[:, 384 * w + a:384 * w + z]
                        act.activation(s, nsa_banks[h % 2][w][:, a:z], ACT.Exp, scale=HSCALE, bias=n_st[:, 8 + n:9 + n],
                                       accum_out=n_st[:, 16 + n:17 + n])
                for qb in range(2):
                    s = n_cs[:, 16 * qb:16 * qb + 15]
                    act.activation(s, s, ACT.Exp, bias=n_st[:, 12 + qb:13 + qb])
                act.drain().then_inc(sem("attn_exp"), 1)

            exponentials(0)
            for h in range(NH):
                n_s, n_pt, n_cs, n_ct, n_st = nsa_bufs[h % 2]
                bank = nsa_banks[h % 2]
                r, b = slice(64 * (h % 2), 64 * (h % 2) + 64), h // 2
                act.wait_ge(sem("attn_turned"), NSA_SOFT_AT + h + 1)
                for w in range(2):
                    act.activation(n_pt[:, 384 * w:384 * w + 384], bank[2 + w][:, 0:384], ACT.Copy)
                act.activation(n_ct[0:NCMP, :], bank[1][0:NCMP, 0:256], ACT.Copy)
                act.drain().then_inc(sem("attn_pt"), 1)
                if h + 1 < NH:
                    exponentials(h + 1)
                act.wait_ge(sem("attn_out"), NSA_AT_HEAD + h + 1)
                act.activation(hT[r, 8 + b, :], bank[0][r, 0:256], ACT.Copy).then_inc(sem("attn_head_done"), 1)

        def nsa_dve(dve):
            dve.wait_ge(sem("nsa_in"), N_LOADS)
            dve.wait_ge(sem("nsa_hidden_sum"), 1)
            dve.wait_ge(sem("attn_head_done"), SB_AT + SB_HEADS)
            dve.memset(n_rows[0:16, 256:384], NEG)
            dve.tensor_copy(n_rows[0:16, 0:256], pm[0][0:16, 0:256])
            dve.tensor_copy(nBC, pm[1][:, 0:480].rearrange("p (q n h) -> p q h n", q=2, h=NH))
            dve.drain().then_inc(sem("bias_rows_ready"), 1)
            dve.wait_ge(sem("bias_rows_stored"), 16)
            dve.wait_ge(sem("nsa_gates"), 1)
            cadd = nc_("cmp_add").rearrange("p (q n) -> p q n", q=2)
            cmul = nc_("cmp_mul").rearrange("p (q n) -> p q n", q=2)
            for h in range(NH):
                n_s, n_pt, n_cs, n_ct, n_st = nsa_bufs[h % 2]
                bank = nsa_banks[h % 2]
                cs = n_cs.rearrange("p (q n) -> p q n", q=2)[:, :, 0:15]
                dve.wait_ge(sem("attn_scores"), NSA_AT_HEAD + h + 1)
                dve.scalar_tensor_tensor(cs, bank[0][:, 384:416].rearrange("p (q n) -> p q n", q=2)[:, :, 0:15], HSCALE,
                                         nBC[:, :, h, :], ALU.mult, ALU.add)
                dve.drain()
                dve.tensor_tensor(cs, cs, cadd, ALU.add)
                for w in range(2):
                    dve.reduce_max(n_st[:, 2 * w:2 * w + 1], bank[w][:, 256:384], AX.X)
                    dve.reduce_max(n_st[:, 2 * w + 1:2 * w + 2], bank[w][:, 0:256], AX.X)
                dve.drain()
                dve.reduce_max(n_st[:, 4:6], cs, AX.X)
                dve.drain()
                dve.tensor_scalar(n_st[:, 8:12], n_st[:, 0:4], -HSCALE, None, ALU.mult)
                dve.tensor_scalar(n_st[:, 12:14], n_st[:, 4:6], -1.0, None, ALU.mult).then_inc(sem("attn_max"), 1)
                dve.wait_ge(sem("attn_exp"), NSA_SOFT_AT + h + 1)
                dve.tensor_tensor(cs, cs, cmul, ALU.mult)
                dve.drain()
                dve.reduce_sum(n_st[:, 20:22], cs, AX.X)
                dve.drain()
                dve.tensor_scalar(n_st[:, 16:22], n_st[:, 16:22], 1e-30, None, ALU.max)
                dve.drain()
                dve.reciprocal(n_st[:, 16:22], n_st[:, 16:22])
                dve.drain()
                f = n_st[:, 24:30].rearrange("p (w q) -> p q w", w=3)
                s = n_st[:, 16:22].rearrange("p (w q) -> p q w", w=3)
                dve.tensor_tensor(f[:, :, 0:2], s[:, :, 0:2], ng[:, :, 3 * h + 1:3 * h + 3], ALU.mult)
                dve.tensor_tensor(f[:, :, 2:3], s[:, :, 2:3], ng[:, :, 3 * h:3 * h + 1], ALU.mult)
                dve.drain()
                for w in range(2):
                    for qb, (a, z) in enumerate([(256, 384), (0, 256)]):
                        v = n_s[:, 384 * w + a:384 * w + z]
                        dve.tensor_scalar(v, v, n_st[:, 24 + 2 * w + qb:25 + 2 * w + qb], None, ALU.mult)
                for qb in range(2):
                    v = n_cs[:, 16 * qb:16 * qb + 15]
                    last = dve.tensor_scalar(v, v, n_st[:, 28 + qb:29 + qb], None, ALU.mult)
                last.then_inc(sem("attn_probs"), 1)

        XH = 4
        (x_q, x_k, x_v) = carve(1024, 1024, 1024)
        x_bufs = [carve(512, 512, 8, at=6144 + 1032 * h) for h in range(XH)]
        xoT = arena[:, 5120:5120 + 1024].rearrange("p (b t) -> p b t", b=XH)

        def xa_pool(pool):
            stage_stored(pool, "xq")
            pool.wait_ge(sem("ln_done"), NCK)
            for n in range(2):
                for dst, name in ((x_q, "xq"), (x_k, "mem_k"), (x_v, "mem_v")):
                    pool.dma_start(dst[:, 512 * n:512 * n + 512], units[PLAN[name].store + n, :, :]).then_inc(sem("xa_in"), 16)

        def xa_pe(pe):
            pe.wait_ge(sem("xa_in"), 96)
            for h in range(XH):
                q, k = x_q[:, h * T:h * T + T], x_k[:, h * T:h * T + T]
                for qb in range(2):
                    mm = pe.matmul(pm[h][:, qb * T:qb * T + T], q[:, qb * P:qb * P + P], k, start=True, stop=True)
                mm.then_inc(sem("attn_scores"), 1)

            def turn(h):
                x_s, x_pt, x_st = x_bufs[h]
                pe.wait_ge(sem("attn_probs"), XA_AT + h + 1)
                for kb in range(2):
                    for qb in range(2):
                        mm = pe.transpose(psg[h][:, kb * T + qb * P:kb * T + qb * P + P],
                                          x_s[:, qb * T + kb * P:qb * T + kb * P + P], const("identity"))
                mm.then_inc(sem("attn_turned"), 1)

            def output(h):
                x_s, x_pt, x_st = x_bufs[h]
                pe.wait_ge(sem("attn_pt"), XA_SOFT_AT + h + 1)
                v = x_v.rearrange("p (n k e) -> p n k e", n=2, k=2)
                for kb in range(2):
                    mm = pe.matmul(pm[h][:, 0:T], v[:, h // 2, kb, (h % 2) * P:(h % 2) * P + P],
                                   x_pt[:, kb * T:kb * T + T], start=kb == 0, stop=kb == 1)
                mm.then_inc(sem("attn_out"), 1)

            turn(0)
            for h in range(XH):
                if h + 1 < XH:
                    turn(h + 1)
                output(h)

        def xa_act(act):
            sc = float(P) ** -0.5

            def exponentials(h):
                x_s, x_pt, x_st = x_bufs[h]
                act.wait_ge(sem("attn_max"), XA_SOFT_AT + h + 1)
                for qb in range(2):
                    act.activation(x_s[:, qb * T:qb * T + T], pm[h][:, qb * T:qb * T + T], ACT.Exp, scale=sc,
                                   bias=x_st[:, 2 + qb:3 + qb], accum_out=x_st[:, 4 + qb:5 + qb])
                act.drain().then_inc(sem("attn_exp"), 1)

            def turned(h):
                x_s, x_pt, x_st = x_bufs[h]
                act.wait_ge(sem("attn_turned"), XA_SOFT_AT + h + 1)
                act.activation(x_pt, psg[h][:, :], ACT.Copy).then_inc(sem("attn_pt"), 1)

            exponentials(0)
            exponentials(1)
            turned(0)
            for h in range(XH):
                if h + 2 < XH:
                    exponentials(h + 2)
                if h + 1 < XH:
                    turned(h + 1)
                act.wait_ge(sem("attn_out"), XA_AT + h + 1)
                act.activation(xoT[:, h, :], pm[h][:, 0:T], ACT.Copy).then_inc(sem("attn_head_done"), 1)

        def xa_dve(dve):
            def maxima(h):
                x_s, x_pt, x_st = x_bufs[h]
                dve.wait_ge(sem("attn_scores"), XA_AT + h + 1)
                dve.reduce_max(x_st[:, 0:2], pm[h][:, :].rearrange("p (q k) -> p q k", q=2), AX.X)
                dve.drain()
                dve.tensor_scalar(x_st[:, 2:4], x_st[:, 0:2], -float(P) ** -0.5, None, ALU.mult).then_inc(sem("attn_max"), 1)

            maxima(0)
            for h in range(XH):
                if h + 1 < XH:
                    maxima(h + 1)
                x_s, x_pt, x_st = x_bufs[h]
                dve.wait_ge(sem("attn_exp"), XA_SOFT_AT + h + 1)
                dve.reciprocal(x_st[:, 4:6], x_st[:, 4:6])
                dve.drain()
                for qb in range(2):
                    v = x_s[:, qb * T:qb * T + T]
                    last = dve.tensor_scalar(v, v, x_st[:, 4 + qb:5 + qb], None, ALU.mult)
                last.then_inc(sem("attn_probs"), 1)

        CV_AT = FB * T
        (cv_p, cv_u, cv_t, cv_g) = carve(352, 4 * 516, 2 * 512, 2 * 256, at=CV_AT)
        cvu = cv_u.rearrange("p (s h t) -> p s h t", s=4, h=2)
        cvt = cv_t.rearrange("p (s h t) -> p s h t", s=2, h=2)
        cvg = cv_g.rearrange("p (s t) -> p s t", s=2)

        def conv_pool(pool):
            pool.wait_ge(sem("ln_done"), 2 * NCK)
            pool.dma_start(cv_p, t_in["conv"]).then_inc(sem("conv_in"), 16)

        def conv_act(act):
            st = PLAN["up2"]
            act.wait_ge(sem("conv_zero"), 1)

            def unit(i, j):
                u = 4 * i + j
                b = (st.bank + j) % 4
                unit_done(act, st, i, j)
                if not (isinstance(u, int) and u < 4):
                    act.wait_ge(sem("conv_read"), u - 3)
                act.activation(cvu[:, j % 4, :, 2:258], psg[b][:, :].rearrange("p (h t) -> p h t", h=2), ACT.Copy)\
                    .then_inc(bank_free[b], 1)
                act.wait_ge(sem("conv_done"), u + 1)
                act.activation(cvg[:, j % 2, :], cvt[:, j % 2, 1, :], ACT.Gelu_apprx_tanh).then_inc(sem("conv_gelu"), 1)
            for u in range(4):
                unit(0, u)
            with act.Fori(1, st.units // 4) as i:
                for j in range(4):
                    unit(i, j)

        def conv_dve(dve):
            st = PLAN["up2"]
            dve.wait_ge(sem("ln_done"), 2 * NCK)
            dve.memset(cvu[:, :, :, 0:2], 0.0).then_inc(sem("conv_zero"), 1)
            dve.wait_ge(sem("conv_in"), 16)

            def unit(i, j):
                u = 4 * i + j
                b = (st.bank + j) % 4
                dve.wait_ge(bank_free[b], i + (st.bank + j) // 4 + 1)
                col = lambda h, k: cv_p[:, 8 * u + 4 * h + k:8 * u + 4 * h + k + 1] if isinstance(u, int) else \
                    arena[:, bass.ds(u * 8 + (CV_AT + 4 * h + k), 1)]
                U, V = cvu[:, j % 4, :, :], cvt[:, j % 2, :, :]
                for h in range(2):
                    dve.tensor_scalar(V[:, h, :], U[:, h, 2:258], col(h, 2), col(h, 3), ALU.mult, ALU.add)
                dve.drain()
                for h in range(2):
                    dve.scalar_tensor_tensor(V[:, h, :], U[:, h, 1:257], col(h, 1), V[:, h, :], ALU.mult, ALU.add)
                dve.drain()
                for h in range(2):
                    last = dve.scalar_tensor_tensor(V[:, h, :], U[:, h, 0:256], col(h, 0), V[:, h, :], ALU.mult, ALU.add)
                dve.drain().then_inc(sem("conv_done"), 1)
                dve.nop().then_inc(sem("conv_read"), 1)
                dve.wait_ge(sem("conv_gelu"), u + 1)
                dst = fT[:, u, :] if isinstance(u, int) else arena[:, bass.ds(u * T, T)]
                dve.tensor_tensor(dst, V[:, 0, :], cvg[:, j % 2, :], ALU.mult)
                dve.drain()
            for u in range(4):
                unit(0, u)
            with dve.Fori(1, st.units // 4) as i:
                for j in range(4):
                    unit(i, j)
            dve.drain().then_inc(sem("conv_ready"), 1)

        block = ctx.enter_context(nc.Block())

        def beside_rw1(n):
            return 1 + n % 2

        def beside_da(n):
            return 1 + (n % 5 in (1, 3))

        def beside_rw2(n):
            return n % 2

        INV_FIRST = 0.3

        def inverse_steps(n):
            done = lambda m: max(0, round((C - 1) * (INV_FIRST + (1 - INV_FIRST) * m / (5 * DA_HEADS)) ** (1 / 3)))
            return done(n + 1) - done(n)

        SECOND = ("sqk", "sv", "nq", "nkc", "nk", "nv", "ng")
        SB_FROM = 16

        def beside_mixers(n):
            return 2 if n < 14 else int(n % 4 > 0)

        def beside_s5(s5, sb):
            for n, _ in enumerate(s5):
                yield
                if n >= SB_FROM:
                    next(sb, None)
            for _ in sb:
                yield

        @block.sync
        def _(sp):
            sp.wait_ge(sem("x_loaded"), 16)
            sp.wait_ge(sem("consts_loaded"), 16)
            stream_weights(sp)

        @block.gpsimd
        def _(pool):
            load_inputs(pool)
            rw1_pool(pool)
            inv_pool(pool)
            da_pool(pool)
            rw2_pool(pool)
            gates_pool(pool)
            mem_pool(pool)
            s5_pool(pool)
            nsa_pool(pool)
            xa_pool(pool)
            conv_pool(pool)
            pool.wait_ge(sem("ln_done"), 3 * NCK)
            pool.dma_start(t_out, xT[:, :, :]).then_inc(sem("out_written"), 16)
            pool.wait_ge(sem("out_written"), 16)

        @block.tensor
        def _(pe):
            pe.wait_ge(sem("consts_loaded"), 16)
            squares_pe(pe, "mix_pre", pm[0])
            products(pe, "rkv", hT, ready="mix_in", count=NCK, chunks=NCK)
            products(pe, "lora", hT)
            weave(chain(quarters(pe, "qk", hT), quarters(pe, "v", hT)), rw1_pe(pe), beside_rw1)
            weave(quarters(pe, "gates", hT), da_pe(pe), beside_da)
            weave(quarters(pe, "branch_a", oaT, ready="attn_head_done", count=DA_HEADS), rw2_pe(pe), beside_rw2)
            products(pe, "branch_b", obT, ready="rw2_group_done", count=RW_TILES // GT)
            post_norm_pe(pe, "out", mixT, "mix_ready")
            squares_pe(pe, "ffn_pre", pm[0])
            products(pe, "ffn_in", hT, ready="ffn_in", count=NCK, chunks=NCK)
            post_norm_pe(pe, "ffn_out", fT, "ffn_ready")
            products(pe, "mem_k", hT, ready="mem_loaded", count=16)
            products(pe, "mem_v", hT)
            products(pe, "u5", xT, ready="block1_done", count=NCK, chunks=NCK)
            weave(chain(*(quarters(pe, name, xT) for name in SECOND)), beside_s5(s5_pe(pe), sb_pe(pe)), beside_mixers)
            nsa_pe(pe)
            ln_product_pe(pe, "out2", hT, 1)
            products(pe, "xq", xT, ready="ln_done", count=NCK, chunks=NCK)
            xa_pe(pe)
            ln_product_pe(pe, "xo", xoT, 2, ready="attn_head_done", count=XA_AT + XH)
            products(pe, "up2", xT, ready="ln_done", count=2 * NCK, chunks=NCK)
            ln_product_pe(pe, "down2", fT, 3, ready="conv_ready")

        @block.scalar
        def _(act):
            act.wait_ge(sem("small_set"), 1)
            squares_act(act, "mix_pre", xT, "x_loaded", 16)
            root_act(act, "mix_pre", pm[0], 0)
            store_units(act, "rkv")
            store_units(act, "lora")
            weave(chain(store_quarters(act, "qk"), store_quarters(act, "v")), rw1_act(act), beside_rw1)
            weave(store_quarters(act, "gates"), da_act(act), beside_da)
            weave(branch_a_act(act), rw2_act(act), beside_rw2)
            gates_act(act)
            scaled_into_y(act, "out", "g_mix_post")
            root_act(act, "mix_post", pm[0], 0)
            squares_act(act, "ffn_pre", xT, "x_mixed", NCK)
            root_act(act, "ffn_pre", pm[0], 0)
            ffn_act(act)
            scaled_into_y(act, "ffn_out", "g_ffn_post")
            root_act(act, "ffn_post", pm[0], 0)
            store_units(act, "mem_k")
            store_units(act, "mem_v")
            s5_angles_act(act)
            store_units(act, "u5")
            weave(chain(*(store_quarters(act, name) for name in SECOND)), beside_s5(s5_act(act), sb_act(act)), beside_mixers)
            nsa_act(act)
            ln_act(act, 1)
            store_units(act, "xq")
            xa_act(act)
            ln_act(act, 2)
            conv_act(act)
            ln_act(act, 3)

        @block.vector
        def _(dve):
            dve.wait_ge(sem("params_loaded"), 16)
            dve.wait_ge(sem("x_loaded"), 16)
            pre_norm_dve(dve, "mix_pre", "g_mix_pre", "mix_in")
            run(rw1_dve(dve))
            inverse, first = inv_dve(dve), round((C - 1) * INV_FIRST ** (1 / 3))
            for _ in range(first):
                next(inverse)
            weave(inverse, da_dve(dve), inverse_steps)
            run(rw2_dve(dve))
            gates_dve(dve)
            post_norm_dve(dve, "mix_post", "x_mixed")
            pre_norm_dve(dve, "ffn_pre", "g_ffn_pre", "ffn_in")
            ffn_dve(dve)
            post_norm_dve(dve, "ffn_post", "block1_done")
            run(beside_s5(s5_dve(dve), sb_dve(dve)))
            nsa_dve(dve)
            ln_dve(dve, 1, "out2")
            xa_dve(dve)
            ln_dve(dve, 2, "xo")
            conv_dve(dve)
            ln_dve(dve, 3, "down2")


def slots_of(w, blocks, cols=256):
    rows, n = w.shape
    parts = rows // (P * blocks)
    s = w.reshape(parts, blocks, P, n // cols, cols).transpose(3, 0, 2, 1, 4)
    s = s.reshape(parts * (n // cols), P, blocks * cols)
    if s.shape[2] < SLOT:
        s = np.concatenate([s, np.zeros((s.shape[0], P, SLOT - s.shape[2]), np.float32)], 2)
    return s


def columns(v):
    return v.reshape(-1, P).T


def padded(w, n):
    return np.concatenate([w, np.zeros((w.shape[0], n - w.shape[1]), w.dtype)], 1)


def second_parts(i, interleave):
    w = i["w_in_2"][0]
    cols = {"u5": (0, 512), "sqk": (512, 1536), "sv": (1536, 2048), "nq": (2048, 3072), "nkc": (3072, 3584)}
    parts = {n: slots_of(w[:, a:b], 16) for n, (a, b) in cols.items()}
    ksl, vsl, ksw, vsw = (w[:, 3584 + 256 * n:3840 + 256 * n] for n in range(4))
    parts["nk"] = slots_of(np.concatenate([ksl, ksw], 1), 16)
    parts["nv"] = slots_of(np.concatenate([vsl, vsw], 1), 16)
    parts["ng"] = slots_of(padded(w[:, 4608:4656], 256), 16)
    parts["mem_k"] = slots_of(i["xa_wkv_2"][0][:, :512], 16)
    parts["mem_v"] = slots_of(i["xa_wkv_2"][0][:, 512:], 16)
    parts["out2"] = slots_of(i["w_out_2"][0], 16)
    parts["xq"] = slots_of(i["xa_wq_2"][0], 16)
    parts["xo"] = slots_of(i["xa_wo_2"][0], 4, 1024)
    parts["up2"] = slots_of(interleave(i["ffn_w_up_2"][0]), 16)
    parts["down2"] = slots_of(i["ffn_w_down_2"][0], 11)
    return parts


def second_arrays(i, put, arrays):
    for n in range(3):
        put(f"ln_g{n}", i["ln_g_2"][0, n])
        put(f"ln_b{n}", i["ln_b_2"][0, n])
    put("s5_d", columns(i["s5_d_2"][0]))
    put("s5_b_glu", columns(i["s5_b_glu_2"][0]))
    put("lam_re", columns(i["s5_lambda_re_2"][0].reshape(-1)))
    put("lam_im", columns(i["s5_lambda_im_2"][0].reshape(-1)))
    put("log_dt", columns(np.repeat(i["s5_log_dt_2"][0], 64)))
    bc = np.zeros((16, P, 4 * P), np.float32)
    for g in range(32):
        n, s, ch = g // 2, slice(64 * (g % 2), 64 * (g % 2) + 64), 16 * (g % 8)
        for w, name in enumerate(["s5_b_re_2", "s5_b_im_2"]):
            bc[n, ch:ch + 16, w * P + s.start:w * P + s.stop] = i[name][0, g].T
        for w, name in enumerate(["s5_c_re_2", "s5_c_im_2"]):
            bc[n, s, (2 + w) * P + ch:(2 + w) * P + ch + 16] = i[name][0, g].T
    arrays["s5_bc"] = bc
    arrays["w_glu"] = i["s5_w_glu_2"][0].reshape(4, P, 512).transpose(1, 0, 2)
    arrays["memT"] = i["mem_2"][0].T.reshape(DB, P, T).transpose(1, 0, 2)
    nsa = np.zeros((P, NSA_CONST_W), np.float32)
    nsa_constants(nsa)
    for name, v in [("tab", i["rel_bias_2"]), ("w2", np.concatenate(list(i["nsa_cmp_w2_2"][0]), 1)),
                    ("pos", i["nsa_cmp_pos_2"][0].reshape(32, P).T)]:
        a, b = NSA_AT[name]
        nsa[:v.shape[0], a:b] = v
    arrays["nsa_const"] = nsa
    arrays["cmp_w1"] = i["nsa_cmp_w1_2"][0].reshape(2, 16, P, P).transpose(2, 0, 1, 3)
    conv = np.zeros((P, FB, 2, 4), np.float32)
    conv[:, :, :, 0:3] = i["ffn_conv_w_2"][0].reshape(3, 2, FB, P).transpose(3, 2, 1, 0)
    conv[:, :, :, 3] = i["ffn_conv_b_2"][0].reshape(2, FB, P).transpose(2, 1, 0)
    arrays["conv"] = conv.reshape(P, FB * 8)


def lay_out(i):
    w_in = i["w_in"][0]
    da_q, da_k, da_v, rwkv = w_in[:, 0:2048], w_in[:, 2048:4096], w_in[:, 4096:6144], w_in[:, 6144:12288]
    lora, gate_cols = w_in[:, 12288:12736], w_in[:, 12736:16832]
    lora = np.concatenate([padded(lora[:, 0:96], P), padded(lora[:, 96:192], P), lora[:, 192:448]], 1)
    interleave = lambda w: np.stack([w[:, :D_FF].reshape(D, FB, P), w[:, D_FF:].reshape(D, FB, P)], 2).reshape(D, 2 * D_FF)
    parts = {
        "rkv": slots_of(rwkv, 16), "lora": slots_of(lora, 16),
        "qk": slots_of(np.concatenate([da_q, da_k], 1), 16), "v": slots_of(da_v, 16),
        "gates": slots_of(gate_cols, 16), "branch_a": slots_of(i["w_branch_a"][0], 16),
        "branch_b": slots_of(i["w_branch_b"][0], 16), "out": slots_of(i["w_out"][0], 16),
        "ffn_in": slots_of(interleave(i["w_ffn_in"][0]), 16), "ffn_out": slots_of(i["w_ffn_out"][0], 11),
    }
    parts.update(second_parts(i, interleave) if "mem_k" in PLAN else {})
    weights = np.concatenate([parts[s[0]] for s in STAGES])
    assert weights.shape[0] == N_SLOTS

    mu = i["rw_mu"][0]
    params = np.zeros((P, 16 * len(NORMS) + MISC_W), np.float32)

    def put(name, v):
        if name in NORMS:
            params[:, 16 * NORMS.index(name):16 * NORMS.index(name) + 16] = columns(v)
        else:
            a, b = MISC_AT[name]
            params[:v.shape[0], 16 * len(NORMS) + a:16 * len(NORMS) + b] = v

    for name in ("g_mix_pre", "g_mix_post", "g_ffn_pre", "g_ffn_post"):
        put(name, i[name][0])
    put("ln_w", i["rw_ln_w"][0])
    put("ln_b", i["rw_ln_b"][0])
    put("b_gate_a", i["b_gate"][0, :D])
    put("b_gate_b", i["b_gate"][0, D:])
    put("mu_wl", mu[6144:6240][:, None])
    put("mu_al", mu[6240:6336][:, None])
    put("mu_gl0", mu[6336:6464][:, None])
    put("mu_gl1", mu[6464:6592][:, None])
    put("lam_q", i["da_lambda_q"][0].T)
    put("lam_k", i["da_lambda_k"][0].T)
    put("subln", columns(i["da_subln_g"][0]))

    rw_pack = np.zeros((RW_TILES, P, RW_PW), np.float32)
    tiles = lambda w: w.reshape(w.shape[0], RW_TILES, P).transpose(1, 0, 2)
    rw_pack[:, :LORA, 0:P] = tiles(i["rw_w_up"][0])
    rw_pack[:, :LORA, P:2 * P] = tiles(i["rw_a_up"][0])
    rw_pack[:, :, 2 * P:3 * P] = tiles(i["rw_g_up"][0][:P])
    rw_pack[:, :, 3 * P:4 * P] = tiles(i["rw_g_up"][0][P:])
    cols = {"mu_r": mu[:2048], "mu_k": mu[2048:4096], "mu_v": mu[4096:6144], "w0": i["rw_w0"][0], "a0": i["rw_a0"][0],
            "k_k": i["rw_k_k"][0], "k_a": i["rw_k_a"][0], "r_k": i["rw_r_k"][0].reshape(-1),
            "ln_w": i["rw_ln_w"][0], "ln_b": i["rw_ln_b"][0]}
    for n, name in enumerate(RW_PACK):
        rw_pack[:, :, 4 * P + n] = cols[name].reshape(RW_TILES, P)

    arrays = {"weights": weights, "consts": constants(), "rw_pack": rw_pack,
              "xT": i["x"][0].T.reshape(DB, P, T).transpose(1, 0, 2)}
    if "mem_k" in PLAN:
        second_arrays(i, put, arrays)
    arrays["params"] = params
    return {"in_" + k: np.ascontiguousarray(v, dtype=np.float32) for k, v in arrays.items()}


def program(nc, arrays):
    t_in = {n[3:]: nc.dram_tensor(n, a.shape, F32, kind="ExternalInput").ap() for n, a in arrays.items()}
    t_out = nc.dram_tensor("outT", (P, DB, T), F32, kind="ExternalOutput").ap()
    build(nc, t_in, t_out)


def kernel(**inputs):
    import concourse.bacc as bacc
    from concourse.bass_utils import run_bass_kernel_spmd

    arrays = lay_out({k: np.asarray(v) for k, v in inputs.items()})
    nc = bacc.Bacc("TRN2", target_bir_lowering=False, num_devices=1)
    program(nc, arrays)
    r = run_bass_kernel_spmd(nc, [arrays], core_ids=[0])
    out = r.results[0]["outT"]
    return np.ascontiguousarray(out.transpose(2, 1, 0).reshape(1, T, D))
```
